# Optimizing a Trainium2 kernel written in Bass

```python
import math
import jax, jax.numpy as jnp
from jax import lax
import numpy as np

D_MODEL = 1024
BATCH = 1
SEQ = 512
DEPTH = 1

M_HEADS = 4
M_DV = 128
M_DQK = 64
M_CHUNK = 64
M_CONV = 4
A_HEADS = 8
A_DH = 64
IDX_HEADS = 8
IDX_DIM = 64
TOPK_MAX = 256
Q_BLOCK = 128
REL_BUCKETS = 32
REL_MAX_DIST = 128
D_FF = 2816
FFN_CONV = 3
EPS = 1e-6

M_WIDTH = M_HEADS * M_DV
A_WIDTH = A_HEADS * A_DH
D_MIX = M_WIDTH + A_WIDTH
IN_SIZES = (M_HEADS * M_DQK, M_HEADS * M_DQK, M_WIDTH, M_WIDTH, M_HEADS, M_HEADS,
            A_WIDTH, A_WIDTH, A_WIDTH, IDX_HEADS * IDX_DIM, IDX_DIM, IDX_HEADS)
D_IN = 2 * M_HEADS * M_DQK + 2 * M_WIDTH + 2 * M_HEADS + 3 * A_WIDTH + IDX_HEADS * IDX_DIM + IDX_DIM + IDX_HEADS


def rms_norm(x, g):
    xf = x.astype(jnp.float32)
    y = xf * lax.rsqrt(jnp.mean(xf * xf, axis=-1, keepdims=True) + EPS)
    return (y * g.astype(jnp.float32)).astype(x.dtype)

def causal_dwconv(x, w, b):
    width = w.shape[0]
    s = x.shape[1]
    xp = jnp.pad(x, ((0, 0), (width - 1, 0), (0, 0)))
    y = b + xp[:, 0:s] * w[0]
    for j in range(1, width):
        y = y + xp[:, j:j + s] * w[j]
    return y

def split_cols(z, sizes):
    out, off = [], 0
    for sz in sizes:
        out.append(z[..., off:off + sz])
        off += sz
    return out

def rel_bucket(dist):
    max_exact = REL_BUCKETS // 2
    d = jnp.maximum(dist, 0)
    large = max_exact + (jnp.log(jnp.maximum(d, 1).astype(jnp.float32) / max_exact)
                         / math.log(REL_MAX_DIST / max_exact) * (REL_BUCKETS - max_exact)).astype(jnp.int32)
    large = jnp.minimum(large, REL_BUCKETS - 1)
    return jnp.where(d < max_exact, d, large)

def mlstm_chunkwise(q, k, v, i_pre, f_pre):
    bsz, s, nh, dqk = q.shape
    dv = v.shape[-1]
    L = M_CHUNK
    nc = s // L
    f32 = jnp.float32

    def heads_chunks(t):
        return t.astype(f32).reshape(bsz, nc, L, nh, t.shape[-1]).transpose(0, 3, 1, 2, 4)

    q = heads_chunks(q) * (dqk ** -0.5)
    k = heads_chunks(k)
    v = heads_chunks(v)
    ig = i_pre.astype(f32).reshape(bsz, nc, L, nh).transpose(0, 3, 1, 2)
    logf = jax.nn.log_sigmoid(f_pre.astype(f32)).reshape(bsz, nc, L, nh).transpose(0, 3, 1, 2)

    b = jnp.cumsum(logf, axis=-1)
    g = b[..., -1]
    a = g[..., None] - b + ig
    m_loc = jnp.max(a, axis=-1)
    wgt = jnp.exp(a - m_loc[..., None])
    kv_c = jnp.einsum('bhcl,bhcld,bhcle->bhcde', wgt, k, v)
    ks_c = jnp.einsum('bhcl,bhcld->bhcd', wgt, k)

    def step(carry, xs):
        c_st, n_st, m_st = carry
        kv, ks, gc, ml = xs
        m_new = jnp.maximum(gc + m_st, ml)
        decay = jnp.exp(gc + m_st - m_new)
        scale = jnp.exp(ml - m_new)
        c_new = decay[..., None, None] * c_st + scale[..., None, None] * kv
        n_new = decay[..., None] * n_st + scale[..., None] * ks
        return (c_new, n_new, m_new), (c_st, n_st, m_st)

    init = (jnp.zeros((bsz, nh, dqk, dv), f32), jnp.zeros((bsz, nh, dqk), f32), jnp.zeros((bsz, nh), f32))
    xs = (jnp.moveaxis(kv_c, 2, 0), jnp.moveaxis(ks_c, 2, 0), jnp.moveaxis(g, 2, 0), jnp.moveaxis(m_loc, 2, 0))
    _, (c_prev, n_prev, m_prev) = lax.scan(step, init, xs)
    c_prev = jnp.moveaxis(c_prev, 0, 2)
    n_prev = jnp.moveaxis(n_prev, 0, 2)
    m_prev = jnp.moveaxis(m_prev, 0, 2)

    tril = jnp.tril(jnp.ones((L, L), dtype=bool))
    dmat = b[..., :, None] - b[..., None, :] + ig[..., None, :]
    dmat = jnp.where(tril, dmat, -jnp.inf)
    inter_log = b + m_prev[..., None]
    m_t = jnp.maximum(inter_log, jnp.max(dmat, axis=-1))
    sc = jnp.einsum('bhcld,bhcsd->bhcls', q, k) * jnp.exp(dmat - m_t[..., None])
    inter_w = jnp.exp(inter_log - m_t)
    num = inter_w[..., None] * jnp.einsum('bhcld,bhcde->bhcle', q, c_prev) + jnp.einsum('bhcls,bhcse->bhcle', sc, v)
    den = inter_w * jnp.einsum('bhcld,bhcd->bhcl', q, n_prev) + jnp.sum(sc, axis=-1)
    h = num / jnp.maximum(jnp.abs(den), jnp.exp(-m_t))[..., None]
    return h.transpose(0, 2, 3, 1, 4).reshape(bsz, s, nh, dv)

def dsa_attention(q_att, k_att, v_att, q_idx, k_idx, w_idx, rel_bias):
    bsz, s = q_att.shape[0], q_att.shape[1]
    topk = min(TOPK_MAX, s // 4)
    nqb = s // Q_BLOCK
    key_pos = jnp.arange(s, dtype=jnp.int32)

    def to_blocks(t):
        return t.reshape(bsz, nqb, Q_BLOCK, *t.shape[2:]).swapaxes(0, 1)

    def one_block(args):
        qa, qi, wi, st = args
        qpos = st + jnp.arange(Q_BLOCK, dtype=jnp.int32)
        isc = jnp.einsum('bqhd,bsd->bqhs', qi, k_idx).astype(jnp.float32) * (IDX_DIM ** -0.5)
        score = jnp.einsum('bqhs,bqh->bqs', jax.nn.relu(isc), wi.astype(jnp.float32))
        score = jnp.where(key_pos[None, None, :] <= qpos[None, :, None], score, -jnp.inf)
        _, idx = lax.top_k(score, topk)
        valid = idx <= qpos[None, :, None]
        ks = jax.vmap(lambda kb, ib: kb[ib])(k_att, idx)
        vs = jax.vmap(lambda vb, ib: vb[ib])(v_att, idx)
        bias = rel_bias[rel_bucket(qpos[None, :, None] - idx)]
        logits = jnp.einsum('bqhd,bqkhd->bqhk', qa, ks).astype(jnp.float32) * (A_DH ** -0.5)
        logits = logits + bias.astype(jnp.float32).transpose(0, 1, 3, 2)
        logits = jnp.where(valid[:, :, None, :], logits, -jnp.inf)
        p = jax.nn.softmax(logits, axis=-1)
        return jnp.einsum('bqhk,bqkhd->bqhd', p.astype(vs.dtype), vs)

    starts = jnp.arange(nqb, dtype=jnp.int32) * Q_BLOCK
    out = lax.map(one_block, (to_blocks(q_att), to_blocks(q_idx), to_blocks(w_idx), starts))
    return out.swapaxes(0, 1).reshape(bsz, s, A_HEADS, A_DH)

def first_inputs(seed: int = 0) -> dict:
    key = jax.random.key(seed)
    ks = jax.random.split(key, 20)
    f32 = jnp.float32
    nrm = lambda k, shape, scale: jax.random.normal(k, shape, f32) * scale
    return {
        'x': nrm(ks[0], (BATCH, SEQ, D_MODEL), 1.0),
        'norm_mix': 1.0 + nrm(ks[1], (DEPTH, D_MODEL), 0.01),
        'w_in': nrm(ks[2], (DEPTH, D_MODEL, D_IN), D_MODEL ** -0.5),
        'mlstm_conv_w': nrm(ks[3], (DEPTH, M_CONV, 2 * M_HEADS * M_DQK), M_CONV ** -0.5),
        'mlstm_conv_b': nrm(ks[4], (DEPTH, 2 * M_HEADS * M_DQK), 0.01),
        'i_bias': nrm(ks[5], (DEPTH, M_HEADS), 0.1),
        'f_bias': 3.0 + nrm(ks[6], (DEPTH, M_HEADS), 0.5),
        'mlstm_norm': 1.0 + nrm(ks[7], (DEPTH, M_WIDTH), 0.01),
        'idx_k_norm': 1.0 + nrm(ks[8], (DEPTH, IDX_DIM), 0.01),
        'rel_bias': nrm(ks[9], (REL_BUCKETS, A_HEADS), 0.5),
        'w_out': nrm(ks[10], (DEPTH, D_MIX, D_MODEL), D_MIX ** -0.5),
        'norm_ffn': 1.0 + nrm(ks[11], (DEPTH, D_MODEL), 0.01),
        'w_up': nrm(ks[12], (DEPTH, D_MODEL, 2 * D_FF), D_MODEL ** -0.5),
        'ffn_conv_w': nrm(ks[13], (DEPTH, FFN_CONV, 2 * D_FF), FFN_CONV ** -0.5),
        'ffn_conv_b': nrm(ks[14], (DEPTH, 2 * D_FF), 0.01),
        'w_down': nrm(ks[15], (DEPTH, D_FF, D_MODEL), D_FF ** -0.5),
        'norm_final': 1.0 + nrm(ks[16], (D_MODEL,), 0.01),
    }

def first_block(x, norm_mix, w_in, mlstm_conv_w, mlstm_conv_b, i_bias, f_bias, mlstm_norm,
              idx_k_norm, rel_bias, w_out, norm_ffn, w_up, ffn_conv_w, ffn_conv_b, w_down, norm_final):
    bsz, s, _ = x.shape
    for l in range(DEPTH):
        h = rms_norm(x, norm_mix[l])
        z = h @ w_in[l]
        (m_q, m_k, m_v, m_o, m_i, m_f, a_q, a_k, a_v, i_q, i_k, i_w) = split_cols(z, IN_SIZES)

        qk = jax.nn.silu(causal_dwconv(jnp.concatenate([m_q, m_k], axis=-1), mlstm_conv_w[l], mlstm_conv_b[l]))
        m_q, m_k = qk[..., :M_HEADS * M_DQK], qk[..., M_HEADS * M_DQK:]
        hm = mlstm_chunkwise(m_q.reshape(bsz, s, M_HEADS, M_DQK), m_k.reshape(bsz, s, M_HEADS, M_DQK),
                             m_v.reshape(bsz, s, M_HEADS, M_DV), m_i + i_bias[l], m_f + f_bias[l])
        hm = rms_norm(hm, mlstm_norm[l].reshape(M_HEADS, M_DV)).astype(x.dtype)
        hm = jax.nn.sigmoid(m_o) * hm.reshape(bsz, s, M_WIDTH)

        ha = dsa_attention(a_q.reshape(bsz, s, A_HEADS, A_DH), a_k.reshape(bsz, s, A_HEADS, A_DH),
                           a_v.reshape(bsz, s, A_HEADS, A_DH), i_q.reshape(bsz, s, IDX_HEADS, IDX_DIM),
                           rms_norm(i_k, idx_k_norm[l]), i_w * (IDX_HEADS ** -0.5), rel_bias)
        ha = ha.reshape(bsz, s, A_WIDTH)

        x = x + jnp.concatenate([hm, ha], axis=-1) @ w_out[l]

        h = rms_norm(x, norm_ffn[l])
        u = causal_dwconv(h @ w_up[l], ffn_conv_w[l], ffn_conv_b[l])
        gate, val = u[..., :D_FF], u[..., D_FF:]
        x = x + (jax.nn.silu(gate) * val) @ w_down[l]
    return rms_norm(x, norm_final)


_first_inputs = first_inputs


def first_inputs(seed=0):
    import zlib

    import numpy as np

    out = dict(_first_inputs(seed))
    spreads = {}
    factors = {'norm_mix': 4.225,
     'mlstm_conv_b': 8.0,
     'i_bias': 8.0,
     'mlstm_norm': 8.0,
     'idx_k_norm': 7.559,
     'norm_ffn': 7.797,
     'ffn_conv_b': 8.0,
     'norm_final': 5.707}
    for name, (base, spread) in spreads.items():
        noise = np.random.default_rng([zlib.crc32(name.encode()), seed]).standard_normal(out[name].shape)
        drawn = base * np.exp(spread * noise) if base else spread * noise
        out[name] = __import__('jax').numpy.asarray(drawn.astype(out[name].dtype))
    for name, factor in factors.items():
        out[name] = (out[name] * factor).astype(out[name].dtype)
    return out


_narrow_inputs = first_inputs


def first_inputs(seed=0):

    out = dict(_narrow_inputs(seed))
    wider = {'i_bias': 12.0,
     'mlstm_norm': 5.89,
     'norm_ffn': 4.5,
     'ffn_conv_b': 4.52,
     'norm_final': 6.43}
    for name, times in wider.items():
        mean = out[name].mean()
        out[name] = (mean + times * (out[name] - mean)).astype(out[name].dtype)
    return out


CHUNK = 64
SUB_CHUNK = 16
HG_DK = 128
HG_HEADS = D_MODEL // HG_DK
HG_DV = D_MODEL // HG_HEADS
HG_FD = HG_HEADS * HG_DK
HG_DI = HG_HEADS * HG_DV
LB_TAIL_LOGIT = 2.0
GM_BLOCK = 128
GM_WIDTH = D_MODEL
GM_GROUPS = 8
GM_CG = GM_WIDTH // GM_GROUPS
D_FF_2 = -(-8 * D_MODEL // (3 * 256)) * 256
IN_WIDTH = 2 * HG_FD + 2 * HG_DI + 2 * GM_WIDTH + 2 * D_MODEL
IN_SPLITS = (HG_FD, 2 * HG_FD, 2 * HG_FD + HG_DI, 2 * HG_FD + 2 * HG_DI,
             2 * HG_FD + 2 * HG_DI + GM_WIDTH, 2 * HG_FD + 2 * HG_DI + 2 * GM_WIDTH,
             2 * HG_FD + 2 * HG_DI + 2 * GM_WIDTH + D_MODEL)
DEEPNORM_ALPHA = (2.0 * DEPTH) ** 0.25
DEEPNORM_BETA = (8.0 * DEPTH) ** -0.25
LN_EPS = 1e-5
RMS_EPS = 1e-6


def _layer_norm(x):
    x = x.astype(jnp.float32)
    xc = x - jnp.mean(x, axis=-1, keepdims=True)
    return xc * lax.rsqrt(jnp.mean(xc * xc, axis=-1, keepdims=True) + LN_EPS)

def _to_chunks(t, heads):
    b, s, _ = t.shape
    return t.reshape(b, s // CHUNK, CHUNK, heads, -1).transpose(0, 3, 1, 2, 4)

def hgrn2_mixer(zq, zf, zi, zg, lower_bound, norm_w):
    b_, s_, _ = zq.shape
    n_sub = CHUNK // SUB_CHUNK
    f = lower_bound + (1.0 - lower_bound) * jax.nn.sigmoid(zf.astype(jnp.float32))
    q = _to_chunks(jax.nn.silu(zq.astype(jnp.float32)), HG_HEADS)
    k = _to_chunks(1.0 - f, HG_HEADS)
    log_f = _to_chunks(jnp.log(f), HG_HEADS)
    v = _to_chunks(zi.astype(jnp.float32), HG_HEADS)
    cum = jnp.cumsum(log_f, axis=3)
    cum_last = cum[:, :, :, -1:, :]

    u_chunk = jnp.einsum('bhnlk,bhnlv->bhnkv', k * jnp.exp(cum_last - cum), v)
    decay = jnp.exp(cum_last[:, :, :, 0, :])

    def step(state, inp):
        dec, upd = inp
        return dec[..., None] * state + upd, state

    state0 = jnp.zeros((b_, HG_HEADS, HG_DK, HG_DV), jnp.float32)
    _, s_prev = lax.scan(step, state0, (jnp.moveaxis(decay, 2, 0), jnp.moveaxis(u_chunk, 2, 0)))
    s_prev = jnp.moveaxis(s_prev, 0, 2)
    o_inter = jnp.einsum('bhnlk,bhnkv->bhnlv', q * jnp.exp(cum), s_prev)

    shp = q.shape[:3] + (n_sub, SUB_CHUNK, HG_DK)
    ref = (cum - log_f)[:, :, :, ::SUB_CHUNK, :]
    q_sub = q.reshape(shp) * jnp.exp(cum.reshape(shp) - ref[:, :, :, :, None, :])
    key_pos = jnp.arange(CHUNK)
    sub_idx = jnp.arange(n_sub)
    key_ok = key_pos[None, :] < (sub_idx[:, None] + 1) * SUB_CHUNK
    expo = ref[:, :, :, :, None, :] - cum[:, :, :, None, :, :]
    k_sub = k[:, :, :, None] * jnp.exp(jnp.where(key_ok[:, :, None], expo, -jnp.inf))
    scores = jnp.einsum('bhnimk,bhnisk->bhnims', q_sub, k_sub)
    q_pos = sub_idx[:, None] * SUB_CHUNK + jnp.arange(SUB_CHUNK)[None, :]
    causal = key_pos[None, None, :] <= q_pos[:, :, None]
    scores = jnp.where(causal, scores, 0.0)
    o_intra = jnp.einsum('bhnims,bhnsv->bhnimv', scores, v).reshape(o_inter.shape)

    o = (o_inter + o_intra).transpose(0, 2, 3, 1, 4).reshape(b_, s_, HG_HEADS, HG_DV)
    o = o * lax.rsqrt(jnp.mean(o * o, axis=-1, keepdims=True) + RMS_EPS) * norm_w
    gate = jax.nn.silu(zg.astype(jnp.float32)).reshape(b_, s_, HG_HEADS, HG_DV)
    return (o * gate).reshape(b_, s_, HG_DI)

def gmlp_mixer(zu, zv, ln_w, ln_b, w_s, b_s):
    b_, s_, _ = zu.shape
    u = jax.nn.gelu(zu.astype(jnp.float32), approximate=False)
    v = jax.nn.gelu(zv.astype(jnp.float32), approximate=False)
    v = _layer_norm(v) * ln_w + ln_b
    v = v.reshape(b_, s_ // GM_BLOCK, GM_BLOCK, GM_GROUPS, GM_CG)
    pos = jnp.arange(GM_BLOCK) // CHUNK
    mask = pos[:, None] >= pos[None, :]
    w = jnp.where(mask[None], w_s, 0.0)
    sv = jnp.einsum('gts,bnsgc->bntgc', w, v) + b_s.T[None, None, :, :, None]
    return u * sv.reshape(b_, s_, GM_WIDTH)

def second_inputs(seed: int = 0) -> dict:
    key = jax.random.key(seed)
    ks = jax.random.split(key, 24)

    def nrm(k, shape, scale):
        return jax.random.normal(k, shape, jnp.float32) * scale

    L = DEPTH
    return {
        "x": nrm(ks[0], (BATCH, SEQ, D_MODEL), 1.0),
        "c": nrm(ks[1], (BATCH, D_MODEL), 1.0),
        "w_ada": nrm(ks[2], (L, D_MODEL, 6 * D_MODEL), D_MODEL ** -0.5),
        "b_ada": nrm(ks[3], (L, 6 * D_MODEL), 0.01),
        "w_in": nrm(ks[4], (L, D_MODEL, IN_WIDTH), D_MODEL ** -0.5),
        "b_gate": nrm(ks[5], (L, 2, D_MODEL), 0.01),
        "hgrn_lb_logits": nrm(ks[6], (L + 1, HG_FD), 0.1).at[L].add(LB_TAIL_LOGIT),
        "hgrn_norm_w": 1.0 + nrm(ks[7], (L, HG_DV), 0.02),
        "w_proj_a": nrm(ks[8], (L, HG_DI, D_MODEL), HG_DI ** -0.5),
        "gmlp_ln_w": 1.0 + nrm(ks[9], (L, GM_WIDTH), 0.02),
        "gmlp_ln_b": nrm(ks[10], (L, GM_WIDTH), 0.02),
        "gmlp_ws": nrm(ks[11], (L, GM_GROUPS, GM_BLOCK, GM_BLOCK), GM_BLOCK ** -0.5),
        "gmlp_bs": 1.0 + nrm(ks[12], (L, GM_GROUPS, GM_BLOCK), 0.1),
        "w_proj_b": nrm(ks[13], (L, GM_WIDTH, D_MODEL), GM_WIDTH ** -0.5),
        "w_out": nrm(ks[14], (L, D_MODEL, D_MODEL), DEEPNORM_BETA * D_MODEL ** -0.5),
        "ln1_w": 1.0 + nrm(ks[15], (L, D_MODEL), 0.02),
        "ln1_b": nrm(ks[16], (L, D_MODEL), 0.02),
        "w_ffn_in": nrm(ks[17], (L, D_MODEL, 2 * D_FF_2), D_MODEL ** -0.5),
        "w_ffn_out": nrm(ks[18], (L, D_FF_2, D_MODEL), DEEPNORM_BETA * D_FF_2 ** -0.5),
        "ln2_w": 1.0 + nrm(ks[19], (L, D_MODEL), 0.02),
        "ln2_b": nrm(ks[20], (L, D_MODEL), 0.02),
    }

def second_block(x, c, w_ada, b_ada, w_in, b_gate, hgrn_lb_logits, hgrn_norm_w, w_proj_a,
              gmlp_ln_w, gmlp_ln_b, gmlp_ws, gmlp_bs, w_proj_b, w_out, ln1_w, ln1_b,
              w_ffn_in, w_ffn_out, ln2_w, ln2_b):
    lower_bounds = jnp.cumsum(jax.nn.softmax(hgrn_lb_logits.astype(jnp.float32), axis=0), axis=0)
    h = x.astype(jnp.float32)
    cond = jax.nn.silu(c.astype(jnp.float32))
    for l in range(DEPTH):
        mod = cond @ w_ada[l] + b_ada[l]
        sh1, sc1, g1, sh2, sc2, g2 = [m[:, None, :] for m in jnp.split(mod, 6, axis=-1)]

        u = _layer_norm(h) * (1.0 + sc1) + sh1
        z = u @ w_in[l]
        zq, zf, zi, zg, zu, zv, zga, zgb = jnp.split(z, IN_SPLITS, axis=-1)
        y_a = hgrn2_mixer(zq, zf, zi, zg, lower_bounds[l], hgrn_norm_w[l]) @ w_proj_a[l]
        y_b = gmlp_mixer(zu, zv, gmlp_ln_w[l], gmlp_ln_b[l], gmlp_ws[l], gmlp_bs[l]) @ w_proj_b[l]
        gate_a = jax.nn.sigmoid(zga + b_gate[l, 0])
        gate_b = jax.nn.sigmoid(zgb + b_gate[l, 1])
        mix = (gate_a * y_a + gate_b * y_b) @ w_out[l]
        h = _layer_norm(DEEPNORM_ALPHA * h + g1 * mix) * ln1_w[l] + ln1_b[l]

        u2 = _layer_norm(h) * (1.0 + sc2) + sh2
        a, bb = jnp.split(u2 @ w_ffn_in[l], 2, axis=-1)
        ffn = (jax.nn.silu(a) * bb) @ w_ffn_out[l]
        h = _layer_norm(DEEPNORM_ALPHA * h + g2 * ffn) * ln2_w[l] + ln2_b[l]
    return h.astype(x.dtype)


_first_inputs_2 = second_inputs


def second_inputs(seed=0):
    import zlib

    import numpy as np

    out = dict(_first_inputs_2(seed))
    spreads = {}
    factors = {'b_ada': 6.447,
     'b_gate': 8.0,
     'hgrn_norm_w': 8.0,
     'gmlp_ln_w': 8.0,
     'gmlp_ln_b': 8.0,
     'gmlp_bs': 3.77,
     'ln1_w': 2.794,
     'ln1_b': 2.771,
     'ln2_w': 2.826,
     'ln2_b': 2.949}
    for name, (base, spread) in spreads.items():
        noise = np.random.default_rng([zlib.crc32(name.encode()), seed]).standard_normal(out[name].shape)
        drawn = base * np.exp(spread * noise) if base else spread * noise
        out[name] = __import__('jax').numpy.asarray(drawn.astype(out[name].dtype))
    for name, factor in factors.items():
        out[name] = (out[name] * factor).astype(out[name].dtype)
    return out


_narrow_inputs_2 = second_inputs


def second_inputs(seed=0):

    out = dict(_narrow_inputs_2(seed))
    wider = {'hgrn_norm_w': 5.21,
     'gmlp_ln_w': 5.87,
     'gmlp_ln_b': 5.86,
     'ln1_w': 3.2,
     'ln1_b': 3.23,
     'ln2_w': 3.1,
     'ln2_b': 3.18}
    for name, times in wider.items():
        mean = out[name].mean()
        out[name] = (mean + times * (out[name] - mean)).astype(out[name].dtype)
    return out


D_MIX_3 = D_MODEL
D_POOL = D_MIX_3 // 2
D_CONV = D_MIX_3 - D_POOL
POOL_WINDOWS = (2, 4, 8, 16)
N_POOL_GROUPS = len(POOL_WINDOWS)
POOL_GROUP_DIM = D_POOL // N_POOL_GROUPS
N_CONV_HEADS = 8
CONV_WIDTH = 3
D_IN_PROJ = D_POOL + 3 * D_CONV

N_EXPERTS = 32
TOP_K = 4
D_FF_3 = D_MODEL
SWIGLU_LIMIT = 7.0
SWIGLU_ALPHA = 1.702
EXPERT_BLOCK = 128

PLE_DIM = 256

DEEPNORM_ALPHA_3 = (2.0 * DEPTH) ** 0.25
DEEPNORM_BETA_3 = (8.0 * DEPTH) ** -0.25


def layer_norm(x, g, b):
    xf = x.astype(jnp.float32)
    mu = jnp.mean(xf, axis=-1, keepdims=True)
    var = jnp.mean(jnp.square(xf - mu), axis=-1, keepdims=True)
    y = (xf - mu) * lax.rsqrt(var + LN_EPS)
    return (y * g.astype(jnp.float32) + b.astype(jnp.float32)).astype(x.dtype)

def pool_mixer(v, pool_mix, pool_scale):
    B, S, _ = v.shape
    vf = v.astype(jnp.float32)
    t = jnp.arange(S)
    outs = []
    for g, w in enumerate(POOL_WINDOWS):
        vg = vf[..., g * POOL_GROUP_DIM:(g + 1) * POOL_GROUP_DIM]
        cs = jnp.cumsum(vg, axis=1)
        lagged = jnp.pad(cs, ((0, 0), (w, 0), (0, 0)))[:, :S]
        cnt = jnp.minimum(t + 1, w).astype(jnp.float32)[None, :, None]
        outs.append((cs - lagged) / cnt - vg)
    d = jnp.stack(outs, axis=2).astype(v.dtype)
    y = jnp.einsum('bsgc,gcd->bsgd', d, pool_mix).reshape(B, S, D_POOL)
    return y * pool_scale

def conv_mixer(b_gate, c_gate, v, conv_w):
    S = v.shape[1]
    u = c_gate * v
    up = jnp.pad(u, ((0, 0), (CONV_WIDTH - 1, 0), (0, 0)))
    y = conv_w[0] * up[:, 0:S]
    for k in range(1, CONV_WIDTH):
        y = y + conv_w[k] * up[:, k:k + S]
    return b_gate * y

def clamped_swiglu_expert(xb, w_gu, b_gu, w_dn, b_dn):
    gu = xb @ w_gu + b_gu
    gate = jnp.minimum(gu[:, :D_FF_3], SWIGLU_LIMIT)
    up = jnp.clip(gu[:, D_FF_3:], -SWIGLU_LIMIT, SWIGLU_LIMIT)
    glu = gate * jax.nn.sigmoid(SWIGLU_ALPHA * gate)
    return ((up + 1.0) * glu) @ w_dn + b_dn

def moe(h, router_w, router_b, w_gate_up, b_gate_up, w_down, b_down):
    B, S, D = h.shape
    N = B * S
    hf = h.reshape(N, D)
    logits = (hf @ router_w + router_b).astype(jnp.float32)
    top_v, top_i = lax.top_k(logits, TOP_K)
    gates = jax.nn.softmax(top_v, axis=-1)
    A = N * TOP_K
    flat_e = top_i.reshape(A).astype(jnp.int32)
    flat_tok = jnp.repeat(jnp.arange(N, dtype=jnp.int32), TOP_K)
    flat_g = gates.reshape(A)
    order = jnp.argsort(flat_e)
    e_sorted = flat_e[order]
    counts = jax.ops.segment_sum(jnp.ones((A,), jnp.int32), flat_e, num_segments=N_EXPERTS)
    offsets = jnp.cumsum(counts) - counts
    padded = ((counts + EXPERT_BLOCK - 1) // EXPERT_BLOCK) * EXPERT_BLOCK
    pad_end = jnp.cumsum(padded)
    pad_start = pad_end - padded
    dest = pad_start[e_sorted] + (jnp.arange(A, dtype=jnp.int32) - offsets[e_sorted])
    P = A + N_EXPERTS * EXPERT_BLOCK
    NB = P // EXPERT_BLOCK
    row_tok = jnp.zeros((P,), jnp.int32).at[dest].set(flat_tok[order])
    row_gate = jnp.zeros((P,), jnp.float32).at[dest].set(flat_g[order])
    blk_start = jnp.arange(NB, dtype=jnp.int32) * EXPERT_BLOCK
    blk_e = jnp.minimum(jnp.sum(blk_start[:, None] >= pad_end[None, :], axis=1),
                        N_EXPERTS - 1).astype(jnp.int32)
    xb = hf[row_tok].reshape(NB, EXPERT_BLOCK, D)

    def run_block(args):
        xblk, e = args
        return clamped_swiglu_expert(xblk, w_gate_up[e], b_gate_up[e], w_down[e], b_down[e])

    yb = lax.map(run_block, (xb, blk_e)).reshape(P, D)
    y = jax.ops.segment_sum(yb * row_gate[:, None].astype(yb.dtype), row_tok, num_segments=N)
    return y.reshape(B, S, D)

def third_inputs(seed: int = 0) -> dict:
    key = jax.random.key(seed)
    ks = jax.random.split(key, 24)
    L, D, E, F = DEPTH, D_MODEL, N_EXPERTS, D_FF_3
    nrm = lambda k, shape, s: jax.random.normal(k, shape, jnp.float32) * s
    return {
        "x": nrm(ks[0], (BATCH, SEQ, D), 1.0),
        "p": nrm(ks[1], (L, BATCH, SEQ, PLE_DIM), 1.0),
        "w_in": nrm(ks[2], (L, D, D_IN_PROJ), D ** -0.5),
        "pool_mix": nrm(ks[3], (L, N_POOL_GROUPS, POOL_GROUP_DIM, POOL_GROUP_DIM), POOL_GROUP_DIM ** -0.5),
        "pool_scale": 1.0 + nrm(ks[4], (L, D_POOL), 0.1),
        "conv_w": nrm(ks[5], (L, CONV_WIDTH, D_CONV), CONV_WIDTH ** -0.5),
        "w_out": nrm(ks[6], (L, D_MIX_3, D), D_MIX_3 ** -0.5 * DEEPNORM_BETA_3),
        "ln1_g": 1.0 + nrm(ks[7], (L, D), 0.02),
        "ln1_b": nrm(ks[8], (L, D), 0.02),
        "router_w": nrm(ks[9], (L, D, E), D ** -0.5),
        "router_b": nrm(ks[10], (L, E), 0.01),
        "w_gate_up": nrm(ks[11], (L, E, D, 2 * F), D ** -0.5),
        "b_gate_up": nrm(ks[12], (L, E, 2 * F), 0.02),
        "w_down": nrm(ks[13], (L, E, F, D), F ** -0.5 * DEEPNORM_BETA_3),
        "b_down": nrm(ks[14], (L, E, D), 0.02),
        "ln2_g": 1.0 + nrm(ks[15], (L, D), 0.02),
        "ln2_b": nrm(ks[16], (L, D), 0.02),
        "ple_proj": nrm(ks[17], (L, PLE_DIM, D), PLE_DIM ** -0.5 * DEEPNORM_BETA_3),
        "ple_gate_w": nrm(ks[18], (L, D, D), D ** -0.5),
        "ple_gate_b": nrm(ks[19], (L, D), 0.02),
        "ln3_g": 1.0 + nrm(ks[20], (L, D), 0.02),
        "ln3_b": nrm(ks[21], (L, D), 0.02),
    }

def third_block(x, p, w_in, pool_mix, pool_scale, conv_w, w_out, ln1_g, ln1_b,
              router_w, router_b, w_gate_up, b_gate_up, w_down, b_down,
              ln2_g, ln2_b, ple_proj, ple_gate_w, ple_gate_b, ln3_g, ln3_b):
    for i in range(DEPTH):
        proj = x @ w_in[i]
        v_pool = proj[..., :D_POOL]
        b_gate = proj[..., D_POOL:D_POOL + D_CONV]
        c_gate = proj[..., D_POOL + D_CONV:D_POOL + 2 * D_CONV]
        v_conv = proj[..., D_POOL + 2 * D_CONV:]
        y_pool = pool_mixer(v_pool, pool_mix[i], pool_scale[i])
        y_conv = conv_mixer(b_gate, c_gate, v_conv, conv_w[i])
        mix = jnp.concatenate([y_pool, y_conv], axis=-1) @ w_out[i]
        x = layer_norm(DEEPNORM_ALPHA_3 * x + mix, ln1_g[i], ln1_b[i])
        ffn = moe(x, router_w[i], router_b[i], w_gate_up[i], b_gate_up[i], w_down[i], b_down[i])
        x = layer_norm(DEEPNORM_ALPHA_3 * x + ffn, ln2_g[i], ln2_b[i])
        gate = jax.nn.sigmoid((x @ ple_gate_w[i] + ple_gate_b[i]).astype(jnp.float32)).astype(x.dtype)
        ple = p[i] @ ple_proj[i]
        x = layer_norm(DEEPNORM_ALPHA_3 * x + gate * ple, ln3_g[i], ln3_b[i])
    return x


_first_inputs_3 = third_inputs


def third_inputs(seed=0):
    import zlib

    import numpy as np

    out = dict(_first_inputs_3(seed))
    spreads = {}
    factors = {'router_b': 2.977,
     'b_gate_up': 8.0,
     'b_down': 6.63,
     'ln2_g': 2.952,
     'ln2_b': 2.944,
     'ple_gate_b': 8.0,
     'ln3_g': 2.952,
     'ln3_b': 2.749}
    for name, (base, spread) in spreads.items():
        noise = np.random.default_rng([zlib.crc32(name.encode()), seed]).standard_normal(out[name].shape)
        drawn = base * np.exp(spread * noise) if base else spread * noise
        out[name] = __import__('jax').numpy.asarray(drawn.astype(out[name].dtype))
    for name, factor in factors.items():
        out[name] = (out[name] * factor).astype(out[name].dtype)
    return out


_narrow_inputs_3 = third_inputs


def third_inputs(seed=0):

    out = dict(_narrow_inputs_3(seed))
    wider = {'ln2_g': 3.23, 'ln2_b': 3.23, 'ple_gate_b': 12.0, 'ln3_g': 3.32, 'ln3_b': 3.32}
    for name, times in wider.items():
        mean = out[name].mean()
        out[name] = (mean + times * (out[name] - mean)).astype(out[name].dtype)
    return out


def setup_inputs(seed=0):
    out = dict(first_inputs(seed))
    for name, value in second_inputs(seed + 1).items():
        if name != "x":
            out[name + "_2"] = value
    for name, value in third_inputs(seed + 2).items():
        if name != "x":
            out[name + "_3"] = value
    return out


def reference(
    x, norm_mix, w_in, mlstm_conv_w, mlstm_conv_b, i_bias, f_bias, mlstm_norm, idx_k_norm,
    rel_bias, w_out, norm_ffn, w_up, ffn_conv_w, ffn_conv_b, w_down, norm_final, c_2, w_ada_2,
    b_ada_2, w_in_2, b_gate_2, hgrn_lb_logits_2, hgrn_norm_w_2, w_proj_a_2, gmlp_ln_w_2,
    gmlp_ln_b_2, gmlp_ws_2, gmlp_bs_2, w_proj_b_2, w_out_2, ln1_w_2, ln1_b_2, w_ffn_in_2,
    w_ffn_out_2, ln2_w_2, ln2_b_2, p_3, w_in_3, pool_mix_3, pool_scale_3, conv_w_3, w_out_3,
    ln1_g_3, ln1_b_3, router_w_3, router_b_3, w_gate_up_3, b_gate_up_3, w_down_3, b_down_3,
    ln2_g_3, ln2_b_3, ple_proj_3, ple_gate_w_3, ple_gate_b_3, ln3_g_3, ln3_b_3,
):
    x = first_block(
        x, norm_mix, w_in, mlstm_conv_w, mlstm_conv_b, i_bias, f_bias, mlstm_norm, idx_k_norm,
        rel_bias, w_out, norm_ffn, w_up, ffn_conv_w, ffn_conv_b, w_down, norm_final,
    )
    x = second_block(
        x, c_2, w_ada_2, b_ada_2, w_in_2, b_gate_2, hgrn_lb_logits_2, hgrn_norm_w_2, w_proj_a_2,
        gmlp_ln_w_2, gmlp_ln_b_2, gmlp_ws_2, gmlp_bs_2, w_proj_b_2, w_out_2, ln1_w_2, ln1_b_2,
        w_ffn_in_2, w_ffn_out_2, ln2_w_2, ln2_b_2,
    )
    return third_block(
        x, p_3, w_in_3, pool_mix_3, pool_scale_3, conv_w_3, w_out_3, ln1_g_3, ln1_b_3,
        router_w_3, router_b_3, w_gate_up_3, b_gate_up_3, w_down_3, b_down_3, ln2_g_3, ln2_b_3,
        ple_proj_3, ple_gate_w_3, ple_gate_b_3, ln3_g_3, ln3_b_3,
    )


_drawn_inputs = setup_inputs


def setup_inputs(seed=0):
    import zlib

    import numpy as np

    out = dict(_drawn_inputs(seed))
    spreads = {}
    factors = {'pool_scale_3': 3.314}
    for name, (base, spread) in spreads.items():
        noise = np.random.default_rng([zlib.crc32(name.encode()), seed]).standard_normal(out[name].shape)
        drawn = base * np.exp(spread * noise) if base else spread * noise
        out[name] = __import__('jax').numpy.asarray(drawn.astype(out[name].dtype))
    for name, factor in factors.items():
        out[name] = (out[name] * factor).astype(out[name].dtype)
    return out
```

```python
from contextlib import ExitStack

import numpy as np

import concourse.bass as bass
from concourse import mybir

F32 = mybir.dt.float32
I32 = mybir.dt.int32
U32 = mybir.dt.uint32
ALU = mybir.AluOpType
ACT = mybir.ActivationFunctionType
AX_X = mybir.AxisListType.X

P = 128
S = 512
D = 1024
DT = D // P
TT = S // P
PANEL = 512
KT = 8
SLOTS = 2
BANKS = 8

MH, M_DQK, M_DV, M_CONV = 4, 64, 128, 4
AH, ADH, IH, IDIM = 8, 64, 8, 64
TOPK = min(256, S // 4)
REL_BUCKETS = 32
DFF = 2816
FT = DFF // P
FFN_CONV = 3
EPS_RMS, EPS_LN = 1e-6, 1e-5
HH, SUB, CHUNK = 8, 16, 64
NCH = S // CHUNK
ALPHA = 2.0 ** 0.25
WINDOWS = (2, 4, 8, 16)
NE, TOPE, PLE = 32, 4, 256
SW_LIMIT, SW_ALPHA = 7.0, 1.702
ROWS = 128
NBLK = (S * TOPE) // ROWS + NE - 1
TABLE = NBLK + 1

MASKED, TAKEN, ACAUSAL = -1e30, -2e38, -3e38

FFN_PANELS = FT // 2


class Columns:

    def __init__(self):
        self.at, self.n = {}, 0

    def add(self, name, n):
        self.at[name] = self.n
        self.n += n


COLS = Columns()
for _name, _n in (
    ("norm_mix", DT), ("conv_w", M_CONV * 4), ("conv_b", 4), ("i_bias", 1), ("f_bias", 1),
    ("mlstm_norm", MH), ("idx_norm", 1), ("norm_ffn", DT), ("ffn_conv", FFN_PANELS * 16),
    ("norm_final", DT),
    ("c2", DT), ("b_ada", 48), ("b_gate", 2 * DT), ("lb0", HH), ("lb1", HH), ("hgrn_norm", 1),
    ("ln1_w2", DT), ("ln1_b2", DT), ("ln2_w2", DT), ("ln2_b2", DT),
    ("conv_w3", 3 * 4), ("pool_scale", 4), ("ln1_g3", DT), ("ln1_b3", DT), ("ln2_g3", DT), ("ln2_b3", DT),
    ("ple_b", DT), ("ln3_g3", DT), ("ln3_b3", DT),
):
    COLS.add(_name, _n)

PANELS = (
    ("w_in", 8), ("w_out", 2), ("w_up", 11), ("w_down", 6),
    ("w_ada", 12), ("w_zi", 2), ("w_head", 8), ("w_mix_a", 4), ("w_zv", 2), ("w_mix_b", 4),
    ("w_out_2", 2), ("w_ffn_in", 11), ("w_ffn_out", 6),
    ("w_in_3", 4), ("w_out_3", 2), ("ple_proj", 1), ("ple_gate", 2),
)
FIRST = {}
_n = 0
for _name, _c in PANELS:
    FIRST[_name] = _n
    _n += _c
N_PANELS = _n


class Ring:

    def __init__(self, tile, source, landed):
        self.tile, self.source, self.landed = tile, source, landed
        self.loaded, self.freed = 0, {}

    def load_until(self, sp, end):
        for n in range(self.loaded, min(end, N_PANELS)):
            if n - SLOTS in self.freed:
                sp.wait_ge(*self.freed[n - SLOTS])
            sp.dma_start(self.tile[:, n % SLOTS, :], self.source[n]).then_inc(self.landed[n % SLOTS], 16)
        self.loaded = max(self.loaded, min(end, N_PANELS))

    def wait_landed(self, pe, n):
        pe.wait_ge(self.landed[n % SLOTS], 16 * (n // SLOTS + 1))

    def weights(self, n, k, col, width):
        return self.tile[:, n % SLOTS, k * PANEL + col:k * PANEL + col + width]


def tile_of(t, i):
    return t[:, i, :]


def norm_stage(g, name, src, dst, scale, eps, ones_mean, bias=None, centre=False, tiles=DT, last_panel=0):
    nc, ring, psum, eps_col = g.nc, g.ring, g.psum, g.eps[eps]
    with ExitStack() as own:
        sem = g.stage_semaphores(name)
        squares = own.enter_context(nc.sbuf_tensor(f"{name}_squares", [P, 2, S], F32))
        std = own.enter_context(nc.sbuf_tensor(f"{name}_std", [P, S], F32))
        rstd = own.enter_context(nc.sbuf_tensor(f"{name}_rstd", [P, S], F32))
        mean_ready, centred, squared, summed = sem("mean_ready"), sem("centred"), sem("squared"), sem("summed")
        std_ready, rstd_ready, scaled = sem("std_ready"), sem("rstd_ready"), sem("scaled")
        mean, var = psum[:, 0, :], psum[:, 1, :]
        body = dst if centre else src
        with nc.Block(no_gpsimd_drain=True) as block:

            @block.tensor
            def _(pe):
                if centre:
                    for t in range(tiles):
                        mm = pe.matmul(mean, ones_mean, tile_of(src, t), start=t == 0, stop=t == tiles - 1)
                    mm.then_inc(mean_ready, 1)
                for t in range(tiles):
                    pe.wait_ge(squared, t + 1)
                    pe.matmul(var, ones_mean, squares[:, t % 2, :], start=t == 0, stop=t == tiles - 1)\
                        .then_inc(summed, 1)

            @block.sync
            def _(sp):
                g.clear_past(sp)
                ring.load_until(sp, last_panel)

            @block.scalar
            def _(act):
                for t in range(tiles):
                    if centre:
                        act.wait_ge(centred, t + 1)
                    if t >= 2:
                        act.wait_ge(summed, t - 1)
                    act.activation(squares[:, t % 2, :], tile_of(body, t), ACT.Square).then_inc(squared, 1)
                act.wait_ge(summed, tiles)
                act.activation(std[:, :], var, ACT.Sqrt, bias=eps_col).then_inc(std_ready, 1)
                if bias is not None:
                    for t in range(tiles):
                        act.wait_ge(scaled, t + 1)
                        act.activation(tile_of(dst, t), tile_of(dst, t), ACT.Identity, bias=bias(t))

            @block.vector
            def _(dve):
                if centre:
                    dve.wait_ge(mean_ready, 1)
                    for t in range(tiles):
                        dve.tensor_tensor(tile_of(dst, t), tile_of(src, t), mean, ALU.subtract).then_inc(centred, 1)
                dve.wait_ge(std_ready, 1)
                dve.reciprocal(rstd[:, :], std[:, :]).then_inc(rstd_ready, 1)
                dve.wait_ge(rstd_ready, 1)
                if centre:
                    dve.wait_ge(centred, tiles)
                for t in range(tiles):
                    dve.scalar_tensor_tensor(tile_of(dst, t), tile_of(body, t), scale(t), rstd[:, :],
                                             ALU.mult, ALU.mult).then_inc(scaled, 1)


class Tile:

    def __init__(self, panels, col, width, rhs, out, engine, take, tokens=None, kts=(KT,)):
        self.panels, self.col, self.width, self.rhs, self.out = panels, col, width, rhs, out
        self.engine, self.take, self.tokens, self.kts = engine, take, tokens, kts


def dense_stage(g, name, tiles, last_panel, before_dve=None):
    nc, ring, psum = g.nc, g.ring, g.psum
    with ExitStack() as own:
        sem = g.stage_semaphores(name)
        tile_ready, act_took, dve_took = sem("tile_ready"), sem("act_took"), sem("dve_took")
        taken = {"act": [], "dve": []}
        for t in tiles:
            for e, counts in taken.items():
                counts.append((counts[-1] if counts else 0) + (t.engine == e))
        with nc.Block(no_gpsimd_drain=True) as block:

            @block.tensor
            def _(pe):
                for i, t in enumerate(tiles):
                    if i >= BANKS:
                        e = tiles[i - BANKS].engine
                        pe.wait_ge(act_took if e == "act" else dve_took, taken[e][i - BANKS])
                    bank = psum[:, i % BANKS, :]
                    k0, total = 0, sum(t.kts)
                    for n, kt in zip(t.panels, t.kts):
                        ring.wait_landed(pe, n)
                        for k in range(kt):
                            w = ring.weights(n, k, t.col, t.width)
                            x = tile_of(t.rhs, k0 + k)
                            if t.tokens is None:
                                a, b, out = w, x, bank[0:t.width, :]
                            else:
                                a, b, out = x[:, t.tokens * P:(t.tokens + 1) * P], w, bank[:, 0:t.width]
                            mm = pe.matmul(out, a, b, start=k0 + k == 0, stop=k0 + k == total - 1)
                        k0 += kt
                        ring.freed[n] = (tile_ready, i + 1)
                    mm.then_inc(tile_ready, 1)

            @block.sync
            def _(sp):
                g.clear_past(sp)
                ring.load_until(sp, last_panel)

            @block.scalar
            def _(act):
                for i, t in enumerate(tiles):
                    if t.engine == "act":
                        act.wait_ge(tile_ready, i + 1)
                        t.take(act, psum[:, i % BANKS, :]).then_inc(act_took, 1)

            @block.vector
            def _(dve):
                if before_dve is not None:
                    before_dve(dve)
                for i, t in enumerate(tiles):
                    if t.engine == "dve":
                        dve.wait_ge(tile_ready, i + 1)
                        t.take(dve, psum[:, i % BANKS, :]).then_inc(dve_took, 1)


def feed_forward(g, name, x, h, mid, taps, up, down, combine, conv):
    nc, ring, psum, cols = g.nc, g.ring, g.psum, g.cols
    with ExitStack() as own:
        sem = g.stage_semaphores(name)
        gate_val = own.enter_context(nc.sbuf_tensor(f"{name}_gate_val", [P, 2, 2, S], F32))
        gate_act = own.enter_context(nc.sbuf_tensor(f"{name}_gate_act", [P, 2, S], F32))
        up_ready = [sem(f"up_ready{q}") for q in range(2)]
        based, tapped, silued, made = sem("based"), sem("tapped"), sem("silued"), sem("made")
        half = [psum[:, 4 * q:4 * q + 4, :] for q in range(2)]
        loops = FFN_PANELS // 2
        last = FFN_PANELS - 1

        with nc.Block(no_gpsimd_drain=True) as block:

            @block.tensor
            def _(pe):
                n0 = FIRST[up]
                with pe.Fori(0, loops) as i:
                    for q in range(2):
                        n = n0 + q
                        pe.wait_ge(ring.landed[n % SLOTS], 16 * (n // SLOTS + 1) + i * 16)
                        pe.wait_ge(made, i * 4 + 2 * q + 2)
                        for m in range(4):
                            for k in range(KT):
                                mm = pe.matmul(half[q][:, m, :], ring.weights(n, k, m * P, P), tile_of(h, k),
                                               start=k == 0, stop=k == KT - 1)
                            mm.then_inc(up_ready[q], 1)
                n = n0 + last
                ring.wait_landed(pe, n)
                pe.wait_ge(made, 4 + 2 * (last - 1))
                for m in range(4):
                    for k in range(KT):
                        mm = pe.matmul(half[0][:, m, :], ring.weights(n, k, m * P, P), tile_of(h, k),
                                       start=k == 0, stop=k == KT - 1)
                    mm.then_inc(up_ready[0], 1)
                for p in range(FFN_PANELS):
                    ring.freed[n0 + p] = (up_ready[p % 2], 4 * (p // 2 + 1))

            @block.sync
            def _(sp):
                g.clear_past(sp)
                ring.load_until(sp, FIRST[up] + FFN_PANELS + SLOTS)

            def act_pair(act, q, j, ready, pair, column):
                buf = j
                act.wait_ge(up_ready[q], ready)
                act.wait_ge(made, pair + 3)
                if conv:
                    for part in range(2):
                        act.activation(gate_val[:, buf, part, :], half[q][:, 2 * part + j, :], ACT.Identity,
                                       scale=column(2, part, j), bias=column(3, part, j)).then_inc(based, 1)
                    act.wait_ge(tapped, (pair + 1) * 2)
                    act.activation(gate_act[:, buf, :], gate_val[:, buf, 0, :], ACT.Silu).then_inc(silued, 1)
                else:
                    act.activation(gate_act[:, buf, :], half[q][:, j, :], ACT.Silu).then_inc(silued, 1)

            def dve_pair(dve, q, j, ready, pair, column, out):
                buf = j
                if conv:
                    dve.wait_ge(based, (pair + 1) * 2)
                    for tap, back in ((1, 1), (0, 2)):
                        if tap == 0:
                            dve.wait_ge(first_tap, (pair + 1) * 2)
                        for part in range(2):
                            to = gate_val[:, buf, part, back:]
                            dve.scalar_tensor_tensor(to, half[q][:, 2 * part + j, 0:S - back],
                                                     column(tap, part, j), to, ALU.mult, ALU.add)\
                                .then_inc(first_tap if tap else tapped, 1)
                    dve.wait_ge(tapped, (pair + 1) * 2)
                    dve.wait_ge(silued, pair + 1)
                    dve.tensor_tensor(out, gate_act[:, buf, :], gate_val[:, buf, 1, :], ALU.mult).then_inc(made, 1)
                else:
                    dve.wait_ge(silued, pair + 1)
                    dve.tensor_tensor(out, gate_act[:, buf, :], half[q][:, 2 + j, :], ALU.mult).then_inc(made, 1)

            first_tap = sem("first_tap")

            def column(base):
                return lambda tap, part, j: cols[:, bass.ds(base + 4 * tap + 2 * part + j, 1)]

            @block.scalar
            def _(act):
                with act.Fori(0, loops) as i:
                    for q in range(2):
                        for j in range(2):
                            act_pair(act, q, j, i * 4 + 3 + j, i * 4 + 2 * q + j, column(i * 32 + taps + 16 * q))
                for j in range(2):
                    act_pair(act, 0, j, loops * 4 + 3 + j, 2 * last + j, column(taps + 16 * last))

            @block.vector
            def _(dve):
                for _ in range(4):
                    dve.sem_inc(made, 1)
                with dve.Fori(0, loops) as i:
                    for q in range(2):
                        for j in range(2):
                            pair = i * 4 + 2 * q + j
                            dve_pair(dve, q, j, None, pair, column(i * 32 + taps + 16 * q),
                                     mid[:, bass.ds(pair, 1), :].rearrange("p a s -> p (a s)"))
                for j in range(2):
                    dve_pair(dve, 0, j, None, 2 * last + j, column(taps + 16 * last), tile_of(mid, 2 * last + j))

    n0 = FIRST[down]
    tiles = []
    for c in range(2):
        for m in range(4):
            t = 4 * c + m
            tiles.append(Tile([n0 + 3 * c + p for p in range(3)], m * P, P, mid, None, "dve", combine(t),
                              kts=(KT, KT, FT - 2 * KT)))
    wide_stage(g, name + "_down", tiles, n0 + 6 + SLOTS)


def wide_stage(g, name, tiles, last_panel):
    nc, ring, psum = g.nc, g.ring, g.psum
    with ExitStack() as own:
        sem = g.stage_semaphores(name)
        part_done, tile_ready, took = sem("part_done"), sem("tile_ready"), sem("took")
        with nc.Block(no_gpsimd_drain=True) as block:

            @block.tensor
            def _(pe):
                parts = 0
                for c in range(0, len(tiles), 4):
                    group = tiles[c:c + 4]
                    k0, total = 0, sum(group[0].kts)
                    for n, kt in zip(group[0].panels, group[0].kts):
                        ring.wait_landed(pe, n)
                        for m, t in enumerate(group):
                            for k in range(kt):
                                mm = pe.matmul(psum[:, c % BANKS + m, :], ring.weights(n, k, t.col, P),
                                               tile_of(t.rhs, k0 + k), start=k0 + k == 0, stop=k0 + k == total - 1)
                            if k0 + kt == total:
                                mm.then_inc(tile_ready, 1)
                        k0 += kt
                        if k0 < total:
                            mm.then_inc(part_done, 1)
                            parts += 1
                            ring.freed[n] = (part_done, parts)
                        else:
                            ring.freed[n] = (tile_ready, c + 4)

            @block.sync
            def _(sp):
                g.clear_past(sp)
                ring.load_until(sp, last_panel)

            @block.vector
            def _(dve):
                for i, t in enumerate(tiles):
                    dve.wait_ge(tile_ready, i + 1)
                    t.take(dve, psum[:, i % BANKS, :]).then_inc(took, 1)


def mlstm_stage(g, b1, mix):
    nc, ring, psum, cols, col = g.nc, g.ring, g.psum, g.cols, g.col
    with ExitStack() as own:
        sb = lambda n, shape: own.enter_context(nc.sbuf_tensor(f"ml_{n}", shape, F32))
        sem = g.stage_semaphores("ml")
        conv = sb("conv", [P, 4, S])
        f_pre, f_abs, f_exp, f_log = (sb(n, [MH, S]) for n in ("f_pre", "f_abs", "f_exp", "f_log"))
        logf, cum, i_row, a_row, max_row, m_row = (sb(n, [MH, S]) for n in ("logf", "cum", "i_row", "a_row", "max_row", "m_row"))
        ones_row = sb("ones_row", [MH, S])
        a_col = sb("a_col", [P, TT, MH])
        weight, prob = (sb(n, [P, TT, S]) for n in ("weight", "prob"))
        floor, den, num, sq = (sb(n, [P, 2, S]) for n in ("floor", "den", "num", "sq"))
        std, rstd = sb("std", [P, S]), sb("rstd", [P, S])
        base_done, tap_done, conv_done, qk_ready = sem("base_done"), sem("tap_done"), sem("conv_done"), sem("qk_ready")
        row_act, row_dve, rows_ready, acol_psum, acol_ready = (sem(n) for n in ("row_act", "row_dve", "rows_ready", "acol_psum", "acol_ready"))
        spread, floored, arg_ready, weight_ready, score_ready = (sem(n) for n in ("spread", "floored", "arg_ready", "weight_ready", "score_ready"))
        scaled, prob_ready, summed, den_ready, inv_ready, num_ready = (sem(n) for n in ("scaled", "prob_ready", "summed", "den_ready", "inv_ready", "num_ready"))
        squared, sq_summed, std_ready, rstd_ready, normed, mixed, ones_set, absed = (sem(n) for n in ("squared", "sq_summed", "std_ready", "rstd_ready", "normed", "mixed", "ones_set", "absed"))
        max_bank, m_bank, num_bank, den_bank = psum[:, 4, :], psum[:, 5, :], psum[:, 6, :], psum[:, 7, :]

        def of_head(h, first):
            return first + h // 2, slice(64 * (h % 2), 64 * (h % 2) + 64)

        with nc.Block(no_gpsimd_drain=True) as block:

            @block.sync
            def _(sp):
                g.clear_past(sp)
                ring.load_until(sp, FIRST["w_out"] + SLOTS)

            @block.scalar
            def _(act):
                act.activation(f_pre[:, :], b1["f_raw"][:, :], ACT.Identity, bias=col("f_bias")[0:MH]).then_inc(row_act, 1)
                act.activation(i_row[:, :], b1["i_raw"][:, :], ACT.Identity, bias=col("i_bias")[0:MH]).then_inc(row_act, 1)
                act.wait_ge(row_act, 1)
                act.activation(f_abs[:, :], f_pre[:, :], ACT.Abs).then_inc(row_act, 1)
                act.wait_ge(row_act, 3)
                act.activation(f_exp[:, :], f_abs[:, :], ACT.Exp, scale=-1.0).then_inc(row_act, 1)
                act.wait_ge(row_act, 4)
                act.activation(f_log[:, :], f_exp[:, :], ACT.Ln, bias=1.0).then_inc(row_act, 1)
                for t in range(4):
                    act.activation(conv[:, t, :], b1["qk"][:, t, :], ACT.Identity, scale=col("conv_w", 3 * 4 + t),
                                   bias=col("conv_b", t)).then_inc(base_done, 1)
                for t in range(4):
                    act.wait_ge(conv_done, t + 1)
                    act.activation(b1["qk"][:, t, :], conv[:, t, :], ACT.Silu).then_inc(qk_ready, 1)
                for h in range(MH):
                    act.wait_ge(spread, 2 * h + 2)
                    if h >= 2:
                        act.wait_ge(den_ready, h - 1)
                    act.activation(floor[:, h % 2, :], m_bank, ACT.Exp).then_inc(floored, 1)
                    for j in range(TT):
                        w = S - P * j
                        act.wait_ge(arg_ready, TT * h + j + 1)
                        act.activation(weight[:, j, 0:w], weight[:, j, 0:w], ACT.Exp).then_inc(weight_ready, 1)
                    act.wait_ge(summed, h + 1)
                    if h >= 2:
                        act.wait_ge(num_ready, h - 1)
                    act.activation(den[:, h % 2, :], den_bank, ACT.Abs).then_inc(absed, 1)
                    act.wait_ge(num_ready, h + 1)
                    if h >= 2:
                        act.wait_ge(sq_summed, h - 1)
                    act.activation(sq[:, h % 2, :], num[:, h % 2, :], ACT.Square).then_inc(squared, 1)
                    act.wait_ge(sq_summed, h + 1)
                    if h >= 1:
                        act.wait_ge(rstd_ready, h)
                    act.activation(std[:, :], m_bank, ACT.Sqrt, scale=1.0 / M_DV, bias=g.eps[EPS_RMS]).then_inc(std_ready, 1)

            @block.tensor
            def _(pe):
                pe.wait_ge(rows_ready, 2)
                for j in range(TT):
                    mm = pe.matmul(psum[:, 0, MH * j:MH * j + MH], a_row[:, j * P:(j + 1) * P], g.ident[0:MH, 0:MH],
                                   start=True, stop=True)
                mm.then_inc(acol_psum, 1)
                pe.wait_ge(qk_ready, 4)
                pe.wait_ge(acol_ready, 1)
                for h in range(MH):
                    if h >= 1:
                        pe.wait_ge(arg_ready, TT * h)
                        pe.wait_ge(std_ready, h)
                    pe.matmul(max_bank, g.neg_head[:, h, :], max_row[:, :], start=True, stop=True).then_inc(spread, 1)
                    pe.matmul(m_bank, g.neg_head[:, h, :], m_row[:, :], start=True, stop=True).then_inc(spread, 1)
                    tq, pq = of_head(h, 0)
                    tk, pk = of_head(h, 2)
                    for j in range(TT):
                        if h >= 1:
                            pe.wait_ge(scaled, TT * (h - 1) + j + 1)
                        pe.matmul(psum[:, j, 0:S - P * j], b1["qk"][pk, tk, j * P:(j + 1) * P], b1["qk"][pq, tq, j * P:S],
                                  start=True, stop=True).then_inc(score_ready, 1)
                    if h >= 1:
                        pe.wait_ge(num_ready, h)
                    for j in range(TT):
                        pe.wait_ge(prob_ready, TT * h + j + 1)
                        w = S - P * j
                        pe.matmul(num_bank[:, P * j:S], b1["mv"][:, j, h * M_DV:(h + 1) * M_DV], prob[:, j, 0:w],
                                  start=j == 0, stop=j == TT - 1)
                        mm = pe.matmul(den_bank[:, P * j:S], g.ones, prob[:, j, 0:w], start=j == 0, stop=j == TT - 1)
                    mm.then_inc(summed, 1)
                    pe.wait_ge(squared, h + 1)
                    pe.wait_ge(floored, h + 1)
                    pe.matmul(m_bank, g.ones, sq[:, h % 2, :], start=True, stop=True).then_inc(sq_summed, 1)

            @block.vector
            def _(dve):
                dve.memset(ones_row[:, :], 1.0).then_inc(ones_set, 1)
                dve.wait_ge(row_act, 5)
                dve.scalar_tensor_tensor(logf[:, :], f_pre[:, :], 0.0, f_log[:, :], ALU.min, ALU.subtract).then_inc(row_dve, 1)
                dve.wait_ge(row_dve, 1)
                dve.wait_ge(ones_set, 1)
                dve.tensor_tensor_scan(cum[:, :], ones_row[:, :], logf[:, :], 0.0, ALU.mult, ALU.add).then_inc(row_dve, 1)
                dve.wait_ge(row_dve, 2)
                dve.tensor_tensor(a_row[:, :], i_row[:, :], cum[:, :], ALU.subtract).then_inc(rows_ready, 1)
                dve.wait_ge(rows_ready, 1)
                dve.tensor_tensor_scan(max_row[:, :], a_row[:, :], a_row[:, :], 0.0, ALU.max, ALU.max).then_inc(row_dve, 1)
                dve.wait_ge(row_dve, 3)
                dve.tensor_tensor(m_row[:, :], cum[:, :], max_row[:, :], ALU.add).then_inc(rows_ready, 1)
                for t in range(4):
                    dve.wait_ge(base_done, t + 1)
                    for tap in (2, 1, 0):
                        back = M_CONV - 1 - tap
                        if tap < 2:
                            dve.wait_ge(tap_done, 2 * t + 2 - tap)
                        to = conv[:, t, back:]
                        dve.scalar_tensor_tensor(to, b1["qk"][:, t, 0:S - back], col("conv_w", tap * 4 + t), to,
                                                 ALU.mult, ALU.add).then_inc(tap_done if tap else conv_done, 1)
                dve.wait_ge(acol_psum, 1)
                dve.tensor_copy(a_col[:, :, :], psum[:, 0, 0:TT * MH].rearrange("p (j h) -> p j h", h=MH)).then_inc(acol_ready, 1)
                dve.wait_ge(acol_ready, 1)
                for h in range(MH):
                    b = h % 2
                    dve.wait_ge(spread, 2 * h + 1)
                    for j in range(TT):
                        w = S - P * j
                        if h >= 1:
                            dve.wait_ge(scaled, TT * (h - 1) + j + 1)
                        dve.tensor_scalar(weight[:, j, 0:w], max_bank[:, P * j:S], a_col[:, j, h:h + 1], 0.0,
                                          ALU.add, ALU.min).then_inc(arg_ready, 1)
                    for j in range(TT):
                        w = S - P * j
                        dve.wait_ge(weight_ready, TT * h + j + 1)
                        dve.wait_ge(score_ready, TT * h + j + 1)
                        dve.scalar_tensor_tensor(prob[:, j, 0:w], psum[:, j, 0:w], M_DQK ** -0.5, weight[:, j, 0:w],
                                                 ALU.mult, ALU.mult).then_inc(scaled, 1)
                        dve.wait_ge(scaled, TT * h + j + 1)
                        dve.tensor_tensor(prob[:, j, 0:P], prob[:, j, 0:P], g.upper, ALU.mult).then_inc(prob_ready, 1)
                    dve.wait_ge(floored, h + 1)
                    dve.wait_ge(absed, h + 1)
                    dve.tensor_tensor(den[:, b, :], den[:, b, :], floor[:, b, :], ALU.max).then_inc(den_ready, 1)
                    dve.wait_ge(den_ready, h + 1)
                    dve.reciprocal(den[:, b, :], den[:, b, :]).then_inc(inv_ready, 1)
                    dve.wait_ge(inv_ready, h + 1)
                    if h >= 2:
                        dve.wait_ge(squared, h - 1)
                    dve.tensor_tensor(num[:, b, :], num_bank, den[:, b, :], ALU.mult).then_inc(num_ready, 1)
                    dve.wait_ge(std_ready, h + 1)
                    dve.reciprocal(rstd[:, :], std[:, :]).then_inc(rstd_ready, 1)
                    dve.wait_ge(rstd_ready, h + 1)
                    dve.scalar_tensor_tensor(mix[:, h, :], num[:, b, :], col("mlstm_norm", h), rstd[:, :],
                                             ALU.mult, ALU.mult).then_inc(normed, 1)
                    dve.wait_ge(normed, h + 1)
                    dve.tensor_tensor(mix[:, h, :], mix[:, h, :], b1["o_gate"][:, h, :], ALU.mult).then_inc(mixed, 1)


def index_stage(g, b1, mask):
    nc, ring, psum, cols, col = g.nc, g.ring, g.psum, g.cols, g.col
    with ExitStack() as own:
        sb = lambda n, shape: own.enter_context(nc.sbuf_tensor(f"ix_{n}", shape, F32))
        sem = g.stage_semaphores("ix")
        sq, std, rstd = sb("sq", [P, S]), sb("std", [P, S]), sb("rstd", [P, S])
        keys = sb("keys", [P, S])
        relued = sb("relued", [P, 4, S])
        work = sb("work", [P, TT, S])
        best = sb("best", [P, TT, 8])
        squared, sq_summed, std_ready, rstd_ready, keys_ready = (sem(n) for n in ("squared", "sq_summed", "std_ready", "rstd_ready", "keys_ready"))
        raw_ready, relu_ready, added, limited, found, replaced, masked = (sem(n) for n in ("raw_ready", "relu_ready", "added", "limited", "found", "replaced", "masked"))
        with nc.Block(no_gpsimd_drain=True) as block:

            @block.sync
            def _(sp):
                g.clear_past(sp)
                ring.load_until(sp, FIRST["w_out"] + SLOTS)

            @block.scalar
            def _(act):
                act.activation(sq[:, :], b1["ik"][:, :], ACT.Square).then_inc(squared, 1)
                act.wait_ge(sq_summed, 1)
                act.activation(std[:, :], psum[:, 0, :], ACT.Sqrt, scale=1.0 / IDIM, bias=g.eps[EPS_RMS]).then_inc(std_ready, 1)
                n = 0
                for i in range(TT):
                    for h in range(IH):
                        act.wait_ge(raw_ready, n + 1)
                        if n >= 4:
                            act.wait_ge(added, n - 3)
                        w = P * (i + 1)
                        act.activation(relued[:, n % 4, 0:w], psum[:, n % BANKS, 0:w], ACT.Relu, scale=IDIM ** -0.5)\
                            .then_inc(relu_ready, 1)
                        n += 1

            @block.tensor
            def _(pe):
                pe.wait_ge(squared, 1)
                pe.matmul(psum[:, 0, :], g.half_ones, sq[:, :], start=True, stop=True).then_inc(sq_summed, 1)
                pe.wait_ge(keys_ready, 1)
                n = 0
                for i in range(TT):
                    for h in range(IH):
                        if n >= BANKS:
                            pe.wait_ge(relu_ready, n - BANKS + 1)
                        half = slice(64 * (h % 2), 64 * (h % 2) + 64)
                        w = P * (i + 1)
                        pe.matmul(psum[:, n % BANKS, 0:w], b1["iq"][half, h // 2, i * P:(i + 1) * P], keys[half, 0:w],
                                  start=True, stop=True).then_inc(raw_ready, 1)
                        n += 1

            @block.vector
            def _(dve):
                dve.wait_ge(std_ready, 1)
                dve.reciprocal(rstd[:, :], std[:, :]).then_inc(rstd_ready, 1)
                dve.wait_ge(rstd_ready, 1)
                dve.scalar_tensor_tensor(keys[:, :], b1["ik"][:, :], col("idx_norm"), rstd[:, :], ALU.mult, ALU.mult)\
                    .then_inc(keys_ready, 1)
                n = 0
                for i in range(TT):
                    w = P * (i + 1)
                    for h in range(IH):
                        dve.wait_ge(relu_ready, n + 1)
                        if h == 0:
                            dve.tensor_scalar(work[:, i, 0:w], relued[:, n % 4, 0:w], b1["iw"][:, i, 0:1], None,
                                              ALU.mult).then_inc(added, 1)
                        else:
                            dve.wait_ge(added, n)
                            dve.scalar_tensor_tensor(work[:, i, 0:w], relued[:, n % 4, 0:w], b1["iw"][:, i, h:h + 1],
                                                     work[:, i, 0:w], ALU.mult, ALU.add).then_inc(added, 1)
                        n += 1
                for i in range(1, TT):
                    dve.wait_ge(added, IH * (i + 1))
                    d = work[:, i, P * i:P * i + P]
                    dve.tensor_tensor(d, d, g.acausal, ALU.min).then_inc(limited, 1)
                dve.tensor_copy(mask[:, 0, 0:P], g.causal_add).then_inc(masked, 1)
                for r in range(TOPK // 8):
                    for i in range(1, TT):
                        w = P * (i + 1)
                        m = (TT - 1) * r + i - 1
                        if r == 0:
                            dve.wait_ge(limited, i)
                        else:
                            dve.wait_ge(replaced, m - TT + 2)
                        dve.max(best[:, i, :], work[:, i, 0:w]).then_inc(found, 1)
                    for i in range(1, TT):
                        w = P * (i + 1)
                        dve.wait_ge(found, (TT - 1) * r + i)
                        dve.match_replace(work[:, i, 0:w], best[:, i, :], work[:, i, 0:w], TAKEN).then_inc(replaced, 1)
                for i in range(1, TT):
                    w = P * (i + 1)
                    dve.wait_ge(replaced, (TT - 1) * (TOPK // 8))
                    dve.tensor_scalar(mask[:, i, 0:w], work[:, i, 0:w], TAKEN, MASKED, ALU.not_equal, ALU.mult)\
                        .then_inc(masked, 1)


def attention_stage(g, b1, mask, rel, mix):
    nc, ring, psum = g.nc, g.ring, g.psum
    with ExitStack() as own:
        sb = lambda n, shape: own.enter_context(nc.sbuf_tensor(f"at_{n}", shape, F32))
        sem = g.stage_semaphores("at")
        logits, prob, prob_t = (sb(n, [P, 2, S]) for n in ("logits", "prob", "prob_t"))
        top, neg, total, inv = (sb(n, [P, TT * AH]) for n in ("top", "neg", "total", "inv"))
        heads = sb("heads", [P, 2, AH * ADH])
        qk_done, biased, masked, negated, exped, turned, copied = (sem(n) for n in ("qk_done", "biased", "masked", "negated", "exped", "turned", "copied"))
        pv_done, inverted, taken, mixed_t, mixed = (sem(n) for n in ("pv_done", "inverted", "taken", "mixed_t", "mixed"))
        NI = TT * AH
        with nc.Block(no_gpsimd_drain=True) as block:

            @block.sync
            def _(sp):
                g.clear_past(sp)
                ring.load_until(sp, FIRST["w_out"] + SLOTS)

            @block.tensor
            def _(pe):
                def scores(n):
                    i, h = divmod(n, AH)
                    if n >= 2:
                        pe.wait_ge(biased, n - 1)
                    half = slice(64 * (h % 2), 64 * (h % 2) + 64)
                    w = P * (i + 1)
                    pe.matmul(psum[:, n % 2, 0:w], b1["aq"][half, h // 2, i * P:(i + 1) * P],
                              b1["ak"][half, h // 2, 0:w], start=True, stop=True).then_inc(qk_done, 1)

                scores(0)
                for n in range(NI):
                    i, h = divmod(n, AH)
                    if n + 1 < NI:
                        scores(n + 1)
                    pe.wait_ge(exped, n + 1)
                    if n >= 2:
                        pe.wait_ge(copied, n - 1)
                    for j in range(i + 1):
                        mm = pe.transpose(psum[:, 2 + n % 2, j * P:(j + 1) * P], prob[:, n % 2, j * P:(j + 1) * P], g.ident)
                    mm.then_inc(turned, 1)
                    pe.wait_ge(copied, n + 1)
                    if n >= 2:
                        pe.wait_ge(taken, n - 1)
                    for j in range(i + 1):
                        mm = pe.matmul(psum[:, 4 + n % 2, 0:ADH], prob_t[:, n % 2, j * P:(j + 1) * P],
                                       b1["av"][:, j, h * ADH:(h + 1) * ADH], start=j == 0, stop=j == i)
                    mm.then_inc(pv_done, 1)
                    if h == AH - 1:
                        pe.wait_ge(taken, n + 1)
                        if i >= 2:
                            pe.wait_ge(mixed, i - 1)
                        for c in range(4):
                            mm = pe.transpose(psum[:, 6 + i % 2, c * P:(c + 1) * P], heads[:, i % 2, c * P:(c + 1) * P], g.ident)
                        mm.then_inc(mixed_t, 1)

            @block.scalar
            def _(act):
                for n in range(NI):
                    i, h = divmod(n, AH)
                    w = P * (i + 1)
                    act.wait_ge(masked, n + 1)
                    act.activation(neg[:, n:n + 1], top[:, n:n + 1], ACT.Copy, scale=-1.0).then_inc(negated, 1)
                    act.wait_ge(negated, n + 1)
                    if n >= 2:
                        act.wait_ge(turned, n - 1)
                    act.activation(prob[:, n % 2, 0:w], logits[:, n % 2, 0:w], ACT.Exp, bias=neg[:, n:n + 1],
                                   accum_out=total[:, n:n + 1]).then_inc(exped, 1)
                    act.wait_ge(turned, n + 1)
                    if n >= 2:
                        act.wait_ge(pv_done, n - 1)
                    act.activation(prob_t[:, n % 2, 0:w], psum[:, 2 + n % 2, 0:w], ACT.Copy).then_inc(copied, 1)

            @block.vector
            def _(dve):
                def soft(n):
                    i, h = divmod(n, AH)
                    w = P * (i + 1)
                    b = logits[:, n % 2, 0:w]
                    dve.wait_ge(qk_done, n + 1)
                    if n >= 2:
                        dve.wait_ge(exped, n - 1)
                    dve.scalar_tensor_tensor(b, psum[:, n % 2, 0:w], ADH ** -0.5, rel[:, h, S - w:S],
                                             ALU.mult, ALU.add).then_inc(biased, 1)
                    dve.wait_ge(biased, n + 1)
                    dve.tensor_tensor_reduce(out=b, in0=b, in1=mask[:, i, 0:w], scale=1.0, scalar=-3e38, op0=ALU.add,
                                             op1=ALU.max, accum_out=top[:, n:n + 1]).then_inc(masked, 1)

                soft(0)
                for n in range(NI):
                    i, h = divmod(n, AH)
                    if n + 1 < NI:
                        soft(n + 1)
                    dve.wait_ge(exped, n + 1)
                    dve.reciprocal(inv[:, n:n + 1], total[:, n:n + 1]).then_inc(inverted, 1)
                    dve.wait_ge(inverted, n + 1)
                    dve.wait_ge(pv_done, n + 1)
                    if i >= 2 and h == 0:
                        dve.wait_ge(mixed_t, i - 1)
                    dve.tensor_scalar(heads[:, i % 2, h * ADH:(h + 1) * ADH], psum[:, 4 + n % 2, 0:ADH], inv[:, n:n + 1],
                                      None, ALU.mult).then_inc(taken, 1)
                    if h == AH - 1:
                        dve.wait_ge(mixed_t, i + 1)
                        dve.tensor_copy(mix[:, 4:8, i * P:(i + 1) * P],
                                        psum[:, 6 + i % 2, :].rearrange("p (c q) -> p c q", q=P)).then_inc(mixed, 1)


def block_1(g, x, h):
    nc, ring, psum, col = g.nc, g.ring, g.psum, g.col
    norm_stage(g, "n1", x, h, lambda t: col("norm_mix", t), EPS_RMS, g.ones_mean, last_panel=SLOTS)
    with ExitStack() as own:
        sb = lambda n, shape: own.enter_context(nc.sbuf_tensor(f"b1_{n}", shape, F32))
        b1 = {"qk": sb("qk", [P, 4, S]), "mv": sb("mv", [P, TT, S]), "o_gate": sb("o_gate", [P, 4, S]),
              "aq": sb("aq", [P, 4, S]), "ak": sb("ak", [P, 4, S]), "av": sb("av", [P, TT, S]),
              "iq": sb("iq", [P, 4, S]), "ik": sb("ik", [P, S]), "i_raw": sb("i_raw", [MH, S]),
              "f_raw": sb("f_raw", [MH, S]), "iw": sb("iw", [P, TT, IH])}
        n0 = FIRST["w_in"]
        copy = {"act": lambda to: lambda e, bank: e.activation(to, bank[:, 0:to.shape[-1]], ACT.Copy),
                "dve": lambda to: lambda e, bank: e.tensor_copy(to, bank[:, 0:to.shape[-1]])}
        tiles = []
        for p, (name, tokens) in enumerate((("qk", 0), ("mv", 1), ("o_gate", 0), ("aq", 0), ("ak", 0), ("av", 1), ("iq", 0))):
            for m in range(4):
                to = b1[name][:, m, :]
                e = "act" if m % 2 or name == "o_gate" else "dve"
                take = copy[e](to) if name != "o_gate" else \
                    (lambda to: lambda a, bank: a.activation(to, bank, ACT.Sigmoid))(to)
                tiles.append(Tile([n0 + p], 0 if tokens else m * P, PANEL if tokens else P, h, to, e, take,
                                  tokens=m if tokens else None))
        last = [n0 + 7]
        tiles.append(Tile(last, 0, P, h, None, "dve", copy["dve"](b1["ik"][:, :])))
        for c, name in ((P, "i_raw"), (P + 4, "f_raw")):
            tiles.append(Tile(last, c, MH, h, None, "dve",
                              (lambda to: lambda e, bank: e.tensor_copy(to, bank[0:MH, :]))(b1[name][:, :])))
        for m in range(TT):
            tiles.append(Tile(last, P + 8, IH, h, None, "act",
                              (lambda to: lambda a, bank: a.activation(to, bank[:, 0:IH], ACT.Copy, scale=IH ** -0.5))(b1["iw"][:, m, :]),
                              tokens=m))
        dense_stage(g, "in1", tiles, n0 + 8 + SLOTS)
        mlstm_stage(g, b1, h)
        with nc.sbuf_tensor("mask", [P, TT, S], F32) as mask:
            index_stage(g, b1, mask)
            with nc.sbuf_tensor("rel", [P, AH, S], F32) as rel:
                rel_in = g.stage_semaphores("rel")("rel_in")
                with nc.Block(no_gpsimd_drain=True) as block:
                    @block.sync
                    def _(sp):
                        g.clear_past(sp)
                        sp.dma_start(rel[:, :, :], g.rel_bias).then_inc(rel_in, 16)
                        sp.wait_ge(rel_in, 16)
                attention_stage(g, b1, mask, rel, h)
    n0 = FIRST["w_out"]
    dense_stage(g, "out1", [
        Tile([n0 + t // 4], t % 4 * P, P, h, None, "dve",
             (lambda to: lambda e, bank: e.tensor_tensor(to, bank, to, ALU.add))(x[:, t, :])) for t in range(DT)],
        n0 + 2 + SLOTS)
    norm_stage(g, "n2", x, h, lambda t: col("norm_ffn", t), EPS_RMS, g.ones_mean, last_panel=FIRST["w_up"] + SLOTS)
    with nc.sbuf_tensor("mid1", [P, FT, S], F32) as mid:
        feed_forward(g, "ff1", x, h, mid, COLS.at["ffn_conv"], "w_up", "w_down",
                     lambda t: (lambda to: lambda e, bank: e.tensor_tensor(to, bank, to, ALU.add))(x[:, t, :]), True)
    norm_stage(g, "n3", x, x, lambda t: col("norm_final", t), EPS_RMS, g.ones_mean, last_panel=FIRST["w_ada"] + SLOTS)


def ada_stage(g, mod):
    nc, ring, psum, col = g.nc, g.ring, g.psum, g.col
    with ExitStack() as own:
        sem = g.stage_semaphores("ada")
        cond = own.enter_context(nc.sbuf_tensor("ada_cond", [P, DT], F32))
        cond_ready, panel_done, summed, plus_one = sem("cond_ready"), sem("panel_done"), sem("summed"), sem("plus_one")
        n0, count = FIRST["w_ada"], 6 * D // PANEL
        at = COLS.at["b_ada"]
        with nc.Block(no_gpsimd_drain=True) as block:

            @block.scalar
            def _(act):
                act.activation(cond[:, :], g.cols[:, COLS.at["c2"]:COLS.at["c2"] + DT], ACT.Silu).then_inc(cond_ready, 1)

            @block.tensor
            def _(pe):
                pe.wait_ge(cond_ready, 1)
                for p in range(count):
                    ring.wait_landed(pe, n0 + p)
                    for m in range(4):
                        j = 4 * p + m
                        for k in range(KT):
                            mm = pe.matmul(psum[:, 0, j:j + 1], ring.weights(n0 + p, k, m * P, P), cond[:, k:k + 1],
                                           start=k == 0, stop=k == KT - 1)
                    mm.then_inc(panel_done, 1)
                    ring.freed[n0 + p] = (panel_done, p + 1)

            @block.sync
            def _(sp):
                g.clear_past(sp)
                ring.load_until(sp, n0 + count + SLOTS)

            @block.vector
            def _(dve):
                dve.wait_ge(panel_done, count)
                dve.tensor_tensor(mod[:, :], psum[:, 0, 0:6 * DT], g.cols[:, at:at + 6 * DT], ALU.add).then_inc(summed, 1)
                dve.wait_ge(summed, 1)
                for part in (1, 4):
                    s = mod[:, part * DT:(part + 1) * DT]
                    dve.tensor_scalar(s, s, 1.0, None, ALU.add).then_inc(plus_one, 1)


def hgrn_stage(g, h, vt, zu, ya):
    nc, ring, psum, cols, col = g.nc, g.ring, g.psum, g.cols, g.col
    n0 = FIRST["w_head"]
    NSUB = CHUNK // SUB
    with ExitStack() as own:
        sb = lambda n, shape: own.enter_context(nc.sbuf_tensor(f"hg_{n}", shape, F32))
        sem = g.stage_semaphores("hg")
        lb, one_less = sb("lb", [P, HH]), sb("one_less", [P, HH])
        forget, query, gate = sb("forget", [P, 2, S]), sb("query", [P, 2, S]), sb("gate", [P, 2, S])
        key, logf, cum16, cum64 = sb("key", [P, S]), sb("logf", [P, S]), sb("cum16", [P, S]), sb("cum64", [P, S])
        e16, e64, q16, q64 = sb("e16", [P, S]), sb("e64", [P, S]), sb("q16", [P, S]), sb("q64", [P, S])
        keys = sb("keys", [P, NSUB + 1, NCH, CHUNK])
        vh = sb("vh", [P, 2, TT, P])
        key_t, state, scores = sb("key_t", [P, TT, P]), sb("state", [P, NCH, P]), sb("scores", [P, TT, P])
        sq, std, rstd = sb("sq", [P, S]), sb("std", [P, S]), sb("rstd", [P, S])
        gemm_ready, gemm_took, lb_ready, zeroed = sem("gemm_ready"), sem("gemm_took"), sem("lb_ready"), sem("zeroed")
        f_ready, k_ready, ln_ready, cum_ready, e_ready, expo_ready, exp_ready = (sem(n) for n in (
            "f_ready", "k_ready", "ln_ready", "cum_ready", "e_ready", "expo_ready", "exp_ready"))
        q_ready, keys_ready, scored, masked, turned, key_t_ready, vh_ready = (sem(n) for n in (
            "q_ready", "keys_ready", "scored", "masked", "turned", "key_t_ready", "vh_ready"))
        u_ready, state_ready, o_ready, squared, sq_summed, std_ready, rstd_ready, normed, head_done = (sem(n) for n in (
            "u_ready", "state_ready", "o_ready", "squared", "sq_summed", "std_ready", "rstd_ready", "normed", "head_done"))
        c16 = cum16[:, :].rearrange("p (n c) -> p n c", c=CHUNK)
        c64 = cum64[:, :].rearrange("p (n c) -> p n c", c=CHUNK)
        k3 = key[:, :].rearrange("p (n c) -> p n c", c=CHUNK)
        e3 = e64[:, :].rearrange("p (n c) -> p n c", c=CHUNK)

        def column(name, i):
            return cols[:, bass.ds(COLS.at[name] + i, 1)]

        def head_of(t, i):
            return t[:, bass.ds(i, 1), :].rearrange("p a s -> p (a s)")

        def every_head(eng, first, body):
            first(0, 0)
            with eng.Fori(0, HH // 2 - 1) as i:
                for q in range(2):
                    first(i * 2 + q + 1, (q + 1) % 2)
                    body(i * 2 + q, q)
            first(HH - 1, 1)
            body(HH - 2, 0)
            body(HH - 1, 1)

        with nc.Block(no_gpsimd_drain=True) as block:

            @block.tensor
            def _(pe):
                def gemm(n, q):
                    p = n0 + q
                    turn = (n - q) * 8
                    pe.wait_ge(ring.landed[p % SLOTS], turn + 16 * (p // SLOTS + 1))
                    for m in range(4):
                        pe.wait_ge(gemm_took, n * 4 + m + 1)
                        for k in range(KT):
                            mm = pe.matmul(psum[:, m, :], ring.weights(p, k, m * P, P), tile_of(h, k),
                                           start=k == 0, stop=k == KT - 1)
                        mm.then_inc(gemm_ready, 1)

                def attend(n, q):
                    pe.wait_ge(head_done, n + 2)
                    pe.wait_ge(q_ready, n * 2 + 1)
                    for i in range(NSUB):
                        pe.wait_ge(keys_ready, n * 5 + i + 1)
                        for c in range(NCH):
                            half = 64 * (c % 2)
                            at = (c // 2) * CHUNK + i * SUB
                            mm = pe.matmul(psum[half:half + 64, 4, at:at + SUB], keys[:, i, c, :],
                                           q16[:, c * CHUNK + i * SUB:c * CHUNK + (i + 1) * SUB], start=True, stop=True)
                    mm.then_inc(scored, 1)
                    pe.wait_ge(keys_ready, n * 5 + 5)
                    for t in range(TT):
                        mm = pe.transpose(psum[:, 5, t * P:(t + 1) * P],
                                          keys[:, NSUB, 2 * t:2 * t + 2, :].rearrange("p n c -> p (n c)"), g.ident)
                    mm.then_inc(turned, 1)
                    pe.wait_ge(key_t_ready, n + 1)
                    pe.wait_ge(vh_ready, n + 1)
                    for c in range(NCH - 1):
                        half = slice(64 * (c % 2), 64 * (c % 2) + 64)
                        mm = pe.matmul(psum[:, 6 + c % 2, c // 2 * P:(c // 2 + 1) * P], key_t[half, c // 2, :],
                                       vh[half, q, c // 2, :], start=True, stop=True)
                    mm.then_inc(u_ready, 1)
                    pe.wait_ge(masked, n * 2 + 2)
                    pe.wait_ge(q_ready, n * 2 + 2)
                    for t in range(TT):
                        pe.matmul(psum[:, 5, t * P:(t + 1) * P], vh[:, q, t, :], scores[:, t, :], start=True, stop=False)
                        for c in range(max(2 * t, 1), 2 * t + 2):
                            pe.wait_ge(state_ready, n * 7 + c)
                            mm = pe.matmul(psum[:, 5, c * CHUNK:(c + 1) * CHUNK], state[:, c, :],
                                           q64[:, c * CHUNK:(c + 1) * CHUNK], start=False, stop=c == 2 * t + 1)
                    mm.then_inc(o_ready, 1)
                    pe.wait_ge(squared, n + 1)
                    pe.matmul(psum[:, 4, :], g.ones, sq[:, :], start=True, stop=True).then_inc(sq_summed, 1)

                every_head(pe, gemm, attend)
                for n in range(HH):
                    ring.freed[n0 + n] = (gemm_ready, 4 * (n + 1))

            @block.sync
            def _(sp):
                g.clear_past(sp)
                ring.load_until(sp, n0 + HH + SLOTS)

            @block.gpsimd
            def _(pool):
                pool.memset(keys[:, 0:NSUB, :, :], 0.0).then_inc(zeroed, 1)
                pool.memset(scores[:, :, :], 0.0).then_inc(zeroed, 1)

                def body(n, q):
                    pool.wait_ge(head_done, n + 1)
                    pool.tensor_copy(vh[:, q, :, :], vt[:, :, bass.ds(n * P, P)]).then_inc(vh_ready, 1)

                every_head(pool, lambda n, q: None, body)

            @block.scalar
            def _(act):
                act.sem_inc(gemm_took, 4)
                act.wait_ge(lb_ready, 1)
                act.activation(lb[:, :], lb[:, :], ACT.Sigmoid).then_inc(lb_ready, 1)

                def take(n, q):
                    act.wait_ge(head_done, n + 1)
                    for m, (to, f) in enumerate(((query[:, q, :], ACT.Silu), (forget[:, q, :], ACT.Sigmoid),
                                                 (gate[:, q, :], ACT.Silu), (head_of(zu, n), ACT.Gelu))):
                        act.wait_ge(gemm_ready, n * 4 + m + 1)
                        act.activation(to, psum[:, m, :], f).then_inc(gemm_took, 1)

                def before(n, q):
                    act.wait_ge(f_ready, n + 1)
                    act.activation(logf[:, :], forget[:, q, :], ACT.Ln).then_inc(ln_ready, 1)
                    for i, (to, of) in enumerate(((e16, cum16), (e64, cum64))):
                        act.wait_ge(cum_ready, n * 2 + i + 1)
                        act.activation(to[:, :], of[:, :], ACT.Exp).then_inc(e_ready, 1)
                    for i in range(NSUB + 1):
                        part = keys[:, i, :, 0:min(SUB * (i + 1), CHUNK)]
                        act.wait_ge(expo_ready, n * 5 + i + 1)
                        act.activation(part, part, ACT.Exp).then_inc(exp_ready, 1)

                def after(n, q):
                    act.wait_ge(turned, n + 1)
                    act.activation(key_t[:, :, :].rearrange("p t k -> p (t k)"), psum[:, 5, :], ACT.Copy).then_inc(key_t_ready, 1)
                    act.wait_ge(o_ready, n + 1)
                    act.activation(sq[:, :], psum[:, 5, :], ACT.Square).then_inc(squared, 1)
                    act.wait_ge(sq_summed, n + 1)
                    act.activation(std[:, :], psum[:, 4, :], ACT.Sqrt, scale=1.0 / P, bias=g.eps[EPS_RMS]).then_inc(std_ready, 1)

                take(0, 0)
                with act.Fori(0, HH // 2 - 1) as i:
                    for q in range(2):
                        n = i * 2 + q
                        before(n, q)
                        take(n + 1, (q + 1) % 2)
                        after(n, q)
                before(HH - 2, 0)
                take(HH - 1, 1)
                after(HH - 2, 0)
                before(HH - 1, 1)
                after(HH - 1, 1)

            @block.vector
            def _(dve):
                dve.sem_inc(head_done, 2)
                at0, at1 = COLS.at["lb0"], COLS.at["lb1"]
                dve.tensor_tensor(lb[:, :], cols[:, at0:at0 + HH], cols[:, at1:at1 + HH], ALU.subtract).then_inc(lb_ready, 1)
                dve.wait_ge(lb_ready, 2)
                dve.tensor_scalar(one_less[:, :], lb[:, :], -1.0, 1.0, ALU.mult, ALU.add).then_inc(lb_ready, 1)
                dve.wait_ge(lb_ready, 3)
                dve.wait_ge(zeroed, 2)

                def body(n, q):
                    f = forget[:, q, :]
                    dve.wait_ge(gemm_took, n * 4 + 6)
                    dve.tensor_scalar(f, f, one_less[:, bass.ds(n, 1)], lb[:, bass.ds(n, 1)], ALU.mult, ALU.add)\
                        .then_inc(f_ready, 1)
                    dve.wait_ge(f_ready, n + 1)
                    dve.tensor_scalar(key[:, :], f, -1.0, 1.0, ALU.mult, ALU.add).then_inc(k_ready, 1)
                    dve.wait_ge(ln_ready, n + 1)
                    dve.tensor_tensor_scan(cum16[:, :], g.starts16, logf[:, :], 0.0, ALU.mult, ALU.add).then_inc(cum_ready, 1)
                    dve.tensor_tensor_scan(cum64[:, :], g.starts64, logf[:, :], 0.0, ALU.mult, ALU.add).then_inc(cum_ready, 1)
                    dve.wait_ge(cum_ready, n * 2 + 2)
                    dve.tensor_scalar(keys[:, 0, :, 0:SUB], c64[:, :, 0:SUB], -1.0, None, ALU.mult).then_inc(expo_ready, 1)
                    for i in range(1, NSUB + 1):
                        w = min(SUB * (i + 1), CHUNK)
                        start = c64[:, :, SUB * i - 1:SUB * i].to_broadcast([P, NCH, w])
                        dve.tensor_tensor(keys[:, i, :, 0:w], start, c64[:, :, 0:w], ALU.subtract).then_inc(expo_ready, 1)
                    for i, (to, e) in enumerate(((q16, e16), (q64, e64))):
                        dve.wait_ge(e_ready, n * 2 + i + 1)
                        dve.tensor_tensor(to[:, :], query[:, q, :], e[:, :], ALU.mult).then_inc(q_ready, 1)
                    dve.wait_ge(k_ready, n + 1)
                    for i in range(NSUB + 1):
                        w = min(SUB * (i + 1), CHUNK)
                        dve.wait_ge(exp_ready, n * 5 + i + 1)
                        part = keys[:, i, :, 0:w]
                        dve.tensor_tensor(part, part, k3[:, :, 0:w], ALU.mult).then_inc(keys_ready, 1)
                    dve.wait_ge(scored, n + 1)
                    for half in range(2):
                        part = slice(64 * half, 64 * half + 64)
                        dve.tensor_tensor(scores[part, :, 64 * half:64 * half + 64],
                                          psum[part, 4, 0:TT * CHUNK].rearrange("p (t c) -> p t c", c=CHUNK),
                                          g.chunk_upper[part], ALU.mult).then_inc(masked, 1)
                    dve.wait_ge(u_ready, n + 1)
                    for c in range(NCH - 1):
                        update = psum[:, 6 + c % 2, c // 2 * P:(c // 2 + 1) * P]
                        if c == 0:
                            dve.tensor_copy(state[:, 1, :], update).then_inc(state_ready, 1)
                        else:
                            dve.wait_ge(state_ready, n * 7 + c)
                            dve.scalar_tensor_tensor(state[:, c + 1, :], state[:, c, :], e3[:, c, CHUNK - 1:CHUNK], update,
                                                     ALU.mult, ALU.add).then_inc(state_ready, 1)
                    dve.wait_ge(std_ready, n + 1)
                    dve.reciprocal(rstd[:, :], std[:, :]).then_inc(rstd_ready, 1)
                    dve.wait_ge(rstd_ready, n + 1)
                    out = head_of(ya, n)
                    dve.scalar_tensor_tensor(out, psum[:, 5, :], col("hgrn_norm"), rstd[:, :], ALU.mult, ALU.mult)\
                        .then_inc(normed, 1)
                    dve.wait_ge(normed, n + 1)
                    dve.tensor_tensor(out, out, gate[:, q, :], ALU.mult).then_inc(head_done, 1)

                every_head(dve, lambda n, q: None, body)


def gmlp_stage(g, gv, zu):
    nc, ring, psum, col = g.nc, g.ring, g.psum, g.col
    with ExitStack() as own:
        sb = lambda n, shape: own.enter_context(nc.sbuf_tensor(f"gm_{n}", shape, F32))
        sem = g.stage_semaphores("gm")
        rows = sb("rows", [P, 3, D])
        ws = sb("ws", [P, HH, P])
        stats, mv, std, rstd = sb("stats", [P, TT, 2, 6]), sb("mv", [P, TT, 2]), sb("std", [P, TT]), sb("rstd", [P, TT])
        sv = sb("sv", [P, 2, S])
        rows_in, ws_in, stated, aggregated, std_ready, rstd_ready, step, ws_ready = (sem(n) for n in (
            "rows_in", "ws_in", "stated", "aggregated", "std_ready", "rstd_ready", "step", "ws_ready"))
        mixed, biased, gated = sem("mixed"), sem("biased"), sem("gated")
        with nc.Block(no_gpsimd_drain=True) as block:

            @block.sync
            def _(sp):
                g.clear_past(sp)
                sp.dma_start(rows[:, :, :], g.extra["gmlp_rows"].partition_broadcast(P)).then_inc(rows_in, 16)
                sp.dma_start(ws[:, :, :], g.extra["gmlp_ws"]).then_inc(ws_in, 16)
                ring.load_until(sp, FIRST["w_mix_b"] + SLOTS)

            @block.gpsimd
            def _(pool):
                pool.wait_ge(ws_in, 16)
                pool.memset(ws[64:128, :, 0:64], 0.0).then_inc(ws_ready, 1)

            @block.scalar
            def _(act):
                act.wait_ge(aggregated, TT)
                act.activation(std[:, :], mv[:, :, 1:2].rearrange("p t a -> p (t a)"), ACT.Sqrt, bias=g.eps[EPS_LN])\
                    .then_inc(std_ready, 1)

            @block.tensor
            def _(pe):
                pe.wait_ge(ws_ready, 1)
                pe.wait_ge(step, 3 * TT)
                for n in range(HH):
                    for t in range(TT):
                        mm = pe.matmul(psum[:, n, t * P:(t + 1) * P], gv[:, t, n * P:(n + 1) * P], ws[:, n, :],
                                       start=True, stop=True)
                    mm.then_inc(mixed, 1)

            @block.vector
            def _(dve):
                for t in range(TT):
                    for c in range(2):
                        dve.bn_stats(stats[:, t, c, :], gv[:, t, c * 512:(c + 1) * 512]).then_inc(stated, 1)
                for t in range(TT):
                    dve.wait_ge(stated, 2 * t + 2)
                    dve.bn_aggr(mv[:, t, :], stats[:, t, :, :].rearrange("p c s -> p (c s)")).then_inc(aggregated, 1)
                dve.wait_ge(std_ready, 1)
                dve.reciprocal(rstd[:, :], std[:, :]).then_inc(rstd_ready, 1)
                dve.wait_ge(rstd_ready, 1)
                dve.wait_ge(aggregated, TT)
                dve.wait_ge(rows_in, 16)
                for t in range(TT):
                    v = gv[:, t, :]
                    dve.tensor_scalar(v, v, mv[:, t, 0:1], rstd[:, t:t + 1], ALU.subtract, ALU.mult).then_inc(step, 1)
                for k, op in ((0, ALU.mult), (1, ALU.add)):
                    for t in range(TT):
                        v = gv[:, t, :]
                        dve.wait_ge(step, TT * (k + 1) - TT + t + 1)
                        dve.tensor_tensor(v, v, rows[:, k, :], op).then_inc(step, 1)
                for n in range(HH):
                    dve.wait_ge(mixed, n + 1)
                    if n >= 2:
                        dve.wait_ge(gated, n - 1)
                    dve.tensor_tensor(sv[:, n % 2, :].rearrange("p (b t) -> p b t", t=P),
                                      psum[:, n, :].rearrange("p (b t) -> p b t", t=P),
                                      rows[:, 2:3, n * P:(n + 1) * P].to_broadcast([P, TT, P]), ALU.add).then_inc(biased, 1)
                    dve.wait_ge(biased, n + 1)
                    dve.tensor_tensor(zu[:, n, :], zu[:, n, :], sv[:, n % 2, :], ALU.mult).then_inc(gated, 1)


def mix_stage(g, name, panels_at, y, u, out, bias, add):
    nc, ring, psum, col = g.nc, g.ring, g.psum, g.col
    with ExitStack() as own:
        sem = g.stage_semaphores(name)
        gate = own.enter_context(nc.sbuf_tensor(f"{name}_gate", [P, 4, S], F32))
        tile_ready, gate_ready, gated, done = sem("tile_ready"), sem("gate_ready"), sem("gated"), sem("done")
        n0 = FIRST[panels_at]
        with nc.Block(no_gpsimd_drain=True) as block:

            @block.tensor
            def _(pe):
                for p in range(4):
                    ring.wait_landed(pe, n0 + p)
                    for m in range(4):
                        if p >= 2:
                            pe.wait_ge(done, 4 * (p // 2 - 1) + m + 1)
                        for k in range(KT):
                            mm = pe.matmul(psum[:, 4 * (p % 2) + m, :], ring.weights(n0 + p, k, m * P, P),
                                           tile_of(u if p % 2 else y, k), start=k == 0, stop=k == KT - 1)
                        mm.then_inc(tile_ready, 1)
                    ring.freed[n0 + p] = (tile_ready, 4 * (p + 1))

            @block.sync
            def _(sp):
                g.clear_past(sp)
                ring.load_until(sp, n0 + 4 + SLOTS)

            @block.scalar
            def _(act):
                for t in range(DT):
                    act.wait_ge(tile_ready, 8 * (t // 4) + 4 + t % 4 + 1)
                    if t >= 4:
                        act.wait_ge(done, t - 3)
                    act.activation(gate[:, t % 4, :], psum[:, 4 + t % 4, :], ACT.Sigmoid, bias=bias(t)).then_inc(gate_ready, 1)

            @block.vector
            def _(dve):
                for t in range(DT):
                    dve.wait_ge(gate_ready, t + 1)
                    gt, y_bank = gate[:, t % 4, :], psum[:, t % 4, :]
                    if not add:
                        dve.tensor_tensor(out[:, t, :], gt, y_bank, ALU.mult).then_inc(done, 1)
                    else:
                        dve.tensor_tensor(gt, gt, y_bank, ALU.mult).then_inc(gated, 1)
                        dve.wait_ge(gated, t + 1)
                        dve.tensor_tensor(out[:, t, :], out[:, t, :], gt, ALU.add).then_inc(done, 1)


def scale_stage(g, name, x, by):
    nc = g.nc
    done = g.stage_semaphores(name)("done")
    with nc.Block(no_gpsimd_drain=True) as block:
        @block.sync
        def _(sp):
            g.clear_past(sp)

        @block.vector
        def _(dve):
            for t in range(0, DT, 2):
                dve.tensor_scalar(x[:, t:t + 2, :], x[:, t:t + 2, :], by, None, ALU.mult).then_inc(done, 1)


def block_2(g, x, h):
    nc, ring, psum, col = g.nc, g.ring, g.psum, g.col
    with ExitStack() as own:
        mod = own.enter_context(nc.sbuf_tensor("mod", [P, 6 * DT], F32))
        m = lambda part, t: mod[:, part * DT + t:part * DT + t + 1]
        gated = lambda part: lambda t: (lambda e, bank: e.scalar_tensor_tensor(
            x[:, t, :], bank, m(part, t), x[:, t, :], ALU.mult, ALU.add))
        ada_stage(g, mod)
        norm_stage(g, "n4", x, h, lambda t: m(1, t), EPS_LN, g.ones_mean, bias=lambda t: m(0, t), centre=True)
        with nc.sbuf_tensor("zu", [P, DT, S], F32) as zu:
            token_tiles = lambda name, to, func: [
                Tile([FIRST[name] + c], 0, PANEL, h, None, "act",
                     (lambda out: lambda a, bank: a.activation(out, bank, func))(to[:, t, c * PANEL:(c + 1) * PANEL]),
                     tokens=t) for c in range(2) for t in range(TT)]
            with nc.sbuf_tensor("ya", [P, DT, S], F32) as ya:
                with nc.sbuf_tensor("vt", [P, TT, D], F32) as vt:
                    dense_stage(g, "zi", token_tiles("w_zi", vt, ACT.Copy), FIRST["w_head"] + SLOTS)
                    hgrn_stage(g, h, vt, zu, ya)
                with nc.sbuf_tensor("merged", [P, DT, S], F32) as merged:
                    mix_stage(g, "mixa", "w_mix_a", ya, h, merged, lambda t: col("b_gate", t), False)
                    with nc.sbuf_tensor("gv", [P, TT, D], F32) as gv:
                        dense_stage(g, "zv", token_tiles("w_zv", gv, ACT.Gelu), FIRST["w_mix_b"] + SLOTS)
                        gmlp_stage(g, gv, zu)
                    mix_stage(g, "mixb", "w_mix_b", zu, h, merged, lambda t: col("b_gate", DT + t), True)
                    scale_stage(g, "alpha1", x, ALPHA)
                    n0 = FIRST["w_out_2"]
                    dense_stage(g, "out2", [Tile([n0 + t // 4], t % 4 * P, P, merged, None, "dve", gated(2)(t))
                                            for t in range(DT)], n0 + 2 + SLOTS)
        norm_stage(g, "n5", x, x, lambda t: col("ln1_w2", t), EPS_LN, g.ones_mean, bias=lambda t: col("ln1_b2", t), centre=True)
        norm_stage(g, "n6", x, h, lambda t: m(4, t), EPS_LN, g.ones_mean, bias=lambda t: m(3, t), centre=True)
        scale_stage(g, "alpha2", x, ALPHA)
        with nc.sbuf_tensor("mid2", [P, FT, S], F32) as mid:
            feed_forward(g, "ff2", x, h, mid, 0, "w_ffn_in", "w_ffn_out", gated(5), False)
        norm_stage(g, "n7", x, x, lambda t: col("ln2_w2", t), EPS_LN, g.ones_mean, bias=lambda t: col("ln2_b2", t), centre=True)


def mixer_stage(g, x, mixed):
    nc, ring, psum, cols, col = g.nc, g.ring, g.psum, g.cols, g.col
    PAD = max(WINDOWS)
    n0 = FIRST["w_in_3"]
    with ExitStack() as own:
        sb = lambda n, shape: own.enter_context(nc.sbuf_tensor(f"mx_{n}", shape, F32))
        sem = g.stage_semaphores("mx")
        factor, u, diff = sb("factor", [P, 2, S]), sb("u", [P, S]), sb("diff", [P, 2, S])
        values, sums = sb("values", [P, 2, PAD + S]), sb("sums", [P, 2, PAD + S])
        pool_mix = sb("pool_mix", [P, 4, P])
        tile_ready, copied, conv_done, diff_ready, pooled, scaled, step, mix_in = (sem(n) for n in (
            "tile_ready", "copied", "conv_done", "diff_ready", "pooled", "scaled", "step", "mix_in"))
        with nc.Block(no_gpsimd_drain=True) as block:

            @block.tensor
            def _(pe):
                def pool(j):
                    pe.wait_ge(diff_ready, j + 1)
                    pe.matmul(psum[:, 4 * (j % 2) + 3, :], pool_mix[:, j, :], diff[:, j % 2, :], start=True, stop=True)\
                        .then_inc(pooled, 1)

                pe.wait_ge(mix_in, 16)
                for j in range(4):
                    if j >= 2:
                        pe.wait_ge(conv_done, j - 1)
                        pe.wait_ge(scaled, j - 1)
                    ring.wait_landed(pe, n0 + j)
                    for m in range(4):
                        for k in range(KT):
                            mm = pe.matmul(psum[:, 4 * (j % 2) + m, :], ring.weights(n0 + j, k, m * P, P), tile_of(x, k),
                                           start=k == 0, stop=k == KT - 1)
                        mm.then_inc(tile_ready, 1)
                    ring.freed[n0 + j] = (tile_ready, 4 * (j + 1))
                    if j >= 1:
                        pool(j - 1)
                pool(3)

            @block.sync
            def _(sp):
                g.clear_past(sp)
                sp.dma_start(pool_mix[:, :, :], g.extra["pool_mix"]).then_inc(mix_in, 16)
                ring.load_until(sp, min(n0 + 4 + SLOTS, FIRST["ple_proj"]))

            @block.scalar
            def _(act):
                for j in range(4):
                    act.wait_ge(tile_ready, 4 * j + 2)
                    if j >= 2:
                        act.wait_ge(conv_done, j - 1)
                        act.wait_ge(diff_ready, j - 1)
                    act.activation(factor[:, j % 2, :], psum[:, 4 * (j % 2) + 1, :], ACT.Copy).then_inc(copied, 1)
                    act.wait_ge(tile_ready, 4 * j + 4)
                    act.activation(values[:, j % 2, PAD:], psum[:, 4 * (j % 2) + 3, :], ACT.Copy).then_inc(copied, 1)
                    if j >= 1:
                        act.wait_ge(pooled, j)
                        act.activation(mixed[:, j - 1, :], psum[:, 4 * ((j - 1) % 2) + 3, :], ACT.Copy,
                                       scale=col("pool_scale", j - 1)).then_inc(scaled, 1)
                act.wait_ge(pooled, 4)
                act.activation(mixed[:, 3, :], psum[:, 7, :], ACT.Copy, scale=col("pool_scale", 3)).then_inc(scaled, 1)

            @block.vector
            def _(dve):
                steps = [0]

                def link(ins):
                    steps[0] += 1
                    ins.then_inc(step, 1)
                    dve.wait_ge(step, steps[0])

                link(dve.memset(values[:, :, 0:PAD], 0.0))
                link(dve.memset(sums[:, :, 0:PAD], 0.0))
                for j in range(4):
                    bank = lambda m: psum[:, 4 * (j % 2) + m, :]
                    out = mixed[:, 4 + j, :]
                    tap = lambda k: col("conv_w3", 4 * k + j)
                    dve.wait_ge(copied, 2 * j + 1)
                    dve.wait_ge(tile_ready, 4 * j + 3)
                    link(dve.tensor_tensor(u[:, :], factor[:, j % 2, :], bank(2), ALU.mult))
                    link(dve.tensor_scalar(out, u[:, :], tap(2), None, ALU.mult))
                    for k in (1, 0):
                        back = 2 - k
                        link(dve.scalar_tensor_tensor(out[:, back:], u[:, 0:S - back], tap(k), out[:, back:],
                                                      ALU.mult, ALU.add))
                    dve.tensor_tensor(out, out, bank(0), ALU.mult).then_inc(conv_done, 1)
                    dve.wait_ge(copied, 2 * j + 2)
                    of, width, b = values[:, j % 2, :], 1, 0
                    while width < WINDOWS[j]:
                        to = sums[:, b, :]
                        link(dve.tensor_tensor(to[:, PAD:], of[:, PAD:], of[:, PAD - width:PAD + S - width], ALU.add))
                        of, width, b = to, 2 * width, 1 - b
                    d, v = diff[:, j % 2, :], values[:, j % 2, PAD:]
                    if j >= 2:
                        dve.wait_ge(pooled, j - 1)
                    at = CONST.at["pool_inv"] + 16 * j
                    link(dve.tensor_tensor(d[:, 0:16], of[:, PAD:PAD + 16], g.const("pool_inv", 64)[:, 16 * j:16 * j + 16], ALU.mult))
                    link(dve.tensor_tensor(d[:, 0:16], d[:, 0:16], v[:, 0:16], ALU.subtract))
                    dve.scalar_tensor_tensor(d[:, 16:], of[:, PAD + 16:], 1.0 / WINDOWS[j], v[:, 16:],
                                             ALU.mult, ALU.subtract).then_inc(diff_ready, 1)


def route_stage(g, x, r):
    nc, ring, psum, cols = g.nc, g.ring, g.psum, g.cols
    with ExitStack() as own:
        sb = lambda n, shape, dt=F32: own.enter_context(nc.sbuf_tensor(f"rt_{n}", shape, dt))
        sem = g.stage_semaphores("rt")
        x_tok = sb("x_tok", [P, TT, D])
        rw, rb = sb("rw", [P, DT, NE]), sb("rb", [P, NE])
        logits, left = sb("logits", [P, TT, NE + 4]), sb("left", [P, TT, NE + 4])
        best, take = sb("best", [P, TT, 8]), sb("take", [P, TT, 8])
        neg_top, chosen, e_sel, total, inv = (sb("neg_top", [P, TT]), sb("chosen", [P, TT, NE]), sb("e_sel", [P, TT, NE]),
                                              sb("total", [P, TT]), sb("inv", [P, TT]))
        rank, over, row, dest, addr = (sb(n, [P, TT, NE]) for n in ("rank", "over", "row", "dest", "addr"))
        count, blocks, upto, first, part, ones_e = (sb(n, [P, NE]) for n in ("count", "blocks", "upto", "first", "part", "ones_e"))
        top_dest, top_addr = sb("top_dest", [P, TT, 8]), sb("top_addr", [P, TT, 8])
        hit = sb("hit", [P, TT, NE])
        token = sb("token", [P, TT], I32)
        addr_i = sb("addr_i", [P, TT, TOPE], U32)
        seen, block_of = sb("seen", [1, TABLE, NE]), sb("block_of", [1, TABLE])
        zero = sb("zero", [P, TABLE], I32)
        in_done, turned, turned_out, x_stored, logit_ready, exp_ready, ranked, zeroed, table_zero, id_ready = (sem(n) for n in (
            "in_done", "turned", "turned_out", "x_stored", "logit_ready", "exp_ready", "ranked", "zeroed", "table_zero", "id_ready"))
        step, gates_ready, addr_ready, scattered, table_in, chosen_ready, top_ready, counts_ready = (sem(n) for n in (
            "step", "gates_ready", "addr_ready", "scattered", "table_in", "chosen_ready", "top_ready", "counts_ready"))
        with nc.Block(no_gpsimd_drain=True) as block:

            @block.sync
            def _(sp):
                g.clear_past(sp)
                sp.dma_start(rw[:, :, :], g.extra["router_w"]).then_inc(in_done, 16)
                sp.dma_start(rb[:, :], g.extra["router_b"][0:1, :].partition_broadcast(P)).then_inc(in_done, 16)
                sp.wait_ge(zeroed, 1)
                sp.dma_start(r.table_dram.rearrange("(s b) a -> s (b a)", s=P), zero[:, :]).then_inc(table_zero, 16)
                sp.wait_ge(turned_out, 8)
                sp.dma_start(r.x_dram.rearrange("(t p) d -> p t d", p=P), x_tok[:, :, :]).then_inc(x_stored, 16)
                sp.wait_ge(x_stored, 16)
                sp.wait_ge(scattered, 16 * TT * TOPE)
                sp.dma_start(r.table[:, :], r.table_dram.rearrange("(s b) a -> s (b a)", s=P)).then_inc(table_in, 16)
                sp.wait_ge(table_in, 16)

            @block.tensor
            def _(pe):
                for t in range(TT):
                    for c in range(2):
                        n = 2 * t + c
                        if n >= 6:
                            pe.wait_ge(turned_out, n - 5)
                        for k in range(4):
                            mm = pe.transpose(psum[:, n % 6, k * P:(k + 1) * P], x[:, 4 * c + k, t * P:(t + 1) * P], g.ident)
                        mm.then_inc(turned, 1)
                pe.wait_ge(in_done, 32)
                for t in range(TT):
                    for k in range(DT):
                        mm = pe.matmul(psum[:, 6, t * NE:(t + 1) * NE], x[:, k, t * P:(t + 1) * P], rw[:, k, :],
                                       start=k == 0, stop=k == DT - 1)
                mm.then_inc(logit_ready, 1)
                pe.wait_ge(chosen_ready, TT)
                for t in range(TT):
                    for b in range(t):
                        pe.matmul(psum[:, 7, t * NE:(t + 1) * NE], g.ones, chosen[:, b, :], start=b == 0, stop=False)
                    pe.matmul(psum[:, 7, t * NE:(t + 1) * NE], g.before, chosen[:, t, :], start=t == 0, stop=True)
                for t in range(TT):
                    mm = pe.matmul(psum[:, 7, TT * NE:(TT + 1) * NE], g.ones, chosen[:, t, :], start=t == 0, stop=t == TT - 1)
                mm.then_inc(ranked, 1)

            @block.gpsimd
            def _(pool):
                pool.memset(zero[:, :], 0).then_inc(zeroed, 1)
                pool.iota(token[:, :], pattern=[[P, TT]], base=0, channel_multiplier=1).then_inc(id_ready, 1)
                pool.wait_ge(id_ready, 1)
                pool.wait_ge(table_zero, 16)
                pool.wait_ge(addr_ready, 1)
                for t in range(TT):
                    for j in range(TOPE):
                        pool.indirect_dma_start(r.table_dram, bass.IndirectOffsetOnAxis(addr_i[:, t, j:j + 1], 0),
                                                token[:, t:t + 1], None).then_inc(scattered, 16)

            @block.scalar
            def _(act):
                for n in range(2 * TT):
                    t, c = divmod(n, 2)
                    act.wait_ge(turned, n + 1)
                    act.activation(x_tok[:, t, c * 512:(c + 1) * 512], psum[:, n % 6, :], ACT.Copy).then_inc(turned_out, 1)
                for t in range(TT):
                    act.wait_ge(top_ready, TT + 1)
                    act.activation(e_sel[:, t, :], logits[:, t, 0:NE], ACT.Exp, bias=neg_top[:, t:t + 1]).then_inc(exp_ready, 1)

            @block.vector
            def _(dve):
                steps = [0]

                def link(ins):
                    steps[0] += 1
                    ins.then_inc(step, 1)
                    dve.wait_ge(step, steps[0])

                link(dve.memset(logits[:, :, NE:], ACAUSAL))
                link(dve.memset(take[:, :, :], ACAUSAL))
                link(dve.memset(ones_e[:, :], 1.0))
                dve.wait_ge(in_done, 32)
                dve.wait_ge(logit_ready, 1)
                link(dve.tensor_tensor(logits[:, :, 0:NE], psum[:, 6, 0:TT * NE].rearrange("p (t e) -> p t e", e=NE),
                                       rb[:, :].rearrange("p (a e) -> p a e", a=1).to_broadcast([P, TT, NE]), ALU.add))
                for t in range(TT):
                    dve.max(best[:, t, :], logits[:, t, 0:NE]).then_inc(top_ready, 1)
                dve.wait_ge(top_ready, TT)
                dve.tensor_scalar(neg_top[:, :], best[:, :, 0:1].rearrange("p t a -> p (t a)"), -1.0, None, ALU.mult)\
                    .then_inc(top_ready, 1)
                link(dve.tensor_copy(take[:, :, 0:TOPE], best[:, :, 0:TOPE]))
                for t in range(TT):
                    link(dve.match_replace(left[:, t, :], take[:, t, :], logits[:, t, :], TAKEN))
                    dve.tensor_scalar(chosen[:, t, :], left[:, t, 0:NE], TAKEN, None, ALU.is_equal).then_inc(chosen_ready, 1)
                dve.wait_ge(chosen_ready, TT)
                dve.wait_ge(exp_ready, TT)
                link(dve.tensor_tensor(e_sel[:, :, :], e_sel[:, :, :], chosen[:, :, :], ALU.mult))
                link(dve.tensor_reduce(total[:, :], e_sel[:, :, :], AX_X, ALU.add))
                link(dve.reciprocal(inv[:, :], total[:, :]))
                dve.wait_ge(ranked, 1)
                link(dve.tensor_copy(rank[:, :, :], psum[:, 7, 0:TT * NE].rearrange("p (t e) -> p t e", e=NE)))
                link(dve.tensor_copy(count[:, :], psum[:, 7, TT * NE:(TT + 1) * NE]))
                link(dve.tensor_scalar(over[:, :, :], rank[:, :, :], float(ROWS), None, ALU.is_ge))
                link(dve.tensor_scalar(blocks[:, :], count[:, :], 0.0, None, ALU.is_gt))
                for n in range(1, S // ROWS):
                    link(dve.scalar_tensor_tensor(blocks[:, :], count[:, :], float(n * ROWS), blocks[:, :], ALU.is_gt, ALU.add))
                    if n > 1:
                        link(dve.scalar_tensor_tensor(over[:, :, :], rank[:, :, :], float(n * ROWS), over[:, :, :],
                                                      ALU.is_ge, ALU.add))
                link(dve.scalar_tensor_tensor(row[:, :, :], over[:, :, :], -float(ROWS), rank[:, :, :], ALU.mult, ALU.add))
                link(dve.tensor_tensor_scan(upto[:, :], ones_e[:, :], blocks[:, :], 0.0, ALU.mult, ALU.add))
                link(dve.tensor_tensor(first[:, :], upto[:, :], blocks[:, :], ALU.subtract))
                link(dve.tensor_tensor(over[:, :, :], over[:, :, :],
                                       first[:, :].rearrange("p (a e) -> p a e", a=1).to_broadcast([P, TT, NE]), ALU.add))
                link(dve.scalar_tensor_tensor(dest[:, :, :], over[:, :, :], float(ROWS), row[:, :, :], ALU.mult, ALU.add))
                link(dve.scalar_tensor_tensor(addr[:, :, :], row[:, :, :], float(TABLE), over[:, :, :], ALU.mult, ALU.add))
                for v in (dest, addr):
                    link(dve.scalar_tensor_tensor(v[:, :, :], v[:, :, :], 1.0, chosen[:, :, :], ALU.add, ALU.mult))
                for t in range(TT):
                    link(dve.max(top_dest[:, t, :], dest[:, t, :]))
                    link(dve.max(top_addr[:, t, :], addr[:, t, :]))
                dve.tensor_scalar(addr_i[:, :, :], top_addr[:, :, 0:TOPE], -1.0, None, ALU.add).then_inc(addr_ready, 1)
                link(dve.tensor_scalar(r.dest[:, :, :], top_dest[:, :, 0:TOPE], -1.0, None, ALU.add))
                for t in range(TT):
                    for j in range(TOPE):
                        link(dve.scalar_tensor_tensor(hit[:, t, :], dest[:, t, :], top_dest[:, t, j:j + 1], e_sel[:, t, :],
                                                      ALU.is_equal, ALU.mult, accum_out=r.gates[:, t, j:j + 1]))
                    link(dve.tensor_scalar(r.gates[:, t, :], r.gates[:, t, :], inv[:, t:t + 1], None, ALU.mult))
                link(dve.tensor_tensor(seen[:, :, :], upto[0:1, :].rearrange("p (a e) -> p a e", a=1).to_broadcast([1, TABLE, NE]),
                                       g.block_iota.rearrange("p (b a) -> p b a", a=1).to_broadcast([1, TABLE, NE]), ALU.is_le))
                link(dve.tensor_reduce(block_of[:, :], seen[:, :, :], AX_X, ALU.add))
                link(dve.tensor_scalar(r.expert[:, :], block_of[:, :], float(NE - 1), None, ALU.min))
                link(dve.tensor_copy(r.n_blocks[:, :], upto[0:1, NE - 1:NE]))


def expert_stage(g, r):
    nc, psum = g.nc, g.psum
    with ExitStack() as own:
        sb = lambda n, shape, dt=F32: own.enter_context(nc.sbuf_tensor(f"ex_{n}", shape, dt))
        sem = g.stage_semaphores("ex")
        more = sb("more", [P, 4, KT * PANEL])
        piece = lambda s: g.ring.tile[:, s, :] if s < SLOTS else more[:, s - SLOTS, :]
        weights = lambda s, k: piece(s)[:, k * PANEL:(k + 1) * PANEL]
        rows, rows_t = sb("rows", [P, D]), sb("rows_t", [P, DT, P])
        bias_row, bias_up, bias_down = sb("bias_row", [1, 3 * D]), sb("bias_up", [P, 2 * D]), sb("bias_down", [P, D])
        gate, up, sig = sb("gate", [P, 512]), sb("up", [P, 512]), sb("sig", [P, 512])
        act_rows, act_t, y = sb("act_rows", [P, 2, 512]), sb("act_t", [P, DT, P]), sb("y", [P, D])
        index = sb("index", [P, 1], U32)
        landed = [sem(f"landed{s}") for s in range(6)]
        gu_ready, dn_ready, rows_in, index_ready, x_turned, x_ready, bias_in, up_spread, down_spread = (sem(n) for n in (
            "gu_ready", "dn_ready", "rows_in", "index_ready", "x_turned", "x_ready", "bias_in", "up_spread", "down_spread"))
        taken, limited, sig_ready, product, h_done, h_turned, h_ready, y_done, y_out = (sem(n) for n in (
            "taken", "limited", "sig_ready", "product", "h_done", "h_turned", "h_ready", "y_done", "y_out"))

        blank, blank_out = sem("blank"), sem("blank_out")
        passed = sem("passed")
        def blocks_of(eng):
            return eng.value_load(r.n_blocks[0:1, 0:1], min_val=1, max_val=NBLK)

        with nc.Block(no_gpsimd_drain=True) as block:

            @block.sync
            def _(sp):
                g.clear_past(sp)
                with sp.Fori(0, blocks_of(sp)) as b:
                    e = sp.value_load(r.expert[0:1, bass.ds(b, 1)], min_val=0, max_val=NE - 1)
                    sp.wait_ge(down_spread, b + 1)
                    sp.dma_start(bias_row[:, :], g.extra["moe_b"][bass.ds(e, 1), :]).then_inc(bias_in, 16)
                    for s in range(6):
                        if s < 4:
                            sp.wait_ge(gu_ready, b * 4 + s + 1)
                        else:
                            sp.wait_ge(dn_ready, b * 2 + s - 3)
                        sp.dma_start(piece(s), g.extra["moe_w"][bass.ds(e * 6 + s, 1), :, :].rearrange("a p f -> (a p) f"))\
                            .then_inc(landed[s], 16)

            @block.gpsimd
            def _(pool):
                pool.sem_inc(down_spread, 1)
                pool.memset(r.scratch, 0.0).then_inc(blank, 1)

                def gather(b):
                    pool.tensor_copy(index[:, :], r.table[:, bass.ds(b, 1)]).then_inc(index_ready, 1)
                    pool.wait_ge(index_ready, b + 1)
                    pool.sem_inc(passed, 1)
                    pool.indirect_dma_start(rows[:, :], None, r.x_dram, bass.IndirectOffsetOnAxis(index[:, 0:1], 0))\
                        .then_inc(rows_in, 16)

                gather(0)
                with pool.Fori(0, blocks_of(pool)) as b:
                    pool.wait_ge(bias_in, b * 16 + 16)
                    pool.wait_ge(h_done, b * 2 + 2)
                    pool.sem_inc(passed, 1)
                    pool.partition_broadcast(bias_up[:, :], bias_row[:, 0:2 * D]).then_inc(up_spread, 1)
                    pool.wait_ge(y_done, b * 2 + 2)
                    pool.sem_inc(passed, 1)
                    pool.partition_broadcast(bias_down[:, :], bias_row[:, 2 * D:]).then_inc(down_spread, 1)
                    pool.wait_ge(rows_in, b * 16 + 16)
                    pool.wait_ge(x_turned, b * 2 + 2)
                    gather(b + 1)

            @block.tensor
            def _(pe):
                pe.sem_inc(gu_ready, 4)
                pe.sem_inc(dn_ready, 2)

                def turn_rows(c):
                    for k in range(4):
                        mm = pe.transpose(psum[:, 5, k * P:(k + 1) * P], rows[:, (4 * c + k) * P:(4 * c + k + 1) * P], g.ident)
                    mm.then_inc(x_turned, 1)

                def turn_act(c):
                    for k in range(4):
                        mm = pe.transpose(psum[:, 4, k * P:(k + 1) * P], act_rows[:, c, k * P:(k + 1) * P], g.ident)
                    mm.then_inc(h_turned, 1)

                pe.wait_ge(rows_in, 16)
                turn_rows(0)
                pe.wait_ge(x_ready, 1)
                turn_rows(1)
                with pe.Fori(0, blocks_of(pe)) as b:
                    pe.wait_ge(x_ready, b * 2 + 2)
                    for s in range(4):
                        pe.wait_ge(landed[s], b * 16 + 16)
                        pe.wait_ge(taken, b * 4 + s + 1)
                        for k in range(KT):
                            mm = pe.matmul(psum[:, s, :], rows_t[:, k, :], weights(s, k), start=k == 0, stop=k == KT - 1)
                        mm.then_inc(gu_ready, 1)
                    pe.wait_ge(h_done, b * 2 + 3)
                    turn_act(0)
                    pe.wait_ge(rows_in, b * 16 + 32)
                    turn_rows(0)
                    pe.wait_ge(y_done, b * 2 + 2)
                    for c in range(2):
                        pe.wait_ge(h_ready, b * 2 + c + 1)
                        if c:
                            pe.wait_ge(x_ready, b * 2 + 3)
                            turn_rows(1)
                        for s in range(2):
                            if c == 0:
                                pe.wait_ge(landed[4 + s], b * 16 + 16)
                            for k in range(4 * c, 4 * c + 4):
                                mm = pe.matmul(psum[:, 6 + s, :], act_t[:, k, :], weights(4 + s, k),
                                               start=k == 0, stop=k == KT - 1)
                            if c:
                                mm.then_inc(dn_ready, 1)
                        if c == 0:
                            pe.wait_ge(h_done, b * 2 + 4)
                            turn_act(1)

            @block.scalar
            def _(act):
                act.sem_inc(y_out, 16)
                n_blocks = blocks_of(act)
                act.wait_ge(blank, 1)
                with act.Fori(n_blocks, TABLE) as b:
                    act.dma_start(r.y_dram[bass.ds(b * ROWS, ROWS), :], r.scratch).then_inc(blank_out, 16)

                def take_rows(c):
                    act.activation(rows_t[:, 4 * c:4 * c + 4, :].rearrange("p k s -> p (k s)"), psum[:, 5, :], ACT.Copy)\
                        .then_inc(x_ready, 1)

                def take_act(c):
                    act.activation(act_t[:, 4 * c:4 * c + 4, :].rearrange("p k s -> p (k s)"), psum[:, 4, :], ACT.Copy)\
                        .then_inc(h_ready, 1)

                for c in range(2):
                    act.wait_ge(x_turned, c + 1)
                    take_rows(c)
                with act.Fori(0, n_blocks) as b:
                    act.sem_inc(blank_out, 16)
                    for c in range(2):
                        act.wait_ge(limited, b * 2 + c + 1)
                        act.wait_ge(h_done, b * 2 + c + 2)
                        act.activation(sig[:, :], gate[:, :], ACT.Sigmoid, scale=SW_ALPHA).then_inc(sig_ready, 1)
                    act.wait_ge(h_turned, b * 2 + 1)
                    take_act(0)
                    act.wait_ge(x_turned, b * 2 + 3)
                    take_rows(0)
                    act.wait_ge(h_turned, b * 2 + 2)
                    take_act(1)
                    act.wait_ge(x_turned, b * 2 + 4)
                    take_rows(1)
                    act.wait_ge(y_done, b * 2 + 4)
                    act.dma_start(r.y_dram[bass.ds(b * ROWS, ROWS), :], y[:, :]).then_inc(y_out, 16)
                act.wait_ge(y_out, n_blocks * 16 + 16)
                act.wait_ge(blank_out, 16 * TABLE)
                act.sem_inc(passed, 1)

            @block.vector
            def _(dve):
                dve.sem_inc(taken, 4)
                dve.sem_inc(h_done, 2)
                dve.sem_inc(y_done, 2)
                with dve.Fori(0, blocks_of(dve)) as b:
                    dve.wait_ge(up_spread, b + 1)
                    for c in range(2):
                        part = slice(512 * c, 512 * c + 512)
                        for m, to in ((2 * c, gate), (2 * c + 1, up)):
                            dve.wait_ge(gu_ready, b * 4 + m + 5)
                            at = D * (m % 2) + 512 * c
                            dve.tensor_tensor(to[:, :], psum[:, m, :], bias_up[:, at:at + 512], ALU.add).then_inc(taken, 1)
                            dve.wait_ge(taken, b * 4 + m + 5)
                            if m % 2 == 0:
                                dve.tensor_scalar(to[:, :], to[:, :], SW_LIMIT, None, ALU.min).then_inc(limited, 1)
                            else:
                                dve.tensor_scalar(to[:, :], to[:, :], SW_LIMIT, -SW_LIMIT, ALU.min, ALU.max)\
                                    .then_inc(product, 1)
                        dve.wait_ge(product, b * 4 + 2 * c + 1)
                        dve.wait_ge(limited, b * 2 + c + 1)
                        dve.scalar_tensor_tensor(up[:, :], up[:, :], 1.0, gate[:, :], ALU.add, ALU.mult).then_inc(product, 1)
                        dve.wait_ge(product, b * 4 + 2 * c + 2)
                        dve.wait_ge(sig_ready, b * 2 + c + 1)
                        if c == 0:
                            dve.wait_ge(x_ready, b * 2 + 2)
                        dve.tensor_tensor(act_rows[:, c, :], up[:, :], sig[:, :], ALU.mult).then_inc(h_done, 1)
                    dve.wait_ge(down_spread, b + 2)
                    dve.wait_ge(y_out, b * 16 + 16)
                    for s in range(2):
                        dve.wait_ge(dn_ready, b * 2 + s + 3)
                        part = slice(512 * s, 512 * s + 512)
                        dve.tensor_tensor(y[:, part], psum[:, 6 + s, :], bias_down[:, part], ALU.add).then_inc(y_done, 1)


def gather_stage(g, r, x, acc):
    nc, psum = g.nc, g.psum
    with ExitStack() as own:
        sem = g.stage_semaphores("ga")
        got = own.enter_context(nc.sbuf_tensor("ga_got", [P, 4, D], F32))
        arrived = [sem(f"arrived{j}") for j in range(TOPE)]
        summed, turned, added = sem("summed"), sem("turned"), sem("added")
        with nc.Block(no_gpsimd_drain=True) as block:

            @block.sync
            def _(sp):
                g.clear_past(sp)
                g.ring.load_until(sp, FIRST["ple_proj"] + SLOTS)

            @block.gpsimd
            def _(pool):
                for t in range(TT):
                    for j in range(TOPE):
                        if t:
                            pool.wait_ge(summed, TOPE * (t - 1) + j + 1)
                        pool.indirect_dma_start(got[:, j, :], None, r.y_dram, bass.IndirectOffsetOnAxis(r.dest[:, t, j:j + 1], 0))\
                            .then_inc(arrived[j], 16)

            @block.vector
            def _(dve):
                def add(t):
                    for c in range(2):
                        n = 2 * t + c
                        dve.wait_ge(turned, n + 1)
                        for k in range(1):
                            to = x[:, 4 * c:4 * c + 4, t * P:(t + 1) * P]
                            dve.scalar_tensor_tensor(to, to, ALPHA, psum[:, n % BANKS, :].rearrange("p (k q) -> p k q", q=P),
                                                     ALU.mult, ALU.add).then_inc(added, 1)

                for t in range(TT):
                    for j in range(TOPE):
                        dve.wait_ge(arrived[j], 16 * (t + 1))
                        gate = r.gates[:, t, j:j + 1]
                        if j == 0:
                            dve.tensor_scalar(acc[:, t, :], got[:, j, :], gate, None, ALU.mult).then_inc(summed, 1)
                        else:
                            dve.wait_ge(summed, TOPE * t + j)
                            dve.scalar_tensor_tensor(acc[:, t, :], got[:, j, :], gate, acc[:, t, :], ALU.mult, ALU.add)\
                                .then_inc(summed, 1)
                    if t:
                        add(t - 1)
                add(TT - 1)

            @block.tensor
            def _(pe):
                for t in range(TT):
                    pe.wait_ge(summed, TOPE * (t + 1))
                    for c in range(2):
                        n = 2 * t + c
                        for k in range(4):
                            mm = pe.transpose(psum[:, n % BANKS, k * P:(k + 1) * P],
                                              acc[:, t, (4 * c + k) * P:(4 * c + k + 1) * P], g.ident)
                        mm.then_inc(turned, 1)


def ple_stage(g, x, ple):
    nc, ring, psum, col = g.nc, g.ring, g.psum, g.col
    with ExitStack() as own:
        sem = g.stage_semaphores("pl")
        pt = own.enter_context(nc.sbuf_tensor("pl_pt", [P, PLE // P, S], F32))
        gate = own.enter_context(nc.sbuf_tensor("pl_gate", [P, 2, S], F32))
        p_in, ple_ready, tile_ready, copied, gate_ready, gated, done = (sem(n) for n in (
            "p_in", "ple_ready", "tile_ready", "copied", "gate_ready", "gated", "done"))
        n0 = FIRST["ple_proj"]
        with nc.Block(no_gpsimd_drain=True) as block:

            @block.tensor
            def _(pe):
                pe.wait_ge(p_in, 16)
                ring.wait_landed(pe, n0)
                for t in range(DT):
                    for k in range(PLE // P):
                        mm = pe.matmul(psum[:, t, :], ring.weights(n0, 2 * k + t // 4, t % 4 * P, P), pt[:, k, :],
                                       start=k == 0, stop=k == PLE // P - 1)
                    mm.then_inc(ple_ready, 1)
                ring.freed[n0] = (ple_ready, DT)
                for t in range(DT):
                    ring.wait_landed(pe, n0 + 1 + t // 4)
                    pe.wait_ge(copied, t + 1)
                    for k in range(KT):
                        mm = pe.matmul(psum[:, t, :], ring.weights(n0 + 1 + t // 4, k, t % 4 * P, P), tile_of(x, k),
                                       start=k == 0, stop=k == KT - 1)
                    mm.then_inc(tile_ready, 1)

            @block.sync
            def _(sp):
                g.clear_past(sp)
                sp.dma_start(pt[:, :, :], g.extra["pt"]).then_inc(p_in, 16)
                ring.load_until(sp, n0 + 3)

            @block.scalar
            def _(act):
                for t in range(DT):
                    act.wait_ge(ple_ready, t + 1)
                    act.activation(ple[:, t, :], psum[:, t, :], ACT.Copy).then_inc(copied, 1)
                for t in range(DT):
                    act.wait_ge(tile_ready, t + 1)
                    if t >= 2:
                        act.wait_ge(gated, t - 1)
                    act.activation(gate[:, t % 2, :], psum[:, t, :], ACT.Sigmoid, bias=col("ple_b", t)).then_inc(gate_ready, 1)

            @block.vector
            def _(dve):
                for t in range(DT):
                    dve.wait_ge(gate_ready, t + 1)
                    dve.wait_ge(copied, t + 1)
                    dve.tensor_tensor(ple[:, t, :], ple[:, t, :], gate[:, t % 2, :], ALU.mult).then_inc(gated, 1)
                dve.wait_ge(tile_ready, DT)
                dve.wait_ge(gated, DT)
                for t in range(DT):
                    dve.scalar_tensor_tensor(x[:, t, :], x[:, t, :], ALPHA, ple[:, t, :], ALU.mult, ALU.add).then_inc(done, 1)


class Routes:
    pass


def block_3(g, x, h):
    nc, col = g.nc, g.col
    norm = lambda name, w: norm_stage(g, name, x, x, lambda t: col(w + "_g3", t), EPS_LN, g.ones_mean,
                                      bias=lambda t: col(w + "_b3", t), centre=True)
    mixer_stage(g, x, h)
    scale_stage(g, "alpha3", x, ALPHA)
    n0 = FIRST["w_out_3"]
    dense_stage(g, "out3", [
        Tile([n0 + t // 4], t % 4 * P, P, h, None, "dve",
             (lambda to: lambda e, bank: e.tensor_tensor(to, bank, to, ALU.add))(x[:, t, :])) for t in range(DT)], n0 + 2)
    norm("n8", "ln1")
    r = Routes()
    r.table_dram = nc.dram_tensor("row_table", [P * TABLE, 1], I32, kind="Internal").ap()
    r.x_dram = nc.dram_tensor("x_rows", [S, D], F32, kind="Internal").ap()
    r.y_dram = nc.dram_tensor("y_rows", [TABLE * ROWS, D], F32, kind="Internal").ap()
    r.scratch = h[:, 0:2, :].rearrange("p a s -> p (a s)")
    with ExitStack() as own:
        sb = lambda n, shape, dt=F32: own.enter_context(nc.sbuf_tensor(n, shape, dt))
        r.table, r.dest, r.gates = sb("table", [P, TABLE], I32), sb("dest", [P, TT, TOPE], U32), sb("gates", [P, TT, TOPE])
        r.expert, r.n_blocks = sb("expert", [1, TABLE], I32), sb("n_blocks", [1, 1], I32)
        route_stage(g, x, r)
        expert_stage(g, r)
        g.ring.freed = {}
        gather_stage(g, r, x, h[:, :, :].rearrange("p (t c) s -> p t (c s)", c=2))
    norm("n9", "ln2")
    ple_stage(g, x, h)
    norm("n10", "ln3")


class Shared:

    def __init__(self):
        self.stages = []

    def stage_semaphores(self, name):
        if len(self.stages) == 2:
            self.stages.pop(0)[0].close()
        own, made = ExitStack(), []
        self.stages.append((own, made))

        def semaphore(n):
            made.append(own.enter_context(self.nc.semaphore(f"{name}_{n}")))
            return made[-1]

        return semaphore

    def clear_past(self, sp):
        if len(self.stages) == 2:
            for s in self.stages[0][1]:
                sp.sem_clear(s)

    def col(self, name, i=0):
        at = COLS.at[name] + i
        return self.cols[:, at:at + 1]


def build(nc, wstream, xt, params, consts, rel_bias, extra, out):
    g = Shared()
    g.nc, g.rel_bias, g.extra = nc, rel_bias, extra
    with ExitStack() as ctx:
        sb = lambda n, shape: ctx.enter_context(nc.sbuf_tensor(n, shape, F32))
        g.cols = sb("cols", [P, COLS.n])
        const = sb("const", [P, CONST.n])
        x, h = sb("x", [P, DT, S]), sb("h", [P, DT, S])
        ring = sb("ring", [P, SLOTS, KT * PANEL])
        g.psum = ctx.enter_context(nc.psum_tensor("psum", [P, BANKS, 512], F32))
        g.const = lambda name, n, rows=P: const[0:rows, CONST.at[name]:CONST.at[name] + n]
        g.ident, g.ones, g.ones_mean = g.const("ident", P), g.const("ones", P), g.const("ones_mean", P)
        g.half_ones, g.upper, g.acausal = g.const("half_ones", P), g.const("upper", P), g.const("acausal", P)
        g.causal_add = g.const("causal_add", P)
        g.starts16, g.starts64 = g.const("starts16", S), g.const("starts64", S)
        g.chunk_upper = g.const("chunk_upper", TT * CHUNK).rearrange("p (t c) -> p t c", c=CHUNK)
        g.before, g.block_iota = g.const("before", P), g.const("block_iota", TABLE, 1)
        g.neg_head = g.const("neg_head", MH * P, MH).rearrange("p (h c) -> p h c", c=P)
        g.eps = {EPS_RMS: g.const("eps_rms", 1), EPS_LN: g.const("eps_ln", 1)}
        landed = [ctx.enter_context(nc.semaphore(f"panel_landed{i}")) for i in range(SLOTS)]
        g.ring = Ring(ring, wstream, landed)
        first_in = ctx.enter_context(nc.semaphore("first_in"))
        with nc.Block(no_gpsimd_drain=True) as block:
            @block.sync
            def _(sp):
                sp.dma_start(x[:, :, :], xt).then_inc(first_in, 16)
                sp.dma_start(const[:, :], consts).then_inc(first_in, 16)
                sp.dma_start(g.cols[:, :], params).then_inc(first_in, 16)
                g.ring.load_until(sp, SLOTS)
                sp.wait_ge(first_in, 48)
        block_1(g, x, h)
        block_2(g, x, h)
        block_3(g, x, h)
        out_done = ctx.enter_context(nc.semaphore("out_done"))
        with nc.Block(no_gpsimd_drain=True) as block:
            @block.sync
            def _(sp):
                sp.dma_start(out, x[:, :, :]).then_inc(out_done, 16)
                sp.wait_ge(out_done, 16)


CONST = Columns()
for _name, _c in (("ident", P), ("ones", P), ("ones_mean", P), ("half_ones", P), ("upper", P), ("acausal", P),
                  ("causal_add", P), ("neg_head", MH * P), ("eps_rms", 1), ("eps_ln", 1),
                  ("pool_inv", 4 * 16), ("chunk_upper", TT * CHUNK), ("starts16", S), ("starts64", S),
                  ("before", P), ("block_iota", TABLE)):
    CONST.add(_name, _c)


def constants():
    c = np.zeros((P, CONST.n), np.float32)
    put = lambda name, v: c.__setitem__((slice(0, v.shape[0]), slice(CONST.at[name], CONST.at[name] + v.shape[1])), v)
    p, f = np.arange(P)[:, None], np.arange(P)[None, :]
    put("ident", np.eye(P))
    put("ones", np.ones((P, P)))
    put("ones_mean", np.full((P, P), 1.0 / D))
    put("half_ones", (p // 64 == f // 64) * 1.0)
    put("upper", (p <= f) * 1.0)
    put("acausal", np.where(f <= p, 3.4e38, ACAUSAL))
    put("causal_add", np.where(f <= p, 0.0, MASKED))
    put("neg_head", np.repeat(-np.eye(MH), P, axis=1))
    put("eps_rms", np.full((P, 1), EPS_RMS))
    put("eps_ln", np.full((P, 1), EPS_LN))
    t = np.arange(16)
    put("pool_inv", np.broadcast_to(np.concatenate([1.0 / np.minimum(t + 1, w) for w in WINDOWS])[None], (P, 64)))
    put("chunk_upper", (p % CHUNK <= np.arange(TT * CHUNK)[None] % CHUNK) * 1.0)
    s = np.arange(S)[None]
    put("starts16", np.broadcast_to(s % SUB != 0, (P, S)) * 1.0)
    put("starts64", np.broadcast_to(s % CHUNK != 0, (P, S)) * 1.0)
    put("before", (p < f) * 1.0)
    put("block_iota", np.broadcast_to(np.arange(TABLE)[None], (P, TABLE)))
    return c


def relative_bucket():
    d = np.maximum(np.arange(P)[:, None] + (S - P) - np.arange(S)[None, :], 0)
    exact = REL_BUCKETS // 2
    large = exact + (np.log(np.maximum(d, 1).astype(np.float32) / exact) / np.float32(np.log(128 / exact))
                     * (REL_BUCKETS - exact)).astype(np.int32)
    return np.where(d < exact, d, np.minimum(large, REL_BUCKETS - 1))


def panels(w, columns):
    w = w[:, columns]
    rows, width = w.shape
    w = np.pad(w, ((0, -rows % D), (0, -width % PANEL)))
    w = w.reshape(-1, KT, P, w.shape[1] // PANEL, PANEL).transpose(3, 0, 2, 1, 4)
    return w.reshape(-1, P, KT * PANEL)


def by_turns(a, b):
    return np.stack([a, b], axis=1).reshape(-1, P, KT * PANEL)


def feature_columns(v):
    return np.asarray(v).reshape(-1, P).T


def pad_rows(v):
    return np.pad(np.asarray(v).reshape(-1, 1), ((0, P - np.size(v)), (0, 0)))


def head_panel_order():
    c = np.arange(P)
    return np.concatenate([np.concatenate([h * P + c, D + h * P + c, 3 * D + h * P + c, 4 * D + h * P + c]) for h in range(HH)])


def ffn_order():
    c = np.arange(2 * P)
    return np.concatenate([np.concatenate([n * 2 * P + c, DFF + n * 2 * P + c]) for n in range(FFN_PANELS)])


def lay_out(i):
    w = i["w_in"][0]
    z = lambda n: (np.arange(n[0], n[1]))
    q0 = 0
    offs = np.cumsum([0, 256, 256, 512, 512, 4, 4, 512, 512, 512, 512, 64, 8])
    seg = [np.arange(offs[k], offs[k + 1]) for k in range(12)]
    order = np.concatenate([seg[0], seg[1], seg[2], seg[3], seg[6], seg[7], seg[8], seg[9],
                            seg[10], seg[10], seg[4], seg[5], seg[11]])
    w2 = i["w_in_2"][0]
    al = np.arange
    c3 = np.concatenate([np.concatenate([al(512 + j * P, 512 + j * P + P), al(1024 + j * P, 1024 + j * P + P),
                                         al(1536 + j * P, 1536 + j * P + P), al(j * P, j * P + P)]) for j in range(4)])
    every = lambda a: al(a.shape[1])
    parts = {
        "w_in": panels(w, order), "w_out": panels(i["w_out"][0], every(i["w_out"][0])),
        "w_up": panels(i["w_up"][0], ffn_order()), "w_down": panels(i["w_down"][0], al(D)),
        "w_ada": panels(i["w_ada_2"][0], al(6 * D)),
        "w_zi": panels(w2, al(2 * D, 3 * D)), "w_head": panels(w2, head_panel_order()),
        "w_zv": panels(w2, al(5 * D, 6 * D)),
        "w_mix_a": by_turns(panels(i["w_proj_a_2"][0], al(D)), panels(w2, al(6 * D, 7 * D))),
        "w_mix_b": by_turns(panels(i["w_proj_b_2"][0], al(D)), panels(w2, al(7 * D, 8 * D))),
        "w_out_2": panels(i["w_out_2"][0], al(D)), "w_ffn_in": panels(i["w_ffn_in_2"][0], ffn_order()),
        "w_ffn_out": panels(i["w_ffn_out_2"][0], al(D)),
        "w_in_3": panels(i["w_in_3"][0], c3), "w_out_3": panels(i["w_out_3"][0], al(D)),
        "ple_proj": np.concatenate([i["ple_proj_3"][0].reshape(2, P, D).transpose(1, 0, 2).reshape(P, 2 * D),
                                    np.zeros((P, 2 * D), np.float32)], axis=1)[None],
        "ple_gate": panels(i["ple_gate_w_3"][0], al(D)),
    }
    for name, count in PANELS:
        assert parts[name].shape == (count, P, KT * PANEL), (name, parts[name].shape)
    wstream = np.concatenate([parts[name] for name, _ in PANELS])
    fo = ffn_order()
    taps = np.concatenate([i["ffn_conv_w"][0], i["ffn_conv_b"]])[:, fo]
    taps = taps.reshape(4, FFN_PANELS, 4, P).transpose(3, 1, 0, 2).reshape(P, -1)
    lb = i["hgrn_lb_logits_2"]
    cols = {
        "norm_mix": feature_columns(i["norm_mix"]), "conv_w": feature_columns(i["mlstm_conv_w"][0]),
        "conv_b": feature_columns(i["mlstm_conv_b"]), "i_bias": pad_rows(i["i_bias"]), "f_bias": pad_rows(i["f_bias"]),
        "mlstm_norm": feature_columns(i["mlstm_norm"]), "idx_norm": np.concatenate([i["idx_k_norm"][0]] * 2)[:, None],
        "norm_ffn": feature_columns(i["norm_ffn"]), "ffn_conv": taps, "norm_final": feature_columns(i["norm_final"]),
        "c2": feature_columns(i["c_2"]), "b_ada": feature_columns(i["b_ada_2"]), "b_gate": feature_columns(i["b_gate_2"]),
        "lb0": feature_columns(lb[0]), "lb1": feature_columns(lb[1]), "hgrn_norm": feature_columns(i["hgrn_norm_w_2"]),
        "ln1_w2": feature_columns(i["ln1_w_2"]), "ln1_b2": feature_columns(i["ln1_b_2"]),
        "ln2_w2": feature_columns(i["ln2_w_2"]), "ln2_b2": feature_columns(i["ln2_b_2"]),
        "conv_w3": feature_columns(i["conv_w_3"][0]), "pool_scale": feature_columns(i["pool_scale_3"]),
        "ln1_g3": feature_columns(i["ln1_g_3"]), "ln1_b3": feature_columns(i["ln1_b_3"]),
        "ln2_g3": feature_columns(i["ln2_g_3"]), "ln2_b3": feature_columns(i["ln2_b_3"]),
        "ple_b": feature_columns(i["ple_gate_b_3"]), "ln3_g3": feature_columns(i["ln3_g_3"]),
        "ln3_b3": feature_columns(i["ln3_b_3"]),
    }
    params = np.concatenate([cols[name] for name in COLS.at], axis=1)
    assert params.shape[1] == COLS.n
    rel = i["rel_bias"][relative_bucket()].transpose(0, 2, 1)
    tiles = lambda a: np.ascontiguousarray(a.T.reshape(-1, P, a.shape[0]).transpose(1, 0, 2))
    wgu, wdn = i["w_gate_up_3"][0], i["w_down_3"][0]
    moe_w = np.concatenate([wgu.reshape(NE, KT, P, 4, PANEL)[:, :, :, [0, 2, 1, 3]].transpose(0, 3, 2, 1, 4)
                            .reshape(NE, 4, P, KT * PANEL),
                            wdn.reshape(NE, KT, P, 2, PANEL).transpose(0, 3, 2, 1, 4).reshape(NE, 2, P, KT * PANEL)], axis=1)
    return {
        "wstream": wstream, "xt": tiles(i["x"][0]), "params": params, "consts": constants(),
        "rel_bias": np.ascontiguousarray(rel),
        "gmlp_rows": np.stack([i["gmlp_ln_w_2"][0], i["gmlp_ln_b_2"][0], i["gmlp_bs_2"][0].reshape(-1)]),
        "gmlp_ws": np.ascontiguousarray(i["gmlp_ws_2"][0].transpose(2, 0, 1)),
        "pool_mix": np.ascontiguousarray(i["pool_mix_3"][0].transpose(1, 0, 2)),
        "pt": tiles(i["p_3"][0, 0]),
        "router_w": np.ascontiguousarray(i["router_w_3"][0].reshape(DT, P, NE).transpose(1, 0, 2)),
        "router_b": np.ascontiguousarray(i["router_b_3"]),
        "moe_w": moe_w.reshape(NE * 6, P, KT * PANEL),
        "moe_b": np.concatenate([i["b_gate_up_3"][0], i["b_down_3"][0]], axis=1),
    }


def kernel(**inputs):
    import concourse.bacc as bacc
    from concourse.bass_utils import run_bass_kernel_spmd

    arrays = {k: np.ascontiguousarray(v, dtype=np.float32) for k, v in lay_out({k: np.asarray(v) for k, v in inputs.items()}).items()}
    nc = bacc.Bacc("TRN2", target_bir_lowering=False, num_devices=1)
    ap = {k: nc.dram_tensor(k, v.shape, F32, kind="ExternalInput").ap() for k, v in arrays.items()}
    out = nc.dram_tensor("out", [P, DT, S], F32, kind="ExternalOutput").ap()
    build(nc, ap["wstream"], ap["xt"], ap["params"], ap["consts"], ap["rel_bias"], ap, out)
    r = run_bass_kernel_spmd(nc, [arrays], core_ids=[0])
    return r.results[0]["out"].transpose(2, 1, 0).reshape(1, S, D)
```

```python
from contextlib import ExitStack

import numpy as np

import concourse.bass as bass
from concourse import mybir

F32 = mybir.dt.float32
I32 = mybir.dt.int32
U32 = mybir.dt.uint32
F32R = mybir.dt.float32r
ALU = mybir.AluOpType
ACT = mybir.ActivationFunctionType
AX_X = mybir.AxisListType.X

P = 128
S = 512
D = 1024
DT = D // P
TT = S // P
PANEL = 512
KT = 8
SLOTS = 2
BANKS = 8
PARTS = 4

MH, M_DQK, M_DV, M_CONV = 4, 64, 128, 4
AH, ADH, IH, IDIM = 8, 64, 8, 64
TOPK = min(256, S // 4)
REL_BUCKETS = 32
DFF = 2816
FT = DFF // P
FFN_CONV = 3
EPS_RMS, EPS_LN = 1e-6, 1e-5
HH, SUB, CHUNK = 8, 16, 64
NCH = S // CHUNK
ALPHA = 2.0 ** 0.25
WINDOWS = (2, 4, 8, 16)
NE, TOPE, PLE = 32, 4, 256
SW_LIMIT, SW_ALPHA = 7.0, 1.702
ROWS = 128
NBLK = (S * TOPE) // ROWS + NE - 1
TABLE = NBLK + 1

MASKED, TAKEN, ACAUSAL = -1e30, -2e38, -3e38

FFN_PANELS = FT // 2
N_ADA = 6 * D // PANEL


class Columns:

    def __init__(self):
        self.at, self.n = {}, 0

    def add(self, name, n):
        self.at[name] = self.n
        self.n += n


COLS = Columns()
for _name, _n in (
    ("norm_mix", DT), ("conv_w", M_CONV * 4), ("conv_b", 4), ("i_bias", 1), ("f_bias", 1),
    ("mlstm_norm", MH), ("idx_norm", 1), ("norm_ffn", DT), ("ffn_conv", FFN_PANELS * 16),
    ("norm_final", DT),
    ("c2", DT), ("b_ada", 48), ("b_gate", 2 * DT), ("lb0", HH), ("lb1", HH), ("hgrn_norm", 1),
    ("ln1_w2", DT), ("ln1_b2", DT), ("ln2_w2", DT), ("ln2_b2", DT),
    ("conv_w3", 3 * 4), ("pool_scale", 4), ("ln1_g3", DT), ("ln1_b3", DT), ("ln2_g3", DT), ("ln2_b3", DT),
    ("ple_b", DT), ("ln3_g3", DT), ("ln3_b3", DT),
):
    COLS.add(_name, _n)

PANELS = (
    ("w_in", 8), ("w_ada", 12), ("w_out", 2), ("w_up", 11), ("w_down", 6),
    ("w_zi", 2), ("w_head", 8), ("w_mix_a", 4), ("w_zv", 2), ("w_mix_b", 4),
    ("w_out_2", 2), ("w_ffn_in", 11), ("w_ffn_out", 6),
    ("w_in_3", 4), ("w_out_3", 2), ("ple_proj", 1), ("ple_gate", 2),
)
SPLIT = ("w_in", "w_up", "w_down", "w_mix_a", "w_zv", "w_mix_b", "w_ffn_in", "w_ffn_out")
SPLIT_INDEX = {}
FIRST = {}
_n = 0
for _name, _c in PANELS:
    FIRST[_name] = _n
    if _name in SPLIT:
        SPLIT_INDEX.update({_n + _i: len(SPLIT_INDEX) + _i for _i in range(_c)})
    _n += _c
N_PANELS = _n


class Ring:

    def __init__(self, tile, low, source, landed):
        self.tile, self.low, self.source, self.landed = tile, low, source, landed
        self.loaded, self.freed = 0, {}
        self.high, self.high_done, self.low_done = None, 0, 0

    def load_until(self, sp, end):
        for n in range(self.loaded, min(end, N_PANELS)):
            if n - SLOTS in self.freed:
                sp.wait_ge(*self.freed[n - SLOTS])
            sp.dma_start(self.tile[:, n % SLOTS, :], self.source[n]).then_inc(self.landed[n % SLOTS], 16)
        self.loaded = max(self.loaded, min(end, N_PANELS))

    def split_parts(self, n):
        for c in range(PARTS):
            part = slice(c * KT * PANEL // PARTS, (c + 1) * KT * PANEL // PARTS)
            yield self.tile[:, n % SLOTS, part], self.high[:, n % SLOTS, part], self.low[:, n % SLOTS, part]

    def high_panel(self, act, n, more=0):
        act.wait_ge(self.landed[n % SLOTS], more * 16 + 16 * (n // SLOTS + 1))
        for full, high, _ in self.split_parts(n):
            act.activation(high, full, ACT.Copy).then_inc(self.high_ready, 1)

    def low_panel(self, pool, n, more=0):
        for c, (full, high, low) in enumerate(self.split_parts(n)):
            pool.wait_ge(self.high_ready, more * (2 * PARTS) + PARTS * SPLIT_INDEX[n] + c + 1)
            pool.tensor_tensor(low, full, high.bitcast(F32), ALU.subtract).then_inc(self.low_ready, 1)

    def high_until(self, act, end):
        for n in range(self.high_done, end):
            if n in SPLIT_INDEX:
                self.high_panel(act, n)
        self.high_done = max(self.high_done, end)

    def low_until(self, pool, end):
        for n in range(self.low_done, end):
            if n in SPLIT_INDEX:
                self.low_panel(pool, n)
        self.low_done = max(self.low_done, end)

    def wait_split(self, e):
        e.wait_ge(self.low_ready, PARTS * sum(n < self.low_done for n in SPLIT_INDEX))

    def wait_part(self, pe, n, k, more=0):
        pe.wait_ge(self.low_ready, more * (2 * PARTS) + PARTS * SPLIT_INDEX[n] + k // (KT // PARTS) + 1)

    def halves(self, n, k, col, width):
        at = slice(k * PANEL + col, k * PANEL + col + width)
        return self.high[:, n % SLOTS, at], self.low[:, n % SLOTS, at]

    def wait_landed(self, pe, n):
        pe.wait_ge(self.landed[n % SLOTS], 16 * (n // SLOTS + 1))

    def weights(self, n, k, col, width):
        return self.tile[:, n % SLOTS, k * PANEL + col:k * PANEL + col + width]


def tile_of(t, i):
    return t[:, i, :]


def tile_halves(high, low, i):
    return high[:, i, :], low[:, i, :]


def placed(nc, stack, name, shape, dtype):
    at = -(-nc.sbuf_base // 32) * 32
    t = stack.enter_context(nc.sbuf_tensor(name, shape, dtype))
    assert nc.sbuf_base == at + 4 * int(np.prod(shape[1:]))
    return t, at


def with_low(nc, stack, name, shape):
    t, at = placed(nc, stack, name, shape, F32)
    return t, nc.alloc_sbuf_tensor_at(f"{name}_low", shape, F32R, offset=at)


def split_product(pe, out, a, b, start, stop):
    pe.matmul(out, a[0], b[0], start=start, stop=False)
    pe.matmul(out, a[0], b[1], start=False, stop=False)
    return pe.matmul(out, a[1], b[0], start=False, stop=stop)


def norm_stage(g, name, src, dst, scale, eps, ones_mean, bias=None, centre=False, tiles=DT, last_panel=0,
               high=None, low=None, split_to=0):
    nc, ring, psum, eps_col = g.nc, g.ring, g.psum, g.eps[eps]
    with ExitStack() as own:
        sem = g.stage_semaphores(name)
        squares = own.enter_context(nc.sbuf_tensor(f"{name}_squares", [P, 2, S], F32))
        std = own.enter_context(nc.sbuf_tensor(f"{name}_std", [P, S], F32))
        rstd = own.enter_context(nc.sbuf_tensor(f"{name}_rstd", [P, S], F32))
        mean_ready, centred, squared, summed = sem("mean_ready"), sem("centred"), sem("squared"), sem("summed")
        std_ready, rstd_ready, scaled = sem("std_ready"), sem("rstd_ready"), sem("scaled")
        biased, high_ready, low_ready = sem("biased"), sem("high_ready"), sem("low_ready")
        mean, var = psum[:, 0, :], psum[:, 1, :]
        body = dst if centre else src
        with nc.Block(no_gpsimd_drain=True) as block:

            @block.tensor
            def _(pe):
                if centre:
                    for t in range(tiles):
                        mm = pe.matmul(mean, ones_mean, tile_of(src, t), start=t == 0, stop=t == tiles - 1)
                    mm.then_inc(mean_ready, 1)
                for t in range(tiles):
                    pe.wait_ge(squared, t + 1)
                    pe.matmul(var, ones_mean, squares[:, t % 2, :], start=t == 0, stop=t == tiles - 1)\
                        .then_inc(summed, 1)

            @block.sync
            def _(sp):
                g.clear_past(sp)
                ring.load_until(sp, last_panel)

            @block.scalar
            def _(act):
                for t in range(tiles):
                    if centre:
                        act.wait_ge(centred, t + 1)
                    if t >= 2:
                        act.wait_ge(summed, t - 1)
                    act.activation(squares[:, t % 2, :], tile_of(body, t), ACT.Square).then_inc(squared, 1)
                act.wait_ge(summed, tiles)
                act.activation(std[:, :], var, ACT.Sqrt, bias=eps_col).then_inc(std_ready, 1)
                ring.high_until(act, split_to - 1)
                for t in range(tiles + 1):
                    if bias is not None and t < tiles:
                        act.wait_ge(scaled, t + 1)
                        act.activation(tile_of(dst, t), tile_of(dst, t), ACT.Identity, bias=bias(t)).then_inc(biased, 1)
                    if high is not None and t > 0:
                        act.wait_ge(biased if bias is not None else scaled, t)
                        act.activation(tile_of(high, t - 1), tile_of(dst, t - 1), ACT.Copy).then_inc(high_ready, 1)
                ring.high_until(act, split_to)

            def low_half(e, t):
                e.wait_ge(high_ready, t + 1)
                d = tile_of(dst, t)
                e.tensor_tensor(tile_of(low, t), d, tile_of(high, t).bitcast(F32), ALU.subtract).then_inc(low_ready, 1)

            @block.gpsimd
            def _(pool):
                ring.low_until(pool, split_to - 1)
                if high is not None:
                    for t in range(0, tiles, 2):
                        low_half(pool, t)
                ring.low_until(pool, split_to)
                if high is not None:
                    pool.wait_ge(low_ready, tiles)

            @block.vector
            def _(dve):
                if centre:
                    dve.wait_ge(mean_ready, 1)
                    for t in range(tiles):
                        dve.tensor_tensor(tile_of(dst, t), tile_of(src, t), mean, ALU.subtract).then_inc(centred, 1)
                dve.wait_ge(std_ready, 1)
                dve.reciprocal(rstd[:, :], std[:, :]).then_inc(rstd_ready, 1)
                dve.wait_ge(rstd_ready, 1)
                if centre:
                    dve.wait_ge(centred, tiles)
                for t in range(tiles):
                    dve.scalar_tensor_tensor(tile_of(dst, t), tile_of(body, t), scale(t), rstd[:, :],
                                             ALU.mult, ALU.mult).then_inc(scaled, 1)
                if high is not None:
                    for t in range(1, tiles, 2):
                        low_half(dve, t)


class Tile:

    def __init__(self, panels, col, width, rhs, out, engine, take, tokens=None, kts=(KT,), halves=None):
        self.panels, self.col, self.width, self.rhs, self.out = panels, col, width, rhs, out
        self.engine, self.take, self.tokens, self.kts = engine, take, tokens, kts
        self.halves = halves


def scale_first(dve, x, scaled):
    for t in range(0, DT, 2):
        dve.tensor_scalar(x[:, t:t + 2, :], x[:, t:t + 2, :], ALPHA, None, ALU.mult).then_inc(scaled, 1)
    dve.wait_ge(scaled, DT // 2)


def dense_stage(g, name, tiles, last_panel, split_to=0, scale_x=None):
    nc, ring, psum = g.nc, g.ring, g.psum
    with ExitStack() as own:
        sem = g.stage_semaphores(name)
        tile_ready, act_took, dve_took = sem("tile_ready"), sem("act_took"), sem("dve_took")
        scaled = sem("scaled")
        taken = {"act": [], "dve": []}
        for t in tiles:
            for e, counts in taken.items():
                counts.append((counts[-1] if counts else 0) + (t.engine == e))
        with nc.Block(no_gpsimd_drain=True) as block:

            @block.tensor
            def _(pe):
                for i, t in enumerate(tiles):
                    if i >= BANKS:
                        e = tiles[i - BANKS].engine
                        pe.wait_ge(act_took if e == "act" else dve_took, taken[e][i - BANKS])
                    bank = psum[:, i % BANKS, :]
                    k0, total = 0, sum(t.kts)
                    for n, kt in zip(t.panels, t.kts):
                        if t.halves is None:
                            ring.wait_landed(pe, n)
                        for k in range(kt):
                            start, stop = k0 + k == 0, k0 + k == total - 1
                            out = bank[0:t.width, :] if t.tokens is None else bank[:, 0:t.width]
                            if t.halves is None:
                                w, x = (ring.weights(n, k, t.col, t.width),), (tile_of(t.rhs, k0 + k),)
                            else:
                                ring.wait_part(pe, n, k)
                                w, x = ring.halves(n, k, t.col, t.width), tile_halves(*t.halves, k0 + k)
                            if t.tokens is not None:
                                w, x = tuple(v[:, t.tokens * P:(t.tokens + 1) * P] for v in x), w
                            if t.halves is None:
                                mm = pe.matmul(out, w[0], x[0], start=start, stop=stop)
                            else:
                                mm = split_product(pe, out, w, x, start, stop)
                        k0 += kt
                        ring.freed[n] = (tile_ready, i + 1)
                    mm.then_inc(tile_ready, 1)

            @block.sync
            def _(sp):
                g.clear_past(sp)
                ring.load_until(sp, last_panel)

            @block.scalar
            def _(act):
                for i, t in enumerate(tiles):
                    ring.high_until(act, min(split_to, t.panels[0] + SLOTS))
                    if t.engine == "act":
                        act.wait_ge(tile_ready, i + 1)
                        t.take(act, psum[:, i % BANKS, :]).then_inc(act_took, 1)

            @block.gpsimd
            def _(pool):
                ring.low_until(pool, split_to)

            @block.vector
            def _(dve):
                if scale_x is not None:
                    scale_first(dve, scale_x, scaled)
                for i, t in enumerate(tiles):
                    if t.engine == "dve":
                        dve.wait_ge(tile_ready, i + 1)
                        t.take(dve, psum[:, i % BANKS, :]).then_inc(dve_took, 1)


def feed_forward(g, name, high, low, mid, mid_low, taps, up, down, combine, conv, scale_x=None):
    nc, ring, psum, cols = g.nc, g.ring, g.psum, g.cols
    with ExitStack() as own:
        sem = g.stage_semaphores(name)
        gate_val = own.enter_context(nc.sbuf_tensor(f"{name}_gate_val", [P, 2, 2, S], F32))
        gate_act = own.enter_context(nc.sbuf_tensor(f"{name}_gate_act", [P, 2, S], F32))
        up_ready = [sem(f"up_ready{q}") for q in range(2)]
        based, tapped, silued, made = sem("based"), sem("tapped"), sem("silued"), sem("made")
        half = [psum[:, 4 * q:4 * q + 4, :] for q in range(2)]
        loops = FFN_PANELS // 2
        last = FFN_PANELS - 1

        with nc.Block(no_gpsimd_drain=True) as block:

            @block.tensor
            def _(pe):
                n0 = FIRST[up]
                with pe.Fori(0, loops) as i:
                    for q in range(2):
                        n = n0 + q
                        pe.wait_ge(made, i * 4 + 2 * q + 2)
                        for m in range(4):
                            for k in range(KT):
                                if m == 0 and k % (KT // PARTS) == 0:
                                    ring.wait_part(pe, n, k, i)
                                mm = split_product(pe, half[q][:, m, :], ring.halves(n, k, m * P, P),
                                                   tile_halves(high, low, k), k == 0, k == KT - 1)
                            mm.then_inc(up_ready[q], 1)
                n = n0 + last
                pe.wait_ge(made, 4 + 2 * (last - 1))
                for m in range(4):
                    for k in range(KT):
                        ring.wait_part(pe, n, k)
                        mm = split_product(pe, half[0][:, m, :], ring.halves(n, k, m * P, P),
                                           tile_halves(high, low, k), k == 0, k == KT - 1)
                    mm.then_inc(up_ready[0], 1)
                for p in range(FFN_PANELS):
                    ring.freed[n0 + p] = (up_ready[p % 2], 4 * (p // 2 + 1))

            @block.sync
            def _(sp):
                g.clear_past(sp)
                ring.load_until(sp, FIRST[up] + FFN_PANELS + SLOTS)

            def act_pair(act, q, j, ready, pair, column):
                buf = j
                act.wait_ge(up_ready[q], ready)
                act.wait_ge(made, pair + 3)
                if conv:
                    for part in range(2):
                        act.activation(gate_val[:, buf, part, :], half[q][:, 2 * part + j, :], ACT.Identity,
                                       scale=column(2, part, j), bias=column(3, part, j)).then_inc(based, 1)
                    act.wait_ge(tapped, (pair + 1) * 2)
                    act.activation(gate_act[:, buf, :], gate_val[:, buf, 0, :], ACT.Silu).then_inc(silued, 1)
                else:
                    act.activation(gate_act[:, buf, :], half[q][:, j, :], ACT.Silu).then_inc(silued, 1)

            def dve_pair(dve, q, j, ready, pair, column, out):
                buf = j
                if conv:
                    dve.wait_ge(based, (pair + 1) * 2)
                    for tap, back in ((1, 1), (0, 2)):
                        if tap == 0:
                            dve.wait_ge(first_tap, (pair + 1) * 2)
                        for part in range(2):
                            to = gate_val[:, buf, part, back:]
                            dve.scalar_tensor_tensor(to, half[q][:, 2 * part + j, 0:S - back],
                                                     column(tap, part, j), to, ALU.mult, ALU.add)\
                                .then_inc(first_tap if tap else tapped, 1)
                    dve.wait_ge(tapped, (pair + 1) * 2)
                    dve.wait_ge(silued, pair + 1)
                    dve.tensor_tensor(out, gate_act[:, buf, :], gate_val[:, buf, 1, :], ALU.mult).then_inc(made, 1)
                else:
                    dve.wait_ge(silued, pair + 1)
                    dve.tensor_tensor(out, gate_act[:, buf, :], half[q][:, 2 + j, :], ALU.mult).then_inc(made, 1)

            first_tap = sem("first_tap")

            def column(base):
                return lambda tap, part, j: cols[:, bass.ds(base + 4 * tap + 2 * part + j, 1)]

            @block.scalar
            def _(act):
                with act.Fori(0, loops) as i:
                    for q in range(2):
                        for j in range(2):
                            act_pair(act, q, j, i * 4 + 3 + j, i * 4 + 2 * q + j, column(i * 32 + taps + 16 * q))
                        ring.high_panel(act, FIRST[up] + SLOTS + q, i)
                ring.high_done = FIRST[up] + SLOTS + 2 * loops
                for j in range(2):
                    act_pair(act, 0, j, loops * 4 + 3 + j, 2 * last + j, column(taps + 16 * last))
                ring.high_until(act, FIRST[down] + SLOTS)

            @block.gpsimd
            def _(pool):
                with pool.Fori(0, loops) as i:
                    for q in range(2):
                        ring.low_panel(pool, FIRST[up] + SLOTS + q, i)
                ring.low_done = FIRST[up] + SLOTS + 2 * loops
                ring.low_until(pool, FIRST[down] + SLOTS)

            @block.vector
            def _(dve):
                for _ in range(4):
                    dve.sem_inc(made, 1)
                with dve.Fori(0, loops) as i:
                    for q in range(2):
                        for j in range(2):
                            pair = i * 4 + 2 * q + j
                            dve_pair(dve, q, j, None, pair, column(i * 32 + taps + 16 * q),
                                     mid[:, bass.ds(pair, 1), :].rearrange("p a s -> p (a s)"))
                for j in range(2):
                    dve_pair(dve, 0, j, None, 2 * last + j, column(taps + 16 * last), tile_of(mid, 2 * last + j))

    with nc.sbuf_tensor(f"{name}_more_high", [P, FT - 2 * DT, S], F32R) as more:
        highs = [tile_of(high, t) for t in range(DT)] + [tile_of(low, t) for t in range(DT)] + \
            [tile_of(more, t) for t in range(FT - 2 * DT)]
        wide_stage(g, name + "_down", FIRST[down], mid, mid_low, highs, [combine(t) for t in range(DT)], scale_x)


def wide_stage(g, name, n0, mid, mid_low, highs, takes, scale_x):
    nc, ring, psum = g.nc, g.ring, g.psum
    kts = (KT, KT, FT - 2 * KT)
    with ExitStack() as own:
        sem = g.stage_semaphores(name)
        part_done, tile_ready, took = sem("part_done"), sem("tile_ready"), sem("took")
        high_ready, low_ready, scaled = sem("high_ready"), sem("low_ready"), sem("scaled")
        with nc.Block(no_gpsimd_drain=True) as block:

            @block.tensor
            def _(pe):
                for c in range(2):
                    for p, kt in enumerate(kts):
                        n = n0 + 3 * c + p
                        for m in range(4):
                            if m == 3:
                                ring.wait_part(pe, n, KT - 1)
                            for k in range(kt):
                                at = KT * p + k
                                if m == 0:
                                    ring.wait_part(pe, n, k)
                                    if c == 0:
                                        pe.wait_ge(low_ready, at + 1)
                                mm = split_product(pe, psum[:, 4 * c + m, :], ring.halves(n, k, m * P, P),
                                                   (highs[at], tile_of(mid_low, at)), at == 0, at == FT - 1)
                            if p == 2:
                                mm.then_inc(tile_ready, 1)
                        if p < 2:
                            mm.then_inc(part_done, 1)
                            ring.freed[n] = (part_done, 2 * c + p + 1)
                        else:
                            ring.freed[n] = (tile_ready, 4 * (c + 1))

            @block.sync
            def _(sp):
                g.clear_past(sp)
                ring.load_until(sp, n0 + 6 + SLOTS)

            @block.scalar
            def _(act):
                for t in range(FT):
                    act.activation(highs[t], tile_of(mid, t), ACT.Copy).then_inc(high_ready, 1)
                ring.high_until(act, n0 + 6)

            @block.gpsimd
            def _(pool):
                for t in range(FT):
                    pool.wait_ge(high_ready, t + 1)
                    pool.tensor_tensor(tile_of(mid_low, t), tile_of(mid, t), highs[t].bitcast(F32), ALU.subtract).then_inc(low_ready, 1)
                ring.low_until(pool, n0 + 6)

            @block.vector
            def _(dve):
                if scale_x is not None:
                    scale_first(dve, scale_x, scaled)
                for i, take in enumerate(takes):
                    dve.wait_ge(tile_ready, i + 1)
                    take(dve, psum[:, i, :]).then_inc(took, 1)


class Modulation:
    EARLY = 3

    def __init__(self, cond, early):
        self.cond, self.early, self.later = cond, early, None

    def part(self, p, first=0, width=PANEL):
        row, at = (self.early, p * PANEL) if p < self.EARLY else (self.later, (p - self.EARLY) * PANEL)
        return row[0:1, at + first:at + first + width]

    def product(self, g, pe, p, bank, panel_done, done):
        n = FIRST["w_ada"] + p
        g.ring.wait_landed(pe, n)
        for k in range(KT):
            mm = pe.matmul(bank[0:1, :], self.cond[:, k:k + 1], g.ring.weights(n, k, 0, PANEL),
                           start=k == 0, stop=k == KT - 1)
        mm.then_inc(panel_done, 1)
        g.ring.freed[n] = (panel_done, done)

    def take(self, act, p, bank):
        return act.activation(self.part(p), bank[0:1, :], ACT.Copy)


def mlstm_stage(g, b1, mix, mo):
    nc, ring, psum, cols, col = g.nc, g.ring, g.psum, g.cols, g.col
    with ExitStack() as own:
        sb = lambda n, shape: own.enter_context(nc.sbuf_tensor(f"ml_{n}", shape, F32))
        sem = g.stage_semaphores("ml")
        conv = sb("conv", [P, 4, S])
        f_pre, f_abs, f_exp, f_log = (sb(n, [MH, S]) for n in ("f_pre", "f_abs", "f_exp", "f_log"))
        logf, cum, i_row, a_row, max_row, m_row = (sb(n, [MH, S]) for n in ("logf", "cum", "i_row", "a_row", "max_row", "m_row"))
        ones_row = sb("ones_row", [MH, S])
        a_col = sb("a_col", [P, TT, MH])
        weight, prob = (sb(n, [P, TT, S]) for n in ("weight", "prob"))
        floor, den, num, sq = (sb(n, [P, 2, S]) for n in ("floor", "den", "num", "sq"))
        std, rstd = sb("std", [P, S]), sb("rstd", [P, S])
        base_done, tap_done, conv_done, qk_ready = sem("base_done"), sem("tap_done"), sem("conv_done"), sem("qk_ready")
        row_act, row_dve, rows_ready, acol_psum, acol_ready = (sem(n) for n in ("row_act", "row_dve", "rows_ready", "acol_psum", "acol_ready"))
        spread, floored, arg_ready, weight_ready, score_ready = (sem(n) for n in ("spread", "floored", "arg_ready", "weight_ready", "score_ready"))
        scaled, prob_ready, summed, den_ready, inv_ready, num_ready = (sem(n) for n in ("scaled", "prob_ready", "summed", "den_ready", "inv_ready", "num_ready"))
        squared, sq_summed, std_ready, rstd_ready, normed, mixed, ones_set, absed = (sem(n) for n in ("squared", "sq_summed", "std_ready", "rstd_ready", "normed", "mixed", "ones_set", "absed"))
        max_bank, m_bank, num_bank, den_bank = psum[:, 4, :], psum[:, 5, :], psum[:, 6, :], psum[:, 7, :]

        cond_ready, panel_done, row_ready = sem("cond_ready"), sem("panel_done"), sem("row_ready")

        def of_head(h, first):
            return first + h // 2, slice(64 * (h % 2), 64 * (h % 2) + 64)

        with nc.Block(no_gpsimd_drain=True) as block:

            @block.scalar
            def _(act):
                act.activation(mo.cond[:, :], cols[:, COLS.at["c2"]:COLS.at["c2"] + DT], ACT.Silu).then_inc(cond_ready, 1)
                act.activation(f_pre[:, :], b1["f_raw"][:, :], ACT.Identity, bias=col("f_bias")[0:MH]).then_inc(row_act, 1)
                act.activation(i_row[:, :], b1["i_raw"][:, :], ACT.Identity, bias=col("i_bias")[0:MH]).then_inc(row_act, 1)
                act.wait_ge(row_act, 1)
                act.activation(f_abs[:, :], f_pre[:, :], ACT.Abs).then_inc(row_act, 1)
                act.wait_ge(row_act, 3)
                act.activation(f_exp[:, :], f_abs[:, :], ACT.Exp, scale=-1.0).then_inc(row_act, 1)
                act.wait_ge(row_act, 4)
                act.activation(f_log[:, :], f_exp[:, :], ACT.Ln, bias=1.0).then_inc(row_act, 1)
                for t in range(4):
                    act.activation(conv[:, t, :], b1["qk"][:, t, :], ACT.Identity, scale=col("conv_w", 3 * 4 + t),
                                   bias=col("conv_b", t)).then_inc(base_done, 1)
                for t in range(4):
                    act.wait_ge(conv_done, t + 1)
                    act.activation(b1["qk"][:, t, :], conv[:, t, :], ACT.Silu).then_inc(qk_ready, 1)
                for p in range(mo.EARLY):
                    act.wait_ge(panel_done, p + 1)
                    mo.take(act, p, psum[:, 1 + p, :]).then_inc(row_ready, 1)
                for h in range(MH):
                    act.wait_ge(spread, 2 * h + 2)
                    if h >= 2:
                        act.wait_ge(den_ready, h - 1)
                    act.activation(floor[:, h % 2, :], m_bank, ACT.Exp).then_inc(floored, 1)
                    for j in range(TT):
                        w = S - P * j
                        act.wait_ge(arg_ready, TT * h + j + 1)
                        act.activation(weight[:, j, 0:w], weight[:, j, 0:w], ACT.Exp).then_inc(weight_ready, 1)
                    act.wait_ge(summed, h + 1)
                    if h >= 2:
                        act.wait_ge(num_ready, h - 1)
                    act.activation(den[:, h % 2, :], den_bank, ACT.Abs).then_inc(absed, 1)
                    act.wait_ge(num_ready, h + 1)
                    if h >= 2:
                        act.wait_ge(sq_summed, h - 1)
                    act.activation(sq[:, h % 2, :], num[:, h % 2, :], ACT.Square).then_inc(squared, 1)
                    act.wait_ge(sq_summed, h + 1)
                    if h >= 1:
                        act.wait_ge(rstd_ready, h)
                    act.activation(std[:, :], m_bank, ACT.Sqrt, scale=1.0 / M_DV, bias=g.eps[EPS_RMS]).then_inc(std_ready, 1)

            @block.tensor
            def _(pe):
                pe.wait_ge(cond_ready, 1)
                for p in range(mo.EARLY):
                    mo.product(g, pe, p, psum[:, 1 + p, :], panel_done, p + 1)
                pe.wait_ge(rows_ready, 2)
                for j in range(TT):
                    mm = pe.matmul(psum[:, 0, MH * j:MH * j + MH], a_row[:, j * P:(j + 1) * P], g.ident[0:MH, 0:MH],
                                   start=True, stop=True)
                mm.then_inc(acol_psum, 1)
                pe.wait_ge(qk_ready, 4)
                pe.wait_ge(acol_ready, 1)
                for h in range(MH):
                    if h >= 1:
                        pe.wait_ge(arg_ready, TT * h)
                        pe.wait_ge(std_ready, h)
                    pe.matmul(max_bank, g.neg_head[:, h, :], max_row[:, :], start=True, stop=True).then_inc(spread, 1)
                    pe.matmul(m_bank, g.neg_head[:, h, :], m_row[:, :], start=True, stop=True).then_inc(spread, 1)
                    tq, pq = of_head(h, 0)
                    tk, pk = of_head(h, 2)
                    for j in range(TT):
                        if h >= 1:
                            pe.wait_ge(scaled, TT * (h - 1) + j + 1)
                        elif j >= 1:
                            pe.wait_ge(row_ready, j)
                        pe.matmul(psum[:, j, 0:S - P * j], b1["qk"][pk, tk, j * P:(j + 1) * P], b1["qk"][pq, tq, j * P:S],
                                  start=True, stop=True).then_inc(score_ready, 1)
                    if h >= 1:
                        pe.wait_ge(num_ready, h)
                    for j in range(TT):
                        pe.wait_ge(prob_ready, TT * h + j + 1)
                        w = S - P * j
                        pe.matmul(num_bank[:, P * j:S], b1["mv"][:, j, h * M_DV:(h + 1) * M_DV], prob[:, j, 0:w],
                                  start=j == 0, stop=j == TT - 1)
                        mm = pe.matmul(den_bank[:, P * j:S], g.ones, prob[:, j, 0:w], start=j == 0, stop=j == TT - 1)
                    mm.then_inc(summed, 1)
                    pe.wait_ge(squared, h + 1)
                    pe.wait_ge(floored, h + 1)
                    pe.matmul(m_bank, g.ones, sq[:, h % 2, :], start=True, stop=True).then_inc(sq_summed, 1)

            @block.sync
            def _(sp):
                g.clear_past(sp)
                ring.load_until(sp, FIRST["w_ada"] + mo.EARLY + SLOTS)

            @block.vector
            def _(dve):
                dve.memset(ones_row[:, :], 1.0).then_inc(ones_set, 1)
                dve.wait_ge(row_act, 5)
                dve.scalar_tensor_tensor(logf[:, :], f_pre[:, :], 0.0, f_log[:, :], ALU.min, ALU.subtract).then_inc(row_dve, 1)
                dve.wait_ge(row_dve, 1)
                dve.wait_ge(ones_set, 1)
                dve.tensor_tensor_scan(cum[:, :], ones_row[:, :], logf[:, :], 0.0, ALU.mult, ALU.add).then_inc(row_dve, 1)
                dve.wait_ge(row_dve, 2)
                dve.tensor_tensor(a_row[:, :], i_row[:, :], cum[:, :], ALU.subtract).then_inc(rows_ready, 1)
                dve.wait_ge(rows_ready, 1)
                dve.tensor_tensor_scan(max_row[:, :], a_row[:, :], a_row[:, :], 0.0, ALU.max, ALU.max).then_inc(row_dve, 1)
                dve.wait_ge(row_dve, 3)
                dve.tensor_tensor(m_row[:, :], cum[:, :], max_row[:, :], ALU.add).then_inc(rows_ready, 1)
                for t in range(4):
                    dve.wait_ge(base_done, t + 1)
                    for tap in (2, 1, 0):
                        back = M_CONV - 1 - tap
                        if tap < 2:
                            dve.wait_ge(tap_done, 2 * t + 2 - tap)
                        to = conv[:, t, back:]
                        dve.scalar_tensor_tensor(to, b1["qk"][:, t, 0:S - back], col("conv_w", tap * 4 + t), to,
                                                 ALU.mult, ALU.add).then_inc(tap_done if tap else conv_done, 1)
                dve.wait_ge(acol_psum, 1)
                dve.tensor_copy(a_col[:, :, :], psum[:, 0, 0:TT * MH].rearrange("p (j h) -> p j h", h=MH)).then_inc(acol_ready, 1)
                dve.wait_ge(acol_ready, 1)
                for h in range(MH):
                    b = h % 2
                    dve.wait_ge(spread, 2 * h + 1)
                    for j in range(TT):
                        w = S - P * j
                        if h >= 1:
                            dve.wait_ge(scaled, TT * (h - 1) + j + 1)
                        dve.tensor_scalar(weight[:, j, 0:w], max_bank[:, P * j:S], a_col[:, j, h:h + 1], 0.0,
                                          ALU.add, ALU.min).then_inc(arg_ready, 1)
                    for j in range(TT):
                        w = S - P * j
                        dve.wait_ge(weight_ready, TT * h + j + 1)
                        dve.wait_ge(score_ready, TT * h + j + 1)
                        dve.scalar_tensor_tensor(prob[:, j, 0:w], psum[:, j, 0:w], M_DQK ** -0.5, weight[:, j, 0:w],
                                                 ALU.mult, ALU.mult).then_inc(scaled, 1)
                        dve.wait_ge(scaled, TT * h + j + 1)
                        dve.tensor_tensor(prob[:, j, 0:P], prob[:, j, 0:P], g.upper, ALU.mult).then_inc(prob_ready, 1)
                    dve.wait_ge(floored, h + 1)
                    dve.wait_ge(absed, h + 1)
                    dve.tensor_tensor(den[:, b, :], den[:, b, :], floor[:, b, :], ALU.max).then_inc(den_ready, 1)
                    dve.wait_ge(den_ready, h + 1)
                    dve.reciprocal(den[:, b, :], den[:, b, :]).then_inc(inv_ready, 1)
                    dve.wait_ge(inv_ready, h + 1)
                    if h >= 2:
                        dve.wait_ge(squared, h - 1)
                    dve.tensor_tensor(num[:, b, :], num_bank, den[:, b, :], ALU.mult).then_inc(num_ready, 1)
                    dve.wait_ge(std_ready, h + 1)
                    dve.reciprocal(rstd[:, :], std[:, :]).then_inc(rstd_ready, 1)
                    dve.wait_ge(rstd_ready, h + 1)
                    dve.scalar_tensor_tensor(mix[:, h, :], num[:, b, :], col("mlstm_norm", h), rstd[:, :],
                                             ALU.mult, ALU.mult).then_inc(normed, 1)
                    dve.wait_ge(normed, h + 1)
                    dve.tensor_tensor(mix[:, h, :], mix[:, h, :], b1["o_gate"][:, h, :], ALU.mult).then_inc(mixed, 1)


def index_stage(g, b1, mask, mo):
    nc, ring, psum, cols, col = g.nc, g.ring, g.psum, g.cols, g.col
    with ExitStack() as own:
        sb = lambda n, shape: own.enter_context(nc.sbuf_tensor(f"ix_{n}", shape, F32))
        sem = g.stage_semaphores("ix")
        sq, std, rstd = sb("sq", [P, S]), sb("std", [P, S]), sb("rstd", [P, S])
        keys = sb("keys", [P, S])
        relued = sb("relued", [P, 4, S])
        work = sb("work", [P, TT, S])
        best = sb("best", [P, TT, 8])
        mo.later = sb("mod_row", [1, (N_ADA - mo.EARLY) * PANEL])
        row_ready, columns_ready = sem("row_ready"), sem("columns_ready")
        panel_done, summed, plus_one = sem("panel_done"), sem("summed"), sem("plus_one")
        squared, sq_summed, std_ready, rstd_ready, keys_ready = (sem(n) for n in ("squared", "sq_summed", "std_ready", "rstd_ready", "keys_ready"))
        raw_ready, relu_ready, added, limited, found, replaced, masked = (sem(n) for n in ("raw_ready", "relu_ready", "added", "limited", "found", "replaced", "masked"))
        with nc.Block(no_gpsimd_drain=True) as block:

            @block.scalar
            def _(act):
                act.activation(sq[:, :], b1["ik"][:, :], ACT.Square).then_inc(squared, 1)
                act.wait_ge(sq_summed, 1)
                act.activation(std[:, :], psum[:, 0, :], ACT.Sqrt, scale=1.0 / IDIM, bias=g.eps[EPS_RMS]).then_inc(std_ready, 1)
                n = 0
                for i in range(TT):
                    for h in range(IH):
                        act.wait_ge(raw_ready, n + 1)
                        if n >= 4:
                            act.wait_ge(added, n - 3)
                        w = P * (i + 1)
                        act.activation(relued[:, n % 4, 0:w], psum[:, n % BANKS, 0:w], ACT.Relu, scale=IDIM ** -0.5)\
                            .then_inc(relu_ready, 1)
                        n += 1
                for p in range(mo.EARLY, N_ADA):
                    act.wait_ge(panel_done, p - mo.EARLY + 1)
                    mo.take(act, p, psum[:, p % 4, :]).then_inc(row_ready, 1)

            @block.tensor
            def _(pe):
                pe.wait_ge(squared, 1)
                pe.matmul(psum[:, 0, :], g.half_ones, sq[:, :], start=True, stop=True).then_inc(sq_summed, 1)
                pe.wait_ge(keys_ready, 1)
                n = 0
                for i in range(TT):
                    for h in range(IH):
                        if n >= BANKS:
                            pe.wait_ge(relu_ready, n - BANKS + 1)
                        half = slice(64 * (h % 2), 64 * (h % 2) + 64)
                        w = P * (i + 1)
                        pe.matmul(psum[:, n % BANKS, 0:w], b1["iq"][half, h // 2, i * P:(i + 1) * P], keys[half, 0:w],
                                  start=True, stop=True).then_inc(raw_ready, 1)
                        n += 1
                pe.wait_ge(relu_ready, n)
                for p in range(mo.EARLY, N_ADA):
                    done = p - mo.EARLY + 1
                    if done > 4:
                        pe.wait_ge(row_ready, done - 4)
                    mo.product(g, pe, p, psum[:, p % 4, :], panel_done, done)
                pe.wait_ge(row_ready, N_ADA - mo.EARLY)
                for j in range(6 * DT):
                    mm = pe.matmul(psum[:, 4, j:j + 1], mo.part(j // 4, j % 4 * P, P), g.ident[0:1, 0:1],
                                   start=True, stop=True)
                mm.then_inc(columns_ready, 1)

            @block.sync
            def _(sp):
                g.clear_past(sp)
                ring.load_until(sp, FIRST["w_ada"] + N_ADA + SLOTS)

            @block.vector
            def _(dve):
                dve.wait_ge(std_ready, 1)
                dve.reciprocal(rstd[:, :], std[:, :]).then_inc(rstd_ready, 1)
                dve.wait_ge(rstd_ready, 1)
                dve.scalar_tensor_tensor(keys[:, :], b1["ik"][:, :], col("idx_norm"), rstd[:, :], ALU.mult, ALU.mult)\
                    .then_inc(keys_ready, 1)
                n = 0
                for i in range(TT):
                    w = P * (i + 1)
                    for h in range(IH):
                        dve.wait_ge(relu_ready, n + 1)
                        if h == 0:
                            dve.tensor_scalar(work[:, i, 0:w], relued[:, n % 4, 0:w], b1["iw"][:, i, 0:1], None,
                                              ALU.mult).then_inc(added, 1)
                        else:
                            dve.wait_ge(added, n)
                            dve.scalar_tensor_tensor(work[:, i, 0:w], relued[:, n % 4, 0:w], b1["iw"][:, i, h:h + 1],
                                                     work[:, i, 0:w], ALU.mult, ALU.add).then_inc(added, 1)
                        n += 1
                for i in range(1, TT):
                    dve.wait_ge(added, IH * (i + 1))
                    d = work[:, i, P * i:P * i + P]
                    dve.tensor_tensor(d, d, g.acausal, ALU.min).then_inc(limited, 1)
                dve.tensor_copy(mask[:, 0, 0:P], g.causal_add).then_inc(masked, 1)
                for r in range(TOPK // 8):
                    for i in range(1, TT):
                        w = P * (i + 1)
                        m = (TT - 1) * r + i - 1
                        if r == 0:
                            dve.wait_ge(limited, i)
                        else:
                            dve.wait_ge(replaced, m - TT + 2)
                        dve.max(best[:, i, :], work[:, i, 0:w]).then_inc(found, 1)
                    for i in range(1, TT):
                        w = P * (i + 1)
                        dve.wait_ge(found, (TT - 1) * r + i)
                        dve.match_replace(work[:, i, 0:w], best[:, i, :], work[:, i, 0:w], TAKEN).then_inc(replaced, 1)
                for i in range(1, TT):
                    w = P * (i + 1)
                    dve.wait_ge(replaced, (TT - 1) * (TOPK // 8))
                    dve.tensor_scalar(mask[:, i, 0:w], work[:, i, 0:w], TAKEN, MASKED, ALU.not_equal, ALU.mult)\
                        .then_inc(masked, 1)
                at, mod = COLS.at["b_ada"], g.mod
                dve.wait_ge(columns_ready, 1)
                dve.tensor_tensor(mod[:, :], psum[:, 4, 0:6 * DT], cols[:, at:at + 6 * DT], ALU.add).then_inc(summed, 1)
                dve.wait_ge(summed, 1)
                for part in (1, 4):
                    s = mod[:, part * DT:(part + 1) * DT]
                    dve.tensor_scalar(s, s, 1.0, None, ALU.add).then_inc(plus_one, 1)


def attention_stage(g, b1, mask, rel, mix):
    nc, ring, psum = g.nc, g.ring, g.psum
    with ExitStack() as own:
        sb = lambda n, shape: own.enter_context(nc.sbuf_tensor(f"at_{n}", shape, F32))
        sem = g.stage_semaphores("at")
        logits, prob, prob_t = (sb(n, [P, 2, S]) for n in ("logits", "prob", "prob_t"))
        top, neg, total, inv = (sb(n, [P, TT * AH]) for n in ("top", "neg", "total", "inv"))
        heads = sb("heads", [P, 2, AH * ADH])
        qk_done, biased, masked, negated, exped, turned, copied = (sem(n) for n in ("qk_done", "biased", "masked", "negated", "exped", "turned", "copied"))
        pv_done, inverted, taken, mixed_t, mixed = (sem(n) for n in ("pv_done", "inverted", "taken", "mixed_t", "mixed"))
        NI = TT * AH
        with nc.Block(no_gpsimd_drain=True) as block:

            @block.sync
            def _(sp):
                g.clear_past(sp)
                ring.load_until(sp, FIRST["w_ada"] + SLOTS)

            @block.tensor
            def _(pe):
                def scores(n):
                    i, h = divmod(n, AH)
                    if n >= 2:
                        pe.wait_ge(biased, n - 1)
                    half = slice(64 * (h % 2), 64 * (h % 2) + 64)
                    w = P * (i + 1)
                    pe.matmul(psum[:, n % 2, 0:w], b1["aq"][half, h // 2, i * P:(i + 1) * P],
                              b1["ak"][half, h // 2, 0:w], start=True, stop=True).then_inc(qk_done, 1)

                def turn(n):
                    i, h = divmod(n, AH)
                    pe.wait_ge(exped, n + 1)
                    if n >= 2:
                        pe.wait_ge(copied, n - 1)
                    for j in range(i + 1):
                        mm = pe.transpose(psum[:, 2 + n % 2, j * P:(j + 1) * P], prob[:, n % 2, j * P:(j + 1) * P], g.ident)
                    mm.then_inc(turned, 1)

                def values(n):
                    i, h = divmod(n, AH)
                    pe.wait_ge(copied, n + 1)
                    if n >= 2:
                        pe.wait_ge(taken, n - 1)
                    for j in range(i + 1):
                        mm = pe.matmul(psum[:, 4 + n % 2, 0:ADH], prob_t[:, n % 2, j * P:(j + 1) * P],
                                       b1["av"][:, j, h * ADH:(h + 1) * ADH], start=j == 0, stop=j == i)
                    mm.then_inc(pv_done, 1)

                def turn_heads(i):
                    pe.wait_ge(taken, AH * (i + 1))
                    if i >= 2:
                        pe.wait_ge(mixed, i - 1)
                    for c in range(4):
                        mm = pe.transpose(psum[:, 6 + i % 2, c * P:(c + 1) * P], heads[:, i % 2, c * P:(c + 1) * P], g.ident)
                    mm.then_inc(mixed_t, 1)

                scores(0)
                for n in range(NI + 2):
                    if n + 1 < NI:
                        scores(n + 1)
                    if n < NI:
                        turn(n)
                    if 1 <= n <= NI:
                        values(n - 1)
                    if n >= 2 and (n - 1) % AH == 0:
                        turn_heads((n - 1) // AH - 1)

            @block.scalar
            def _(act):
                for n in range(NI + 1):
                    if n < NI:
                        i, h = divmod(n, AH)
                        w = P * (i + 1)
                        act.wait_ge(masked, n + 1)
                        act.activation(neg[:, n:n + 1], top[:, n:n + 1], ACT.Copy, scale=-1.0).then_inc(negated, 1)
                        act.wait_ge(negated, n + 1)
                        if n >= 2:
                            act.wait_ge(turned, n - 1)
                        act.activation(prob[:, n % 2, 0:w], logits[:, n % 2, 0:w], ACT.Exp, bias=neg[:, n:n + 1],
                                       accum_out=total[:, n:n + 1]).then_inc(exped, 1)
                    if n:
                        m = n - 1
                        w = P * (m // AH + 1)
                        act.wait_ge(turned, m + 1)
                        if m >= 2:
                            act.wait_ge(pv_done, m - 1)
                        act.activation(prob_t[:, m % 2, 0:w], psum[:, 2 + m % 2, 0:w], ACT.Copy).then_inc(copied, 1)

            @block.vector
            def _(dve):
                def soft(n):
                    i, h = divmod(n, AH)
                    w = P * (i + 1)
                    b = logits[:, n % 2, 0:w]
                    dve.wait_ge(qk_done, n + 1)
                    if n >= 2:
                        dve.wait_ge(exped, n - 1)
                    dve.scalar_tensor_tensor(b, psum[:, n % 2, 0:w], ADH ** -0.5, rel[:, h, S - w:S],
                                             ALU.mult, ALU.add).then_inc(biased, 1)
                    dve.wait_ge(biased, n + 1)
                    dve.tensor_tensor_reduce(out=b, in0=b, in1=mask[:, i, 0:w], scale=1.0, scalar=-3e38, op0=ALU.add,
                                             op1=ALU.max, accum_out=top[:, n:n + 1]).then_inc(masked, 1)

                def take(n):
                    i, h = divmod(n, AH)
                    dve.wait_ge(exped, n + 1)
                    dve.reciprocal(inv[:, n:n + 1], total[:, n:n + 1]).then_inc(inverted, 1)
                    dve.wait_ge(inverted, n + 1)
                    dve.wait_ge(pv_done, n + 1)
                    if i >= 2 and h == 0:
                        dve.wait_ge(mixed_t, i - 1)
                    dve.tensor_scalar(heads[:, i % 2, h * ADH:(h + 1) * ADH], psum[:, 4 + n % 2, 0:ADH], inv[:, n:n + 1],
                                      None, ALU.mult).then_inc(taken, 1)

                def mix_heads(i):
                    dve.wait_ge(mixed_t, i + 1)
                    dve.tensor_copy(mix[:, 4:8, i * P:(i + 1) * P],
                                    psum[:, 6 + i % 2, :].rearrange("p (c q) -> p c q", q=P)).then_inc(mixed, 1)

                soft(0)
                for n in range(NI + 2):
                    if n + 1 < NI:
                        soft(n + 1)
                    if 1 <= n <= NI:
                        take(n - 1)
                    if n >= 2 and (n - 1) % AH == 0:
                        mix_heads((n - 1) // AH - 1)


def block_1(g, x, h):
    nc, ring, psum, col = g.nc, g.ring, g.psum, g.col
    with ExitStack() as own:
        sb = lambda n, shape: own.enter_context(nc.sbuf_tensor(f"b1_{n}", shape, F32))
        b1 = {"qk": sb("qk", [P, 4, S]), "mv": sb("mv", [P, TT, S]), "o_gate": sb("o_gate", [P, 4, S]),
              "aq": sb("aq", [P, 4, S]), "ak": sb("ak", [P, 4, S]), "av": sb("av", [P, TT, S]),
              "iq": sb("iq", [P, 4, S]), "ik": sb("ik", [P, S]), "i_raw": sb("i_raw", [MH, S]),
              "f_raw": sb("f_raw", [MH, S]), "iw": sb("iw", [P, TT, IH])}
        split = own.enter_context(ExitStack())
        high = g.open_split(split, "in")
        norm_stage(g, "n1", x, h, lambda t: col("norm_mix", t), EPS_RMS, g.ones_mean, last_panel=SLOTS, high=high, low=g.h_low,
                   split_to=SLOTS)
        n0 = FIRST["w_in"]
        copy = {"act": lambda to: lambda e, bank: e.activation(to, bank[:, 0:to.shape[-1]], ACT.Copy),
                "dve": lambda to: lambda e, bank: e.tensor_copy(to, bank[:, 0:to.shape[-1]])}
        tiles = []
        for p, (name, tokens) in enumerate((("qk", 0), ("mv", 1), ("o_gate", 0), ("aq", 0), ("ak", 0), ("av", 1), ("iq", 0))):
            for m in range(4):
                to = b1[name][:, m, :]
                e = "act" if m % 2 or name == "o_gate" else "dve"
                take = copy[e](to) if name != "o_gate" else \
                    (lambda to: lambda a, bank: a.activation(to, bank, ACT.Sigmoid))(to)
                tiles.append(Tile([n0 + p], 0 if tokens else m * P, PANEL if tokens else P, h, to, e, take,
                                  tokens=m if tokens else None, halves=(high, g.h_low)))
        last = [n0 + 7]
        tiles.append(Tile(last, 0, P, h, None, "dve", copy["dve"](b1["ik"][:, :]), halves=(high, g.h_low)))
        for c, name in ((P, "i_raw"), (P + 4, "f_raw")):
            tiles.append(Tile(last, c, MH, h, None, "dve",
                              (lambda to: lambda e, bank: e.tensor_copy(to, bank[0:MH, :]))(b1[name][:, :]), halves=(high, g.h_low)))
        for m in range(TT):
            tiles.append(Tile(last, P + 8, IH, h, None, "act",
                              (lambda to: lambda a, bank: a.activation(to, bank[:, 0:IH], ACT.Copy, scale=IH ** -0.5))(b1["iw"][:, m, :]),
                              tokens=m, halves=(high, g.h_low)))
        dense_stage(g, "in1", tiles, n0 + 8 + SLOTS, split_to=n0 + 8)
        split.close()
        mo = Modulation(sb("cond", [P, DT]), h[:, 4:8, :].rearrange("p t s -> p (t s)"))
        mlstm_stage(g, b1, h, mo)
        with nc.sbuf_tensor("mask", [P, TT, S], F32) as mask:
            index_stage(g, b1, mask, mo)
            with nc.sbuf_tensor("rel", [P, AH, S], F32) as rel:
                rel_in = g.stage_semaphores("rel")("rel_in")
                with nc.Block(no_gpsimd_drain=True) as block:
                    @block.sync
                    def _(sp):
                        g.clear_past(sp)
                        sp.dma_start(rel[:, :, :], g.rel_bias).then_inc(rel_in, 16)
                        sp.wait_ge(rel_in, 16)
                attention_stage(g, b1, mask, rel, h)
    with ExitStack() as own:
        high = g.open_split(own, "ff1")
        n0 = FIRST["w_out"]
        dense_stage(g, "out1", [
            Tile([n0 + t // 4], t % 4 * P, P, h, None, "dve",
                 (lambda to: lambda e, bank: e.tensor_tensor(to, bank, to, ALU.add))(x[:, t, :])) for t in range(DT)],
            n0 + 2 + SLOTS, split_to=FIRST["w_up"] + 1)
        norm_stage(g, "n2", x, h, lambda t: col("norm_ffn", t), EPS_RMS, g.ones_mean, last_panel=FIRST["w_up"] + SLOTS,
                   high=high, low=g.h_low, split_to=FIRST["w_up"] + SLOTS)
        mid, mid_low = with_low(nc, own, "mid1", [P, FT, S])
        feed_forward(g, "ff1", high, g.h_low, mid, mid_low, COLS.at["ffn_conv"], "w_up", "w_down",
                     lambda t: (lambda to: lambda e, bank: e.tensor_tensor(to, bank, to, ALU.add))(x[:, t, :]), True)
    norm_stage(g, "n3", x, x, lambda t: col("norm_final", t), EPS_RMS, g.ones_mean, last_panel=FIRST["w_zi"] + SLOTS)


def hgrn_stage(g, h, vt, zu, ya):
    nc, ring, psum, cols, col = g.nc, g.ring, g.psum, g.cols, g.col
    n0 = FIRST["w_head"]
    NSUB = CHUNK // SUB
    with ExitStack() as own:
        sb = lambda n, shape: own.enter_context(nc.sbuf_tensor(f"hg_{n}", shape, F32))
        sem = g.stage_semaphores("hg")
        lb, one_less = sb("lb", [P, HH]), sb("one_less", [P, HH])
        forget, query, gate = sb("forget", [P, 2, S]), sb("query", [P, 2, S]), sb("gate", [P, 2, S])
        key, logf, cum16, cum64 = sb("key", [P, S]), sb("logf", [P, S]), sb("cum16", [P, S]), sb("cum64", [P, S])
        e16, e64, q16, q64 = sb("e16", [P, S]), sb("e64", [P, S]), sb("q16", [P, S]), sb("q64", [P, S])
        keys = sb("keys", [P, NSUB + 1, NCH, CHUNK])
        vh = sb("vh", [P, 2, TT, P])
        key_t, state, scores = sb("key_t", [P, TT, P]), sb("state", [P, NCH, P]), sb("scores", [P, TT, P])
        sq, std, rstd = sb("sq", [P, S]), sb("std", [P, S]), sb("rstd", [P, S])
        gemm_ready, gemm_took, lb_ready, zeroed = sem("gemm_ready"), sem("gemm_took"), sem("lb_ready"), sem("zeroed")
        f_ready, k_ready, ln_ready, cum_ready, e_ready, expo_ready, exp_ready = (sem(n) for n in (
            "f_ready", "k_ready", "ln_ready", "cum_ready", "e_ready", "expo_ready", "exp_ready"))
        q_ready, keys_ready, scored, masked, turned, key_t_ready, vh_ready = (sem(n) for n in (
            "q_ready", "keys_ready", "scored", "masked", "turned", "key_t_ready", "vh_ready"))
        u_ready, state_ready, o_ready, squared, sq_summed, std_ready, rstd_ready, normed, head_done = (sem(n) for n in (
            "u_ready", "state_ready", "o_ready", "squared", "sq_summed", "std_ready", "rstd_ready", "normed", "head_done"))
        c16 = cum16[:, :].rearrange("p (n c) -> p n c", c=CHUNK)
        c64 = cum64[:, :].rearrange("p (n c) -> p n c", c=CHUNK)
        k3 = key[:, :].rearrange("p (n c) -> p n c", c=CHUNK)
        e3 = e64[:, :].rearrange("p (n c) -> p n c", c=CHUNK)

        def column(name, i):
            return cols[:, bass.ds(COLS.at[name] + i, 1)]

        def head_of(t, i):
            return t[:, bass.ds(i, 1), :].rearrange("p a s -> p (a s)")

        def every_head(eng, body):
            with eng.Fori(0, HH // 2 - 1) as i:
                for q in range(2):
                    body(i * 2 + q, q, True)
            body(HH - 2, 0, True)
            body(HH - 1, 1, False)

        with nc.Block(no_gpsimd_drain=True) as block:

            @block.tensor
            def _(pe):
                def gemm(n, q, m):
                    p = n0 + q
                    if m == 0:
                        turn = (n - q) * 8
                        pe.wait_ge(ring.landed[p % SLOTS], turn + 16 * (p // SLOTS + 1))
                    pe.wait_ge(gemm_took, n * 4 + m + 1)
                    for k in range(KT):
                        mm = pe.matmul(psum[:, m, :], ring.weights(p, k, m * P, P), tile_of(h, k),
                                       start=k == 0, stop=k == KT - 1)
                    mm.then_inc(gemm_ready, 1)

                def body(n, q, more):
                    following = lambda m: gemm(n + 1, (q + 1) % 2, m) if more else None
                    following(0)
                    following(1)
                    pe.wait_ge(head_done, n + 2)
                    pe.wait_ge(q_ready, n * 2 + 1)
                    for i in range(NSUB):
                        pe.wait_ge(keys_ready, n * 5 + i + 1)
                        for c in range(NCH):
                            half = 64 * (c % 2)
                            at = (c // 2) * CHUNK + i * SUB
                            mm = pe.matmul(psum[half:half + 64, 4, at:at + SUB], keys[:, i, c, :],
                                           q16[:, c * CHUNK + i * SUB:c * CHUNK + (i + 1) * SUB], start=True, stop=True)
                    mm.then_inc(scored, 1)
                    pe.wait_ge(keys_ready, n * 5 + 5)
                    for t in range(TT):
                        mm = pe.transpose(psum[:, 5, t * P:(t + 1) * P],
                                          keys[:, NSUB, 2 * t:2 * t + 2, :].rearrange("p n c -> p (n c)"), g.ident)
                    mm.then_inc(turned, 1)
                    following(2)
                    pe.wait_ge(key_t_ready, n + 1)
                    pe.wait_ge(vh_ready, n + 1)
                    for c in range(NCH - 1):
                        half = slice(64 * (c % 2), 64 * (c % 2) + 64)
                        mm = pe.matmul(psum[:, 6 + c % 2, c // 2 * P:(c // 2 + 1) * P], key_t[half, c // 2, :],
                                       vh[half, q, c // 2, :], start=True, stop=True)
                    mm.then_inc(u_ready, 1)
                    following(3)
                    pe.wait_ge(masked, n * 2 + 2)
                    pe.wait_ge(q_ready, n * 2 + 2)
                    for t in range(TT):
                        pe.matmul(psum[:, 5, t * P:(t + 1) * P], vh[:, q, t, :], scores[:, t, :], start=True, stop=False)
                        for c in range(max(2 * t, 1), 2 * t + 2):
                            pe.wait_ge(state_ready, n * 7 + c)
                            mm = pe.matmul(psum[:, 5, c * CHUNK:(c + 1) * CHUNK], state[:, c, :],
                                           q64[:, c * CHUNK:(c + 1) * CHUNK], start=False, stop=c == 2 * t + 1)
                    mm.then_inc(o_ready, 1)
                    pe.wait_ge(squared, n + 1)
                    pe.matmul(psum[:, 4, :], g.ones, sq[:, :], start=True, stop=True).then_inc(sq_summed, 1)

                for m in range(4):
                    gemm(0, 0, m)
                every_head(pe, body)
                for n in range(HH):
                    ring.freed[n0 + n] = (gemm_ready, 4 * (n + 1))

            @block.sync
            def _(sp):
                g.clear_past(sp)
                ring.load_until(sp, n0 + HH + SLOTS)

            @block.gpsimd
            def _(pool):
                pool.memset(keys[:, 0:NSUB, :, :], 0.0).then_inc(zeroed, 1)
                pool.memset(scores[:, :, :], 0.0).then_inc(zeroed, 1)

                def body(n, q, more):
                    pool.wait_ge(head_done, n + 1)
                    pool.tensor_copy(vh[:, q, :, :], vt[:, :, bass.ds(n * P, P)]).then_inc(vh_ready, 1)

                every_head(pool, body)

            @block.scalar
            def _(act):
                act.sem_inc(gemm_took, 4)
                act.wait_ge(lb_ready, 1)
                act.activation(lb[:, :], lb[:, :], ACT.Sigmoid).then_inc(lb_ready, 1)

                def take(n, q, m):
                    if m == 0:
                        act.wait_ge(head_done, n + 1)
                    to, f = ((query[:, q, :], ACT.Silu), (forget[:, q, :], ACT.Sigmoid),
                             (gate[:, q, :], ACT.Silu), (head_of(zu, n), ACT.Gelu))[m]
                    act.wait_ge(gemm_ready, n * 4 + m + 1)
                    act.activation(to, psum[:, m, :], f).then_inc(gemm_took, 1)

                def log_forget(n, q):
                    act.wait_ge(f_ready, n + 1)
                    act.activation(logf[:, :], forget[:, q, :], ACT.Ln).then_inc(ln_ready, 1)

                def decays(n, first=False):
                    for i, (to, of) in enumerate(((e16, cum16), (e64, cum64))):
                        act.wait_ge(cum_ready, n * 2 + i + 1)
                        if i and not first:
                            act.wait_ge(state_ready, n * 7)
                            act.wait_ge(q_ready, n * 2)
                        act.activation(to[:, :], of[:, :], ACT.Exp).then_inc(e_ready, 1)
                    for i in range(NSUB + 1):
                        part = keys[:, i, :, 0:min(SUB * (i + 1), CHUNK)]
                        act.wait_ge(expo_ready, n * 5 + i + 1)
                        act.activation(part, part, ACT.Exp).then_inc(exp_ready, 1)

                def body(n, q, more):
                    if more:
                        take(n + 1, (q + 1) % 2, 0)
                        take(n + 1, (q + 1) % 2, 1)
                    act.wait_ge(turned, n + 1)
                    act.activation(key_t[:, :, :].rearrange("p t k -> p (t k)"), psum[:, 5, :], ACT.Copy).then_inc(key_t_ready, 1)
                    if more:
                        log_forget(n + 1, (q + 1) % 2)
                        take(n + 1, (q + 1) % 2, 2)
                        decays(n + 1)
                        take(n + 1, (q + 1) % 2, 3)
                    act.wait_ge(o_ready, n + 1)
                    act.activation(sq[:, :], psum[:, 5, :], ACT.Square).then_inc(squared, 1)
                    act.wait_ge(sq_summed, n + 1)
                    act.activation(std[:, :], psum[:, 4, :], ACT.Sqrt, scale=1.0 / P, bias=g.eps[EPS_RMS]).then_inc(std_ready, 1)

                take(0, 0, 0)
                take(0, 0, 1)
                log_forget(0, 0)
                take(0, 0, 2)
                take(0, 0, 3)
                decays(0, True)
                every_head(act, body)

            @block.vector
            def _(dve):
                dve.sem_inc(head_done, 2)
                at0, at1 = COLS.at["lb0"], COLS.at["lb1"]
                dve.tensor_tensor(lb[:, :], cols[:, at0:at0 + HH], cols[:, at1:at1 + HH], ALU.subtract).then_inc(lb_ready, 1)
                dve.wait_ge(lb_ready, 2)
                dve.tensor_scalar(one_less[:, :], lb[:, :], -1.0, 1.0, ALU.mult, ALU.add).then_inc(lb_ready, 1)
                dve.wait_ge(lb_ready, 3)
                dve.wait_ge(zeroed, 2)

                def sums(n, q):
                    f = forget[:, q, :]
                    dve.wait_ge(gemm_took, n * 4 + 6)
                    dve.tensor_scalar(f, f, one_less[:, bass.ds(n, 1)], lb[:, bass.ds(n, 1)], ALU.mult, ALU.add)\
                        .then_inc(f_ready, 1)
                    dve.wait_ge(f_ready, n + 1)
                    dve.tensor_scalar(key[:, :], f, -1.0, 1.0, ALU.mult, ALU.add).then_inc(k_ready, 1)
                    dve.wait_ge(ln_ready, n + 1)
                    dve.tensor_tensor_scan(cum16[:, :], g.starts16, logf[:, :], 0.0, ALU.mult, ALU.add).then_inc(cum_ready, 1)
                    dve.tensor_tensor_scan(cum64[:, :], g.starts64, logf[:, :], 0.0, ALU.mult, ALU.add).then_inc(cum_ready, 1)

                def exponents(n, first=False):
                    dve.wait_ge(cum_ready, n * 2 + 2)
                    if not first:
                        dve.wait_ge(turned, n)
                    dve.tensor_scalar(keys[:, 0, :, 0:SUB], c64[:, :, 0:SUB], -1.0, None, ALU.mult).then_inc(expo_ready, 1)
                    for i in range(1, NSUB + 1):
                        w = min(SUB * (i + 1), CHUNK)
                        start = c64[:, :, SUB * i - 1:SUB * i].to_broadcast([P, NCH, w])
                        dve.tensor_tensor(keys[:, i, :, 0:w], start, c64[:, :, 0:w], ALU.subtract).then_inc(expo_ready, 1)

                def decayed(n, q):
                    dve.wait_ge(e_ready, n * 2 + 1)
                    dve.tensor_tensor(q16[:, :], query[:, q, :], e16[:, :], ALU.mult).then_inc(q_ready, 1)
                    dve.wait_ge(k_ready, n + 1)
                    for i in range(NSUB + 1):
                        w = min(SUB * (i + 1), CHUNK)
                        dve.wait_ge(exp_ready, n * 5 + i + 1)
                        part = keys[:, i, :, 0:w]
                        dve.tensor_tensor(part, part, k3[:, :, 0:w], ALU.mult).then_inc(keys_ready, 1)

                def q_to_state(n, q):
                    dve.wait_ge(e_ready, n * 2 + 2)
                    dve.tensor_tensor(q64[:, :], query[:, q, :], e64[:, :], ALU.mult).then_inc(q_ready, 1)

                def body(n, q, more):
                    dve.wait_ge(scored, n + 1)
                    for half in range(2):
                        part = slice(64 * half, 64 * half + 64)
                        dve.tensor_tensor(scores[part, :, 64 * half:64 * half + 64],
                                          psum[part, 4, 0:TT * CHUNK].rearrange("p (t c) -> p t c", c=CHUNK),
                                          g.chunk_upper[part], ALU.mult).then_inc(masked, 1)
                    if more:
                        sums(n + 1, (q + 1) % 2)
                    dve.wait_ge(u_ready, n + 1)
                    for c in range(NCH - 1):
                        update = psum[:, 6 + c % 2, c // 2 * P:(c // 2 + 1) * P]
                        if c == 0:
                            dve.tensor_copy(state[:, 1, :], update).then_inc(state_ready, 1)
                        else:
                            dve.wait_ge(state_ready, n * 7 + c)
                            dve.scalar_tensor_tensor(state[:, c + 1, :], state[:, c, :], e3[:, c, CHUNK - 1:CHUNK], update,
                                                     ALU.mult, ALU.add).then_inc(state_ready, 1)
                    if more:
                        exponents(n + 1)
                        decayed(n + 1, (q + 1) % 2)
                    dve.wait_ge(std_ready, n + 1)
                    dve.reciprocal(rstd[:, :], std[:, :]).then_inc(rstd_ready, 1)
                    dve.wait_ge(rstd_ready, n + 1)
                    out = head_of(ya, n)
                    dve.scalar_tensor_tensor(out, psum[:, 5, :], col("hgrn_norm"), rstd[:, :], ALU.mult, ALU.mult)\
                        .then_inc(normed, 1)
                    dve.wait_ge(normed, n + 1)
                    dve.tensor_tensor(out, out, gate[:, q, :], ALU.mult).then_inc(head_done, 1)
                    if more:
                        q_to_state(n + 1, (q + 1) % 2)

                sums(0, 0)
                exponents(0, True)
                decayed(0, 0)
                q_to_state(0, 0)
                every_head(dve, body)


def gmlp_stage(g, gv, rows, ws, zu):
    nc, ring, psum, col = g.nc, g.ring, g.psum, g.col
    with ExitStack() as own:
        sb = lambda n, shape: own.enter_context(nc.sbuf_tensor(f"gm_{n}", shape, F32))
        sem = g.stage_semaphores("gm")
        stats, mv, std, rstd = sb("stats", [P, TT, 2, 6]), sb("mv", [P, TT, 2]), sb("std", [P, TT]), sb("rstd", [P, TT])
        sv = sb("sv", [P, 2, S])
        rows_in, ws_in, stated, aggregated, std_ready, rstd_ready, step, ws_ready = (sem(n) for n in (
            "rows_in", "ws_in", "stated", "aggregated", "std_ready", "rstd_ready", "step", "ws_ready"))
        mixed, biased, gated = sem("mixed"), sem("biased"), sem("gated")
        with nc.Block(no_gpsimd_drain=True) as block:

            @block.sync
            def _(sp):
                g.clear_past(sp)
                sp.dma_start(rows[:, :, :], g.extra["gmlp_rows"].partition_broadcast(P)).then_inc(rows_in, 16)
                sp.dma_start(ws[:, :, :], g.extra["gmlp_ws"]).then_inc(ws_in, 16)
                ring.load_until(sp, FIRST["w_mix_b"] + SLOTS)

            @block.gpsimd
            def _(pool):
                pool.wait_ge(ws_in, 16)
                ring.wait_split(pool)
                pool.memset(ws[64:128, :, 0:64], 0.0).then_inc(ws_ready, 1)
                pool.wait_ge(ws_ready, 1)
                ring.low_until(pool, FIRST["w_mix_b"] + SLOTS)

            @block.scalar
            def _(act):
                ring.high_until(act, FIRST["w_mix_b"] + 1)
                act.wait_ge(aggregated, TT)
                act.activation(std[:, :], mv[:, :, 1:2].rearrange("p t a -> p (t a)"), ACT.Sqrt, bias=g.eps[EPS_LN])\
                    .then_inc(std_ready, 1)
                ring.high_until(act, FIRST["w_mix_b"] + SLOTS)

            @block.tensor
            def _(pe):
                pe.wait_ge(ws_ready, 1)
                pe.wait_ge(step, 3 * TT)
                for n in range(HH):
                    for t in range(TT):
                        mm = pe.matmul(psum[:, n, t * P:(t + 1) * P], gv[:, t, n * P:(n + 1) * P], ws[:, n, :],
                                       start=True, stop=True)
                    mm.then_inc(mixed, 1)

            @block.vector
            def _(dve):
                for t in range(TT):
                    for c in range(2):
                        dve.bn_stats(stats[:, t, c, :], gv[:, t, c * 512:(c + 1) * 512]).then_inc(stated, 1)
                for t in range(TT):
                    dve.wait_ge(stated, 2 * t + 2)
                    dve.bn_aggr(mv[:, t, :], stats[:, t, :, :].rearrange("p c s -> p (c s)")).then_inc(aggregated, 1)
                dve.wait_ge(std_ready, 1)
                dve.reciprocal(rstd[:, :], std[:, :]).then_inc(rstd_ready, 1)
                dve.wait_ge(rstd_ready, 1)
                dve.wait_ge(aggregated, TT)
                dve.wait_ge(rows_in, 16)
                for t in range(TT):
                    v = gv[:, t, :]
                    dve.tensor_scalar(v, v, mv[:, t, 0:1], rstd[:, t:t + 1], ALU.subtract, ALU.mult).then_inc(step, 1)
                for k, op in ((0, ALU.mult), (1, ALU.add)):
                    for t in range(TT):
                        v = gv[:, t, :]
                        dve.wait_ge(step, TT * (k + 1) - TT + t + 1)
                        dve.tensor_tensor(v, v, rows[:, k, :], op).then_inc(step, 1)
                for n in range(HH):
                    dve.wait_ge(mixed, n + 1)
                    if n >= 2:
                        dve.wait_ge(gated, n - 1)
                    dve.tensor_tensor(sv[:, n % 2, :].rearrange("p (b t) -> p b t", t=P),
                                      psum[:, n, :].rearrange("p (b t) -> p b t", t=P),
                                      rows[:, 2:3, n * P:(n + 1) * P].to_broadcast([P, TT, P]), ALU.add).then_inc(biased, 1)
                    dve.wait_ge(biased, n + 1)
                    dve.tensor_tensor(zu[:, n, :], zu[:, n, :], sv[:, n % 2, :], ALU.mult).then_inc(gated, 1)


def mix_stage(g, name, panels_at, to_split, y, u, out, bias, add):
    nc, ring, psum, col = g.nc, g.ring, g.psum, g.col
    with ExitStack() as own:
        sem = g.stage_semaphores(name)
        gate = own.enter_context(nc.sbuf_tensor(f"{name}_gate", [P, 4, S], F32))
        tile_ready, gate_ready, gated, done = sem("tile_ready"), sem("gate_ready"), sem("gated"), sem("done")
        high_ready, low_ready = sem("high_ready"), sem("low_ready")
        n0 = FIRST[panels_at]
        with nc.Block(no_gpsimd_drain=True) as block:

            @block.tensor
            def _(pe):
                for p in range(4):
                    for m in range(4):
                        if p >= 2:
                            pe.wait_ge(done, 4 * (p // 2 - 1) + m + 1)
                        for k in range(KT):
                            if m == 0:
                                ring.wait_part(pe, n0 + p, k)
                                if p < len(to_split):
                                    pe.wait_ge(low_ready, DT * p + k + 1)
                            mm = split_product(pe, psum[:, 4 * (p % 2) + m, :], ring.halves(n0 + p, k, m * P, P),
                                               tile_halves(*(u if p % 2 else y), k), k == 0, k == KT - 1)
                        mm.then_inc(tile_ready, 1)
                    ring.freed[n0 + p] = (tile_ready, 4 * (p + 1))

            @block.sync
            def _(sp):
                g.clear_past(sp)
                ring.load_until(sp, n0 + 4 + SLOTS)

            @block.scalar
            def _(act):
                for i, (full, (high, _)) in enumerate(to_split):
                    for t in range(DT):
                        act.activation(tile_of(high, t), tile_of(full, t), ACT.Copy).then_inc(high_ready, 1)
                    if i == 0:
                        ring.high_until(act, n0 + 1)
                for t in range(DT):
                    if t % 4 == 0:
                        ring.high_until(act, n0 + t // 2 + SLOTS)
                        if t == 0:
                            ring.high_until(act, n0 + 3)
                    act.wait_ge(tile_ready, 8 * (t // 4) + 4 + t % 4 + 1)
                    if t >= 4:
                        act.wait_ge(done, t - 3)
                    act.activation(gate[:, t % 4, :], psum[:, 4 + t % 4, :], ACT.Sigmoid, bias=bias(t)).then_inc(gate_ready, 1)
                    if t == 3:
                        ring.high_until(act, n0 + 4)
                        ring.high_until(act, n0 + 5)

            @block.gpsimd
            def _(pool):
                ring.low_until(pool, n0 + 5)

            @block.vector
            def _(dve):
                for i, (full, (high, low)) in enumerate(to_split):
                    for t in range(DT):
                        dve.wait_ge(high_ready, DT * i + t + 1)
                        dve.tensor_tensor(tile_of(low, t), tile_of(full, t), tile_of(high, t).bitcast(F32), ALU.subtract)\
                            .then_inc(low_ready, 1)
                for t in range(DT):
                    dve.wait_ge(gate_ready, t + 1)
                    gt, y_bank = gate[:, t % 4, :], psum[:, t % 4, :]
                    if not add:
                        dve.tensor_tensor(out[:, t, :], gt, y_bank, ALU.mult).then_inc(done, 1)
                    else:
                        dve.tensor_tensor(gt, gt, y_bank, ALU.mult).then_inc(gated, 1)
                        dve.wait_ge(gated, t + 1)
                        dve.tensor_tensor(out[:, t, :], out[:, t, :], gt, ALU.add).then_inc(done, 1)


def block_2(g, x, h):
    nc, ring, psum, col = g.nc, g.ring, g.psum, g.col
    with ExitStack() as own:
        mod = g.mod
        m = lambda part, t: mod[:, part * DT + t:part * DT + t + 1]
        gated = lambda part: lambda t: (lambda e, bank: e.scalar_tensor_tensor(
            x[:, t, :], bank, m(part, t), x[:, t, :], ALU.mult, ALU.add))
        norm_stage(g, "n4", x, h, lambda t: m(1, t), EPS_LN, g.ones_mean, bias=lambda t: m(0, t), centre=True)
        with ExitStack() as two:
            zu, zu_low = with_low(nc, two, "zu", [P, DT, S])
            ya, ya_at = placed(nc, two, "ya", [P, DT, S], F32)
            ya_low = nc.alloc_sbuf_tensor_at("ya_low", [P, DT, S], F32R, offset=ya_at)

            def token_tiles(name, to, func, halves):
                return [Tile([FIRST[name] + c], 0, PANEL, h, None, "act",
                             (lambda out: lambda a, bank: a.activation(out, bank, func))(to[:, t, c * PANEL:(c + 1) * PANEL]),
                             tokens=t, halves=halves) for c in range(2) for t in range(TT)]

            with nc.sbuf_tensor("vt", [P, TT, D], F32) as vt:
                dense_stage(g, "zi", token_tiles("w_zi", vt, ACT.Copy, None), FIRST["w_head"] + SLOTS)
                hgrn_stage(g, h, vt, zu, ya)
            merged = two.enter_context(nc.sbuf_tensor("merged", [P, DT, S], F32))
            with ExitStack() as own2:
                high = g.open_split(own2, "mix")
                y_high, y_high_at = placed(nc, own2, "y_high", [P, DT, S], F32R)
                halves = (high, g.h_low)
                y = (y_high, ya_low)
                mix_stage(g, "mixa", "w_mix_a", [(ya, y), (h, halves)], y, halves, merged, lambda t: col("b_gate", t), False)
                gv = nc.alloc_sbuf_tensor_at("gv", [P, TT, D], F32, offset=ya_at)
                rows = nc.alloc_sbuf_tensor_at("gmlp_rows_on_chip", [P, 3, D], F32, offset=y_high_at)
                ws = nc.alloc_sbuf_tensor_at("gmlp_ws_on_chip", [P, HH, P], F32, offset=y_high_at + 12 * D)
                dense_stage(g, "zv", token_tiles("w_zv", gv, ACT.Gelu, halves), FIRST["w_mix_b"] + SLOTS,
                            split_to=FIRST["w_mix_b"] + 1)
                gmlp_stage(g, gv, rows, ws, zu)
                zu_high = nc.alloc_sbuf_tensor_at("zu_high", [P, DT, S], F32R, offset=y_high_at)
                y = (zu_high, zu_low)
                mix_stage(g, "mixb", "w_mix_b", [(zu, y)], y, halves, merged, lambda t: col("b_gate", DT + t), True)
            n0 = FIRST["w_out_2"]
            dense_stage(g, "out2", [Tile([n0 + t // 4], t % 4 * P, P, merged, None, "dve", gated(2)(t))
                                    for t in range(DT)], n0 + 2 + SLOTS, scale_x=x)
        norm_stage(g, "n5", x, x, lambda t: col("ln1_w2", t), EPS_LN, g.ones_mean, bias=lambda t: col("ln1_b2", t), centre=True)
        with ExitStack() as ffn:
            high = g.open_split(ffn, "ff2")
            norm_stage(g, "n6", x, h, lambda t: m(4, t), EPS_LN, g.ones_mean, bias=lambda t: m(3, t), centre=True,
                       high=high, low=g.h_low, split_to=FIRST["w_ffn_in"] + SLOTS)
            mid, mid_low = with_low(nc, ffn, "mid2", [P, FT, S])
            feed_forward(g, "ff2", high, g.h_low, mid, mid_low, 0, "w_ffn_in", "w_ffn_out", gated(5), False, scale_x=x)
        norm_stage(g, "n7", x, x, lambda t: col("ln2_w2", t), EPS_LN, g.ones_mean, bias=lambda t: col("ln2_b2", t), centre=True)


def mixer_stage(g, x, mixed):
    nc, ring, psum, cols, col = g.nc, g.ring, g.psum, g.cols, g.col
    PAD = max(WINDOWS)
    n0 = FIRST["w_in_3"]
    with ExitStack() as own:
        sb = lambda n, shape: own.enter_context(nc.sbuf_tensor(f"mx_{n}", shape, F32))
        sem = g.stage_semaphores("mx")
        factor, u, diff = sb("factor", [P, 2, S]), sb("u", [P, S]), sb("diff", [P, 2, S])
        values, sums = sb("values", [P, 2, PAD + S]), sb("sums", [P, 2, PAD + S])
        pool_mix = sb("pool_mix", [P, 4, P])
        tile_ready, copied, conv_done, diff_ready, pooled, scaled, step, mix_in = (sem(n) for n in (
            "tile_ready", "copied", "conv_done", "diff_ready", "pooled", "scaled", "step", "mix_in"))
        with nc.Block(no_gpsimd_drain=True) as block:

            @block.tensor
            def _(pe):
                def pool(j):
                    pe.wait_ge(diff_ready, j + 1)
                    pe.matmul(psum[:, 4 * (j % 2) + 3, :], pool_mix[:, j, :], diff[:, j % 2, :], start=True, stop=True)\
                        .then_inc(pooled, 1)

                pe.wait_ge(mix_in, 16)
                for j in range(4):
                    if j >= 2:
                        pe.wait_ge(conv_done, j - 1)
                        pe.wait_ge(scaled, j - 1)
                    ring.wait_landed(pe, n0 + j)
                    for m in range(4):
                        for k in range(KT):
                            mm = pe.matmul(psum[:, 4 * (j % 2) + m, :], ring.weights(n0 + j, k, m * P, P), tile_of(x, k),
                                           start=k == 0, stop=k == KT - 1)
                        mm.then_inc(tile_ready, 1)
                    ring.freed[n0 + j] = (tile_ready, 4 * (j + 1))
                    if j >= 1:
                        pool(j - 1)
                pool(3)

            @block.sync
            def _(sp):
                g.clear_past(sp)
                sp.dma_start(pool_mix[:, :, :], g.extra["pool_mix"]).then_inc(mix_in, 16)
                ring.load_until(sp, min(n0 + 4 + SLOTS, FIRST["ple_proj"]))

            @block.scalar
            def _(act):
                for j in range(4):
                    act.wait_ge(tile_ready, 4 * j + 2)
                    if j >= 2:
                        act.wait_ge(conv_done, j - 1)
                        act.wait_ge(diff_ready, j - 1)
                    act.activation(factor[:, j % 2, :], psum[:, 4 * (j % 2) + 1, :], ACT.Copy).then_inc(copied, 1)
                    act.wait_ge(tile_ready, 4 * j + 4)
                    act.activation(values[:, j % 2, PAD:], psum[:, 4 * (j % 2) + 3, :], ACT.Copy).then_inc(copied, 1)
                    if j >= 1:
                        act.wait_ge(pooled, j)
                        act.activation(mixed[:, j - 1, :], psum[:, 4 * ((j - 1) % 2) + 3, :], ACT.Copy,
                                       scale=col("pool_scale", j - 1)).then_inc(scaled, 1)
                act.wait_ge(pooled, 4)
                act.activation(mixed[:, 3, :], psum[:, 7, :], ACT.Copy, scale=col("pool_scale", 3)).then_inc(scaled, 1)

            @block.vector
            def _(dve):
                steps = [0]

                def link(ins):
                    steps[0] += 1
                    ins.then_inc(step, 1)
                    dve.wait_ge(step, steps[0])

                link(dve.memset(values[:, :, 0:PAD], 0.0))
                link(dve.memset(sums[:, :, 0:PAD], 0.0))
                for j in range(4):
                    bank = lambda m: psum[:, 4 * (j % 2) + m, :]
                    out = mixed[:, 4 + j, :]
                    tap = lambda k: col("conv_w3", 4 * k + j)
                    dve.wait_ge(copied, 2 * j + 1)
                    dve.wait_ge(tile_ready, 4 * j + 3)
                    link(dve.tensor_tensor(u[:, :], factor[:, j % 2, :], bank(2), ALU.mult))
                    link(dve.tensor_scalar(out, u[:, :], tap(2), None, ALU.mult))
                    for k in (1, 0):
                        back = 2 - k
                        link(dve.scalar_tensor_tensor(out[:, back:], u[:, 0:S - back], tap(k), out[:, back:],
                                                      ALU.mult, ALU.add))
                    dve.tensor_tensor(out, out, bank(0), ALU.mult).then_inc(conv_done, 1)
                    dve.wait_ge(copied, 2 * j + 2)
                    of, width, b = values[:, j % 2, :], 1, 0
                    while width < WINDOWS[j]:
                        to = sums[:, b, :]
                        link(dve.tensor_tensor(to[:, PAD:], of[:, PAD:], of[:, PAD - width:PAD + S - width], ALU.add))
                        of, width, b = to, 2 * width, 1 - b
                    d, v = diff[:, j % 2, :], values[:, j % 2, PAD:]
                    if j >= 2:
                        dve.wait_ge(pooled, j - 1)
                    at = CONST.at["pool_inv"] + 16 * j
                    link(dve.tensor_tensor(d[:, 0:16], of[:, PAD:PAD + 16], g.const("pool_inv", 64)[:, 16 * j:16 * j + 16], ALU.mult))
                    link(dve.tensor_tensor(d[:, 0:16], d[:, 0:16], v[:, 0:16], ALU.subtract))
                    dve.scalar_tensor_tensor(d[:, 16:], of[:, PAD + 16:], 1.0 / WINDOWS[j], v[:, 16:],
                                             ALU.mult, ALU.subtract).then_inc(diff_ready, 1)


def route_stage(g, x, r):
    nc, ring, psum, cols = g.nc, g.ring, g.psum, g.cols
    with ExitStack() as own:
        sb = lambda n, shape, dt=F32: own.enter_context(nc.sbuf_tensor(f"rt_{n}", shape, dt))
        sem = g.stage_semaphores("rt")
        x_tok = sb("x_tok", [P, TT, D])
        rw, rb = sb("rw", [P, DT, NE]), sb("rb", [P, NE])
        logits, left = sb("logits", [P, TT, NE + 4]), sb("left", [P, TT, NE + 4])
        best, take = sb("best", [P, TT, 8]), sb("take", [P, TT, 8])
        neg_top, chosen, e_sel, total, inv = (sb("neg_top", [P, TT]), sb("chosen", [P, TT, NE]), sb("e_sel", [P, TT, NE]),
                                              sb("total", [P, TT]), sb("inv", [P, TT]))
        rank, over, row, dest, addr = (sb(n, [P, TT, NE]) for n in ("rank", "over", "row", "dest", "addr"))
        count, blocks, upto, first, part, ones_e = (sb(n, [P, NE]) for n in ("count", "blocks", "upto", "first", "part", "ones_e"))
        top_dest, top_addr = sb("top_dest", [P, TT, 8]), sb("top_addr", [P, TT, 8])
        hit = sb("hit", [P, TT, NE])
        token = sb("token", [P, TT], I32)
        addr_i = sb("addr_i", [P, TT, TOPE], U32)
        seen, block_of = sb("seen", [1, TABLE, NE]), sb("block_of", [1, TABLE])
        zero = sb("zero", [P, TABLE], I32)
        in_done, turned, turned_out, x_stored, logit_ready, exp_ready, ranked, zeroed, table_zero, id_ready = (sem(n) for n in (
            "in_done", "turned", "turned_out", "x_stored", "logit_ready", "exp_ready", "ranked", "zeroed", "table_zero", "id_ready"))
        step, gates_ready, addr_ready, scattered, table_in, chosen_ready, top_ready, counts_ready = (sem(n) for n in (
            "step", "gates_ready", "addr_ready", "scattered", "table_in", "chosen_ready", "top_ready", "counts_ready"))
        with nc.Block(no_gpsimd_drain=True) as block:

            @block.sync
            def _(sp):
                g.clear_past(sp)
                sp.dma_start(rw[:, :, :], g.extra["router_w"]).then_inc(in_done, 16)
                sp.dma_start(rb[:, :], g.extra["router_b"][0:1, :].partition_broadcast(P)).then_inc(in_done, 16)
                sp.wait_ge(zeroed, 1)
                sp.dma_start(r.table_dram.rearrange("(s b) a -> s (b a)", s=P), zero[:, :]).then_inc(table_zero, 16)
                sp.wait_ge(turned_out, 8)
                sp.dma_start(r.x_dram.rearrange("(t p) d -> p t d", p=P), x_tok[:, :, :]).then_inc(x_stored, 16)
                sp.wait_ge(x_stored, 16)
                sp.wait_ge(scattered, 16 * TT * TOPE)
                sp.dma_start(r.table[:, :], r.table_dram.rearrange("(s b) a -> s (b a)", s=P)).then_inc(table_in, 16)
                sp.wait_ge(table_in, 16)

            @block.tensor
            def _(pe):
                for t in range(TT):
                    for c in range(2):
                        n = 2 * t + c
                        if n >= 6:
                            pe.wait_ge(turned_out, n - 5)
                        for k in range(4):
                            mm = pe.transpose(psum[:, n % 6, k * P:(k + 1) * P], x[:, 4 * c + k, t * P:(t + 1) * P], g.ident)
                        mm.then_inc(turned, 1)
                pe.wait_ge(in_done, 32)
                for t in range(TT):
                    for k in range(DT):
                        mm = pe.matmul(psum[:, 6, t * NE:(t + 1) * NE], x[:, k, t * P:(t + 1) * P], rw[:, k, :],
                                       start=k == 0, stop=k == DT - 1)
                mm.then_inc(logit_ready, 1)
                pe.wait_ge(chosen_ready, TT)
                for t in range(TT):
                    for b in range(t):
                        pe.matmul(psum[:, 7, t * NE:(t + 1) * NE], g.ones, chosen[:, b, :], start=b == 0, stop=False)
                    pe.matmul(psum[:, 7, t * NE:(t + 1) * NE], g.before, chosen[:, t, :], start=t == 0, stop=True)
                for t in range(TT):
                    mm = pe.matmul(psum[:, 7, TT * NE:(TT + 1) * NE], g.ones, chosen[:, t, :], start=t == 0, stop=t == TT - 1)
                mm.then_inc(ranked, 1)

            @block.gpsimd
            def _(pool):
                pool.memset(zero[:, :], 0).then_inc(zeroed, 1)
                pool.iota(token[:, :], pattern=[[P, TT]], base=0, channel_multiplier=1).then_inc(id_ready, 1)
                pool.wait_ge(id_ready, 1)
                pool.wait_ge(table_zero, 16)
                pool.wait_ge(addr_ready, 1)
                for t in range(TT):
                    for j in range(TOPE):
                        pool.indirect_dma_start(r.table_dram, bass.IndirectOffsetOnAxis(addr_i[:, t, j:j + 1], 0),
                                                token[:, t:t + 1], None).then_inc(scattered, 16)

            @block.scalar
            def _(act):
                for n in range(2 * TT):
                    t, c = divmod(n, 2)
                    act.wait_ge(turned, n + 1)
                    act.activation(x_tok[:, t, c * 512:(c + 1) * 512], psum[:, n % 6, :], ACT.Copy).then_inc(turned_out, 1)
                for t in range(TT):
                    act.wait_ge(top_ready, TT + 1)
                    act.activation(e_sel[:, t, :], logits[:, t, 0:NE], ACT.Exp, bias=neg_top[:, t:t + 1]).then_inc(exp_ready, 1)

            @block.vector
            def _(dve):
                steps = [0]

                def link(ins):
                    steps[0] += 1
                    ins.then_inc(step, 1)
                    dve.wait_ge(step, steps[0])

                link(dve.memset(logits[:, :, NE:], ACAUSAL))
                link(dve.memset(take[:, :, :], ACAUSAL))
                link(dve.memset(ones_e[:, :], 1.0))
                dve.wait_ge(in_done, 32)
                dve.wait_ge(logit_ready, 1)
                link(dve.tensor_tensor(logits[:, :, 0:NE], psum[:, 6, 0:TT * NE].rearrange("p (t e) -> p t e", e=NE),
                                       rb[:, :].rearrange("p (a e) -> p a e", a=1).to_broadcast([P, TT, NE]), ALU.add))
                for t in range(TT):
                    dve.max(best[:, t, :], logits[:, t, 0:NE]).then_inc(top_ready, 1)
                dve.wait_ge(top_ready, TT)
                dve.tensor_scalar(neg_top[:, :], best[:, :, 0:1].rearrange("p t a -> p (t a)"), -1.0, None, ALU.mult)\
                    .then_inc(top_ready, 1)
                link(dve.tensor_copy(take[:, :, 0:TOPE], best[:, :, 0:TOPE]))
                for t in range(TT):
                    link(dve.match_replace(left[:, t, :], take[:, t, :], logits[:, t, :], TAKEN))
                    dve.tensor_scalar(chosen[:, t, :], left[:, t, 0:NE], TAKEN, None, ALU.is_equal).then_inc(chosen_ready, 1)
                dve.wait_ge(chosen_ready, TT)
                dve.wait_ge(exp_ready, TT)
                link(dve.tensor_tensor(e_sel[:, :, :], e_sel[:, :, :], chosen[:, :, :], ALU.mult))
                link(dve.tensor_reduce(total[:, :], e_sel[:, :, :], AX_X, ALU.add))
                link(dve.reciprocal(inv[:, :], total[:, :]))
                dve.wait_ge(ranked, 1)
                link(dve.tensor_copy(rank[:, :, :], psum[:, 7, 0:TT * NE].rearrange("p (t e) -> p t e", e=NE)))
                link(dve.tensor_copy(count[:, :], psum[:, 7, TT * NE:(TT + 1) * NE]))
                link(dve.tensor_scalar(over[:, :, :], rank[:, :, :], float(ROWS), None, ALU.is_ge))
                link(dve.tensor_scalar(blocks[:, :], count[:, :], 0.0, None, ALU.is_gt))
                for n in range(1, S // ROWS):
                    link(dve.scalar_tensor_tensor(blocks[:, :], count[:, :], float(n * ROWS), blocks[:, :], ALU.is_gt, ALU.add))
                    if n > 1:
                        link(dve.scalar_tensor_tensor(over[:, :, :], rank[:, :, :], float(n * ROWS), over[:, :, :],
                                                      ALU.is_ge, ALU.add))
                link(dve.scalar_tensor_tensor(row[:, :, :], over[:, :, :], -float(ROWS), rank[:, :, :], ALU.mult, ALU.add))
                link(dve.tensor_tensor_scan(upto[:, :], ones_e[:, :], blocks[:, :], 0.0, ALU.mult, ALU.add))
                link(dve.tensor_tensor(first[:, :], upto[:, :], blocks[:, :], ALU.subtract))
                link(dve.tensor_tensor(over[:, :, :], over[:, :, :],
                                       first[:, :].rearrange("p (a e) -> p a e", a=1).to_broadcast([P, TT, NE]), ALU.add))
                link(dve.scalar_tensor_tensor(dest[:, :, :], over[:, :, :], float(ROWS), row[:, :, :], ALU.mult, ALU.add))
                link(dve.scalar_tensor_tensor(addr[:, :, :], row[:, :, :], float(TABLE), over[:, :, :], ALU.mult, ALU.add))
                for v in (dest, addr):
                    link(dve.scalar_tensor_tensor(v[:, :, :], v[:, :, :], 1.0, chosen[:, :, :], ALU.add, ALU.mult))
                for t in range(TT):
                    link(dve.max(top_dest[:, t, :], dest[:, t, :]))
                    link(dve.max(top_addr[:, t, :], addr[:, t, :]))
                dve.tensor_scalar(addr_i[:, :, :], top_addr[:, :, 0:TOPE], -1.0, None, ALU.add).then_inc(addr_ready, 1)
                link(dve.tensor_scalar(r.dest[:, :, :], top_dest[:, :, 0:TOPE], float(ROWS - 1), None, ALU.add))
                for t in range(TT):
                    for j in range(TOPE):
                        link(dve.scalar_tensor_tensor(hit[:, t, :], dest[:, t, :], top_dest[:, t, j:j + 1], e_sel[:, t, :],
                                                      ALU.is_equal, ALU.mult, accum_out=r.gates[:, t, j:j + 1]))
                    link(dve.tensor_scalar(r.gates[:, t, :], r.gates[:, t, :], inv[:, t:t + 1], None, ALU.mult))
                link(dve.tensor_tensor(seen[:, :, :], upto[0:1, :].rearrange("p (a e) -> p a e", a=1).to_broadcast([1, TABLE, NE]),
                                       g.block_iota.rearrange("p (b a) -> p b a", a=1).to_broadcast([1, TABLE, NE]), ALU.is_le))
                link(dve.tensor_reduce(block_of[:, :], seen[:, :, :], AX_X, ALU.add))
                link(dve.tensor_scalar(r.expert[:, :], block_of[:, :], float(NE - 1), None, ALU.min))
                link(dve.tensor_copy(r.n_blocks[:, :], upto[0:1, NE - 1:NE]))


def expert_stage(g, r):
    nc, psum = g.nc, g.psum
    with ExitStack() as own:
        sb = lambda n, shape, dt=F32: own.enter_context(nc.sbuf_tensor(f"ex_{n}", shape, dt))
        sem = g.stage_semaphores("ex")
        more, more_low = with_low(nc, own, "ex_more", [P, 4, KT * PANEL])
        high = own.enter_context(nc.sbuf_tensor("ex_high", [P, KT * PANEL], F32R))
        rows_high, rows_low = (own.enter_context(nc.sbuf_tensor(f"ex_{n}", [P, DT, P], F32R)) for n in ("rows_high", "rows_low"))
        low = {1: g.ring.low[:, 1, :], 3: more_low[:, 3 - SLOTS, :]}
        part_of = lambda c: slice(c * KT * PANEL // PARTS, (c + 1) * KT * PANEL // PARTS)
        piece = lambda s: g.ring.tile[:, s, :] if s < SLOTS else more[:, s - SLOTS, :]
        weights = lambda s, k: piece(s)[:, k * PANEL:(k + 1) * PANEL]
        rows, rows_t = sb("rows", [P, D]), sb("rows_t", [P, DT, P])
        bias_row, bias_up, bias_down = r.bias_row, sb("bias_up", [P, 2 * D]), sb("bias_down", [P, D])
        gate, up, sig = sb("gate", [P, 512]), sb("up", [P, 512]), sb("sig", [P, 512])
        act_rows, act_t, y = sb("act_rows", [P, 2, 512]), sb("act_t", [P, DT, P]), sb("y", [P, D])
        index = sb("index", [P, 1], U32)
        landed = [sem(f"landed{s}") for s in range(6)]
        gu_ready, dn_ready, rows_in, index_ready, x_turned, x_ready, bias_in, up_spread, down_spread = (sem(n) for n in (
            "gu_ready", "dn_ready", "rows_in", "index_ready", "x_turned", "x_ready", "bias_in", "up_spread", "down_spread"))
        taken, limited, sig_ready, product, h_done, h_turned, h_ready, y_done, y_out = (sem(n) for n in (
            "taken", "limited", "sig_ready", "product", "h_done", "h_turned", "h_ready", "y_done", "y_out"))

        high_ready, x_high, x_low = sem("high_ready"), sem("x_high"), sem("x_low")
        low_ready = [sem("low_ready1"), sem("low_ready3")]
        blank, blank_out = sem("blank"), sem("blank_out")
        passed = sem("passed")
        def blocks_of(eng):
            return eng.value_load(r.n_blocks[0:1, 0:1], min_val=1, max_val=NBLK)

        def low_piece(e, b, turn):
            no = 2 * turn + 1
            for c in range(PARTS):
                e.wait_ge(high_ready, b * (2 * PARTS) + turn * PARTS + c + 1)
                at = part_of(c)
                e.tensor_tensor(low[no][:, at], piece(no)[:, at], high[:, at].bitcast(F32), ALU.subtract)\
                    .then_inc(low_ready[turn], 1)

        with nc.Block(no_gpsimd_drain=True) as block:

            @block.sync
            def _(sp):
                g.clear_past(sp)
                n_blocks = blocks_of(sp)
                with sp.Fori(0, n_blocks) as b:
                    e = sp.value_load(r.expert[0:1, bass.ds(b, 1)], min_val=0, max_val=NE - 1)
                    for s in range(6):
                        if s < 4:
                            sp.wait_ge(gu_ready, b * 4 + s + 1)
                        else:
                            sp.wait_ge(dn_ready, b * 2 + s - 3)
                        sp.dma_start(piece(s), g.extra["moe_w"][bass.ds(e * 6 + s, 1), :, :].rearrange("a p f -> (a p) f"))\
                            .then_inc(landed[s], 16)
                        if s == 3:
                            sp.wait_ge(down_spread, b + 1)
                            sp.dma_start(bias_row[:, :], g.extra["moe_b"][bass.ds(e, 1), :]).then_inc(bias_in, 16)
                    sp.wait_ge(y_done, b * 2 + 2)
                    sp.dma_start(r.y_dram[bass.ds(b * ROWS, ROWS), :], y[:, :]).then_inc(y_out, 16)
                sp.wait_ge(y_done, n_blocks * 2 + 2)
                sp.dma_start(r.y_dram[bass.ds(n_blocks * ROWS, ROWS), :], y[:, :]).then_inc(y_out, 16)
                sp.wait_ge(y_out, n_blocks * 16 + 16)
                sp.sem_inc(passed, 1)

            @block.gpsimd
            def _(pool):
                pool.sem_inc(down_spread, 1)
                pool.memset(r.scratch, 0.0).then_inc(blank, 1)

                def gather(b):
                    pool.tensor_copy(index[:, :], r.table[:, bass.ds(b, 1)]).then_inc(index_ready, 1)
                    pool.wait_ge(index_ready, b + 1)
                    pool.sem_inc(passed, 1)
                    pool.indirect_dma_start(rows[:, :], None, r.x_dram, bass.IndirectOffsetOnAxis(index[:, 0:1], 0))\
                        .then_inc(rows_in, 16)

                gather(0)
                with pool.Fori(0, blocks_of(pool)) as b:
                    low_piece(pool, b, 0)
                    pool.wait_ge(rows_in, b * 16 + 16)
                    pool.wait_ge(x_turned, b * 2 + 2)
                    gather(b + 1)
                    pool.wait_ge(bias_in, b * 16 + 16)
                    pool.wait_ge(h_done, b * 2 + 2)
                    pool.wait_ge(low_ready[0], b * PARTS + PARTS)
                    pool.sem_inc(passed, 1)
                    pool.partition_broadcast(bias_up[:, :], bias_row[:, 0:2 * D]).then_inc(up_spread, 1)
                    pool.wait_ge(up_spread, b + 1)
                    pool.wait_ge(y_done, b * 2 + 2)
                    pool.sem_inc(passed, 1)
                    pool.partition_broadcast(bias_down[:, :], bias_row[:, 2 * D:]).then_inc(down_spread, 1)

            @block.tensor
            def _(pe):
                pe.sem_inc(gu_ready, 4)
                pe.sem_inc(dn_ready, 2)

                def turn_rows(c):
                    for k in range(4):
                        mm = pe.transpose(psum[:, 5, k * P:(k + 1) * P], rows[:, (4 * c + k) * P:(4 * c + k + 1) * P], g.ident)
                    mm.then_inc(x_turned, 1)

                def turn_act(c):
                    for k in range(4):
                        mm = pe.transpose(psum[:, 4, k * P:(k + 1) * P], act_rows[:, c, k * P:(k + 1) * P], g.ident)
                    mm.then_inc(h_turned, 1)

                pe.wait_ge(rows_in, 16)
                turn_rows(0)
                pe.wait_ge(x_ready, 1)
                turn_rows(1)
                with pe.Fori(0, blocks_of(pe)) as b:
                    pe.wait_ge(x_ready, b * 2 + 2)
                    for s in range(4):
                        pe.wait_ge(landed[s], b * 16 + 16)
                        pe.wait_ge(taken, b * 4 + s + 1)
                        if s == 1:
                            pe.wait_ge(x_low, b + 1)
                        for k in range(KT):
                            if s % 2 == 0:
                                mm = pe.matmul(psum[:, s, :], rows_t[:, k, :], weights(s, k), start=k == 0, stop=k == KT - 1)
                            else:
                                if k % (KT // PARTS) == 0:
                                    pe.wait_ge(low_ready[s // 2], b * PARTS + k // (KT // PARTS) + 1)
                                at = slice(k * PANEL, (k + 1) * PANEL)
                                mm = split_product(pe, psum[:, s, :], (rows_high[:, k, :], rows_low[:, k, :]),
                                                   (high[:, at], low[s][:, at]), k == 0, k == KT - 1)
                        mm.then_inc(gu_ready, 1)
                    pe.wait_ge(h_done, b * 2 + 3)
                    turn_act(0)
                    pe.wait_ge(rows_in, b * 16 + 32)
                    turn_rows(0)
                    pe.wait_ge(y_done, b * 2 + 2)
                    for c in range(2):
                        pe.wait_ge(h_ready, b * 2 + c + 1)
                        if c:
                            pe.wait_ge(x_ready, b * 2 + 3)
                            turn_rows(1)
                        for s in range(2):
                            if c == 0:
                                pe.wait_ge(landed[4 + s], b * 16 + 16)
                            for k in range(4 * c, 4 * c + 4):
                                mm = pe.matmul(psum[:, 6 + s, :], act_t[:, k, :], weights(4 + s, k),
                                               start=k == 0, stop=k == KT - 1)
                            if c:
                                mm.then_inc(dn_ready, 1)
                        if c == 0:
                            pe.wait_ge(h_done, b * 2 + 4)
                            turn_act(1)

            @block.scalar
            def _(act):
                n_blocks = blocks_of(act)
                act.wait_ge(blank, 1)
                with act.Fori(n_blocks, TABLE) as b:
                    act.dma_start(r.y_dram[bass.ds(b * ROWS + ROWS, ROWS), :], r.scratch).then_inc(blank_out, 16)

                def take_rows(c):
                    for to, signal in ((rows_high, x_high), (rows_t, x_ready)):
                        act.activation(to[:, 4 * c:4 * c + 4, :].rearrange("p k s -> p (k s)"), psum[:, 5, :], ACT.Copy)\
                            .then_inc(signal, 1)

                def high_piece(b, piece_no):
                    act.wait_ge(landed[piece_no], b * 16 + 16)
                    for c in range(PARTS):
                        act.activation(high[:, part_of(c)], piece(piece_no)[:, part_of(c)], ACT.Copy).then_inc(high_ready, 1)

                def take_act(c):
                    act.activation(act_t[:, 4 * c:4 * c + 4, :].rearrange("p k s -> p (k s)"), psum[:, 4, :], ACT.Copy)\
                        .then_inc(h_ready, 1)

                for c in range(2):
                    act.wait_ge(x_turned, c + 1)
                    take_rows(c)
                with act.Fori(0, n_blocks) as b:
                    act.sem_inc(blank_out, 16)
                    act.wait_ge(gu_ready, b * 4 + 4)
                    high_piece(b, 1)
                    act.wait_ge(gu_ready, b * 4 + 6)
                    high_piece(b, 3)
                    for c in range(2):
                        act.wait_ge(limited, b * 2 + c + 1)
                        act.wait_ge(h_done, b * 2 + c + 2)
                        act.activation(sig[:, :], gate[:, :], ACT.Sigmoid, scale=SW_ALPHA).then_inc(sig_ready, 1)
                    act.wait_ge(h_turned, b * 2 + 1)
                    take_act(0)
                    act.wait_ge(x_turned, b * 2 + 3)
                    take_rows(0)
                    act.wait_ge(h_turned, b * 2 + 2)
                    take_act(1)
                    act.wait_ge(x_turned, b * 2 + 4)
                    take_rows(1)
                act.wait_ge(blank_out, 16 * TABLE)

            @block.vector
            def _(dve):
                dve.sem_inc(taken, 4)
                dve.sem_inc(h_done, 2)
                dve.memset(y[:, :], 0.0).then_inc(y_done, 2)

                def low_rows(more):
                    dve.wait_ge(x_high, more + 2)
                    dve.wait_ge(x_ready, more + 2)
                    dve.tensor_tensor(rows_low[:, :, :], rows_t[:, :, :], rows_high[:, :, :].bitcast(F32), ALU.subtract)\
                        .then_inc(x_low, 1)

                low_rows(0)
                with dve.Fori(0, blocks_of(dve)) as b:
                    low_piece(dve, b, 1)
                    dve.wait_ge(up_spread, b + 1)
                    for c in range(2):
                        part = slice(512 * c, 512 * c + 512)
                        for m, to in ((2 * c, gate), (2 * c + 1, up)):
                            dve.wait_ge(gu_ready, b * 4 + m + 5)
                            at = D * (m % 2) + 512 * c
                            dve.tensor_tensor(to[:, :], psum[:, m, :], bias_up[:, at:at + 512], ALU.add).then_inc(taken, 1)
                            dve.wait_ge(taken, b * 4 + m + 5)
                            if m % 2 == 0:
                                dve.tensor_scalar(to[:, :], to[:, :], SW_LIMIT, None, ALU.min).then_inc(limited, 1)
                            else:
                                dve.tensor_scalar(to[:, :], to[:, :], SW_LIMIT, -SW_LIMIT, ALU.min, ALU.max)\
                                    .then_inc(product, 1)
                        dve.wait_ge(product, b * 4 + 2 * c + 1)
                        dve.wait_ge(limited, b * 2 + c + 1)
                        dve.scalar_tensor_tensor(up[:, :], up[:, :], 1.0, gate[:, :], ALU.add, ALU.mult).then_inc(product, 1)
                        dve.wait_ge(product, b * 4 + 2 * c + 2)
                        dve.wait_ge(sig_ready, b * 2 + c + 1)
                        if c == 0:
                            dve.wait_ge(x_ready, b * 2 + 2)
                        dve.tensor_tensor(act_rows[:, c, :], up[:, :], sig[:, :], ALU.mult).then_inc(h_done, 1)
                    dve.wait_ge(down_spread, b + 2)
                    dve.wait_ge(y_out, b * 16 + 16)
                    for s in range(2):
                        dve.wait_ge(dn_ready, b * 2 + s + 3)
                        part = slice(512 * s, 512 * s + 512)
                        dve.tensor_tensor(y[:, part], psum[:, 6 + s, :], bias_down[:, part], ALU.add).then_inc(y_done, 1)
                    low_rows(b * 2 + 2)


def gather_stage(g, r, x, acc):
    nc, psum = g.nc, g.psum
    with ExitStack() as own:
        sem = g.stage_semaphores("ga")
        got = own.enter_context(nc.sbuf_tensor("ga_got", [P, 4, D], F32))
        arrived = [sem(f"arrived{j}") for j in range(TOPE)]
        summed, turned, added = sem("summed"), sem("turned"), sem("added")
        with nc.Block(no_gpsimd_drain=True) as block:

            @block.sync
            def _(sp):
                g.clear_past(sp)
                g.ring.load_until(sp, FIRST["ple_proj"] + SLOTS)

            @block.gpsimd
            def _(pool):
                for t in range(TT):
                    for j in range(TOPE):
                        if t:
                            pool.wait_ge(summed, TOPE * (t - 1) + j + 1)
                        pool.indirect_dma_start(got[:, j, :], None, r.y_dram, bass.IndirectOffsetOnAxis(r.dest[:, t, j:j + 1], 0))\
                            .then_inc(arrived[j], 16)

            @block.vector
            def _(dve):
                def add(t):
                    for c in range(2):
                        n = 2 * t + c
                        dve.wait_ge(turned, n + 1)
                        for k in range(1):
                            to = x[:, 4 * c:4 * c + 4, t * P:(t + 1) * P]
                            dve.scalar_tensor_tensor(to, to, ALPHA, psum[:, n % BANKS, :].rearrange("p (k q) -> p k q", q=P),
                                                     ALU.mult, ALU.add).then_inc(added, 1)

                for t in range(TT):
                    for j in range(TOPE):
                        dve.wait_ge(arrived[j], 16 * (t + 1))
                        gate = r.gates[:, t, j:j + 1]
                        if j == 0:
                            dve.tensor_scalar(acc[:, t, :], got[:, j, :], gate, None, ALU.mult).then_inc(summed, 1)
                        else:
                            dve.wait_ge(summed, TOPE * t + j)
                            dve.scalar_tensor_tensor(acc[:, t, :], got[:, j, :], gate, acc[:, t, :], ALU.mult, ALU.add)\
                                .then_inc(summed, 1)
                    if t:
                        add(t - 1)
                add(TT - 1)

            @block.tensor
            def _(pe):
                for t in range(TT):
                    pe.wait_ge(summed, TOPE * (t + 1))
                    for c in range(2):
                        n = 2 * t + c
                        for k in range(4):
                            mm = pe.transpose(psum[:, n % BANKS, k * P:(k + 1) * P],
                                              acc[:, t, (4 * c + k) * P:(4 * c + k + 1) * P], g.ident)
                        mm.then_inc(turned, 1)


def ple_stage(g, x, ple):
    nc, ring, psum, col = g.nc, g.ring, g.psum, g.col
    with ExitStack() as own:
        sem = g.stage_semaphores("pl")
        pt = own.enter_context(nc.sbuf_tensor("pl_pt", [P, PLE // P, S], F32))
        gate = own.enter_context(nc.sbuf_tensor("pl_gate", [P, 2, S], F32))
        p_in, ple_ready, tile_ready, copied, gate_ready, gated, done = (sem(n) for n in (
            "p_in", "ple_ready", "tile_ready", "copied", "gate_ready", "gated", "done"))
        n0 = FIRST["ple_proj"]
        with nc.Block(no_gpsimd_drain=True) as block:

            @block.tensor
            def _(pe):
                pe.wait_ge(p_in, 16)
                ring.wait_landed(pe, n0)
                for t in range(DT):
                    for k in range(PLE // P):
                        mm = pe.matmul(psum[:, t, :], ring.weights(n0, 2 * k + t // 4, t % 4 * P, P), pt[:, k, :],
                                       start=k == 0, stop=k == PLE // P - 1)
                    mm.then_inc(ple_ready, 1)
                ring.freed[n0] = (ple_ready, DT)
                for t in range(DT):
                    ring.wait_landed(pe, n0 + 1 + t // 4)
                    pe.wait_ge(copied, t + 1)
                    for k in range(KT):
                        mm = pe.matmul(psum[:, t, :], ring.weights(n0 + 1 + t // 4, k, t % 4 * P, P), tile_of(x, k),
                                       start=k == 0, stop=k == KT - 1)
                    mm.then_inc(tile_ready, 1)

            @block.sync
            def _(sp):
                g.clear_past(sp)
                sp.dma_start(pt[:, :, :], g.extra["pt"]).then_inc(p_in, 16)
                ring.load_until(sp, n0 + 3)

            @block.scalar
            def _(act):
                for t in range(DT):
                    act.wait_ge(ple_ready, t + 1)
                    act.activation(ple[:, t, :], psum[:, t, :], ACT.Copy).then_inc(copied, 1)
                for t in range(DT):
                    act.wait_ge(tile_ready, t + 1)
                    if t >= 2:
                        act.wait_ge(gated, t - 1)
                    act.activation(gate[:, t % 2, :], psum[:, t, :], ACT.Sigmoid, bias=col("ple_b", t)).then_inc(gate_ready, 1)

            @block.vector
            def _(dve):
                for t in range(DT):
                    dve.wait_ge(gate_ready, t + 1)
                    dve.wait_ge(copied, t + 1)
                    dve.tensor_tensor(ple[:, t, :], ple[:, t, :], gate[:, t % 2, :], ALU.mult).then_inc(gated, 1)
                dve.wait_ge(tile_ready, DT)
                dve.wait_ge(gated, DT)
                for t in range(DT):
                    dve.scalar_tensor_tensor(x[:, t, :], x[:, t, :], ALPHA, ple[:, t, :], ALU.mult, ALU.add).then_inc(done, 1)


class Routes:
    pass


def block_3(g, x, h):
    nc, col = g.nc, g.col
    norm = lambda name, w: norm_stage(g, name, x, x, lambda t: col(w + "_g3", t), EPS_LN, g.ones_mean,
                                      bias=lambda t: col(w + "_b3", t), centre=True)
    mixer_stage(g, x, h)
    n0 = FIRST["w_out_3"]
    dense_stage(g, "out3", [
        Tile([n0 + t // 4], t % 4 * P, P, h, None, "dve",
             (lambda to: lambda e, bank: e.tensor_tensor(to, bank, to, ALU.add))(x[:, t, :])) for t in range(DT)], n0 + 2, scale_x=x)
    norm("n8", "ln1")
    r = Routes()
    r.table_dram = nc.dram_tensor("row_table", [P * TABLE, 1], I32, kind="Internal").ap()
    r.x_dram = nc.dram_tensor("x_rows", [S, D], F32, kind="Internal").ap()
    r.y_dram = nc.dram_tensor("y_rows", [(TABLE + 1) * ROWS, D], F32, kind="Internal").ap()
    r.scratch = h[:, 0:2, :].rearrange("p a s -> p (a s)")
    r.bias_row = h[0:1, 2:8, :].rearrange("p a s -> p (a s)")
    with ExitStack() as own:
        sb = lambda n, shape, dt=F32: own.enter_context(nc.sbuf_tensor(n, shape, dt))
        r.table, r.dest, r.gates = sb("table", [P, TABLE], I32), sb("dest", [P, TT, TOPE], U32), sb("gates", [P, TT, TOPE])
        r.expert, r.n_blocks = sb("expert", [1, TABLE], I32), sb("n_blocks", [1, 1], I32)
        route_stage(g, x, r)
        expert_stage(g, r)
        g.ring.freed = {}
        gather_stage(g, r, x, h[:, :, :].rearrange("p (t c) s -> p t (c s)", c=2))
    norm("n9", "ln2")
    ple_stage(g, x, h)
    norm("n10", "ln3")


class Shared:

    def __init__(self):
        self.stages = []

    def stage_semaphores(self, name):
        if len(self.stages) == 2:
            self.stages.pop(0)[0].close()
        own, made = ExitStack(), []
        self.stages.append((own, made))

        def semaphore(n):
            made.append(own.enter_context(self.nc.semaphore(f"{name}_{n}")))
            return made[-1]

        return semaphore

    def clear_past(self, sp):
        if len(self.stages) == 2:
            for s in self.stages[0][1]:
                sp.sem_clear(s)

    def open_split(self, stack, name):
        self.ring.high = stack.enter_context(self.nc.sbuf_tensor(f"{name}_ring_high", [P, SLOTS, KT * PANEL], F32R))
        return stack.enter_context(self.nc.sbuf_tensor(f"{name}_high", [P, DT, S], F32R))

    def col(self, name, i=0):
        at = COLS.at[name] + i
        return self.cols[:, at:at + 1]


def build(nc, wstream, xt, params, consts, rel_bias, extra, out):
    g = Shared()
    g.nc, g.rel_bias, g.extra = nc, rel_bias, extra
    with ExitStack() as ctx:
        sb = lambda n, shape: ctx.enter_context(nc.sbuf_tensor(n, shape, F32))
        g.cols = sb("cols", [P, COLS.n])
        const = sb("const", [P, CONST.n])
        x = sb("x", [P, DT, S])
        g.mod = sb("mod", [P, 6 * DT])
        h, g.h_low = with_low(nc, ctx, "h", [P, DT, S])
        ring, ring_low = with_low(nc, ctx, "ring", [P, SLOTS, KT * PANEL])
        g.psum = ctx.enter_context(nc.psum_tensor("psum", [P, BANKS, 512], F32))
        g.const = lambda name, n, rows=P: const[0:rows, CONST.at[name]:CONST.at[name] + n]
        g.ident, g.ones, g.ones_mean = g.const("ident", P), g.const("ones", P), g.const("ones_mean", P)
        g.half_ones, g.upper, g.acausal = g.const("half_ones", P), g.const("upper", P), g.const("acausal", P)
        g.causal_add = g.const("causal_add", P)
        g.starts16, g.starts64 = g.const("starts16", S), g.const("starts64", S)
        g.chunk_upper = g.const("chunk_upper", TT * CHUNK).rearrange("p (t c) -> p t c", c=CHUNK)
        g.before, g.block_iota = g.const("before", P), g.const("block_iota", TABLE, 1)
        g.neg_head = g.const("neg_head", MH * P, MH).rearrange("p (h c) -> p h c", c=P)
        g.eps = {EPS_RMS: g.const("eps_rms", 1), EPS_LN: g.const("eps_ln", 1)}
        landed = [ctx.enter_context(nc.semaphore(f"panel_landed{i}")) for i in range(SLOTS)]
        g.ring = Ring(ring, ring_low, wstream, landed)
        g.ring.high_ready = ctx.enter_context(nc.semaphore("panel_high"))
        g.ring.low_ready = ctx.enter_context(nc.semaphore("panel_low"))
        first_in = ctx.enter_context(nc.semaphore("first_in"))
        with nc.Block(no_gpsimd_drain=True) as block:
            @block.sync
            def _(sp):
                sp.dma_start(x[:, :, :], xt).then_inc(first_in, 16)
                sp.dma_start(const[:, :], consts).then_inc(first_in, 16)
                sp.dma_start(g.cols[:, :], params).then_inc(first_in, 16)
                g.ring.load_until(sp, SLOTS)
                sp.wait_ge(first_in, 48)
        block_1(g, x, h)
        block_2(g, x, h)
        block_3(g, x, h)
        out_done = ctx.enter_context(nc.semaphore("out_done"))
        with nc.Block(no_gpsimd_drain=True) as block:
            @block.sync
            def _(sp):
                sp.dma_start(out, x[:, :, :]).then_inc(out_done, 16)
                sp.wait_ge(out_done, 16)


CONST = Columns()
for _name, _c in (("ident", P), ("ones", P), ("ones_mean", P), ("half_ones", P), ("upper", P), ("acausal", P),
                  ("causal_add", P), ("neg_head", MH * P), ("eps_rms", 1), ("eps_ln", 1),
                  ("pool_inv", 4 * 16), ("chunk_upper", TT * CHUNK), ("starts16", S), ("starts64", S),
                  ("before", P), ("block_iota", TABLE)):
    CONST.add(_name, _c)


def constants():
    c = np.zeros((P, CONST.n), np.float32)
    put = lambda name, v: c.__setitem__((slice(0, v.shape[0]), slice(CONST.at[name], CONST.at[name] + v.shape[1])), v)
    p, f = np.arange(P)[:, None], np.arange(P)[None, :]
    put("ident", np.eye(P))
    put("ones", np.ones((P, P)))
    put("ones_mean", np.full((P, P), 1.0 / D))
    put("half_ones", (p // 64 == f // 64) * 1.0)
    put("upper", (p <= f) * 1.0)
    put("acausal", np.where(f <= p, 3.4e38, ACAUSAL))
    put("causal_add", np.where(f <= p, 0.0, MASKED))
    put("neg_head", np.repeat(-np.eye(MH), P, axis=1))
    put("eps_rms", np.full((P, 1), EPS_RMS))
    put("eps_ln", np.full((P, 1), EPS_LN))
    t = np.arange(16)
    put("pool_inv", np.broadcast_to(np.concatenate([1.0 / np.minimum(t + 1, w) for w in WINDOWS])[None], (P, 64)))
    put("chunk_upper", (p % CHUNK <= np.arange(TT * CHUNK)[None] % CHUNK) * 1.0)
    s = np.arange(S)[None]
    put("starts16", np.broadcast_to(s % SUB != 0, (P, S)) * 1.0)
    put("starts64", np.broadcast_to(s % CHUNK != 0, (P, S)) * 1.0)
    put("before", (p < f) * 1.0)
    put("block_iota", np.broadcast_to(np.arange(TABLE)[None], (P, TABLE)))
    return c


def relative_bucket():
    d = np.maximum(np.arange(P)[:, None] + (S - P) - np.arange(S)[None, :], 0)
    exact = REL_BUCKETS // 2
    large = exact + (np.log(np.maximum(d, 1).astype(np.float32) / exact) / np.float32(np.log(128 / exact))
                     * (REL_BUCKETS - exact)).astype(np.int32)
    return np.where(d < exact, d, np.minimum(large, REL_BUCKETS - 1))


def panels(w, columns):
    w = w[:, columns]
    rows, width = w.shape
    w = np.pad(w, ((0, -rows % D), (0, -width % PANEL)))
    w = w.reshape(-1, KT, P, w.shape[1] // PANEL, PANEL).transpose(3, 0, 2, 1, 4)
    return w.reshape(-1, P, KT * PANEL)


def by_turns(a, b):
    return np.stack([a, b], axis=1).reshape(-1, P, KT * PANEL)


def feature_columns(v):
    return np.asarray(v).reshape(-1, P).T


def pad_rows(v):
    return np.pad(np.asarray(v).reshape(-1, 1), ((0, P - np.size(v)), (0, 0)))


def head_panel_order():
    c = np.arange(P)
    return np.concatenate([np.concatenate([h * P + c, D + h * P + c, 3 * D + h * P + c, 4 * D + h * P + c]) for h in range(HH)])


def ffn_order():
    c = np.arange(2 * P)
    return np.concatenate([np.concatenate([n * 2 * P + c, DFF + n * 2 * P + c]) for n in range(FFN_PANELS)])


def lay_out(i):
    w = i["w_in"][0]
    z = lambda n: (np.arange(n[0], n[1]))
    q0 = 0
    offs = np.cumsum([0, 256, 256, 512, 512, 4, 4, 512, 512, 512, 512, 64, 8])
    seg = [np.arange(offs[k], offs[k + 1]) for k in range(12)]
    order = np.concatenate([seg[0], seg[1], seg[2], seg[3], seg[6], seg[7], seg[8], seg[9],
                            seg[10], seg[10], seg[4], seg[5], seg[11]])
    w2 = i["w_in_2"][0]
    al = np.arange
    c3 = np.concatenate([np.concatenate([al(512 + j * P, 512 + j * P + P), al(1024 + j * P, 1024 + j * P + P),
                                         al(1536 + j * P, 1536 + j * P + P), al(j * P, j * P + P)]) for j in range(4)])
    every = lambda a: al(a.shape[1])
    parts = {
        "w_in": panels(w, order), "w_out": panels(i["w_out"][0], every(i["w_out"][0])),
        "w_up": panels(i["w_up"][0], ffn_order()), "w_down": panels(i["w_down"][0], al(D)),
        "w_ada": panels(i["w_ada_2"][0], al(6 * D)),
        "w_zi": panels(w2, al(2 * D, 3 * D)), "w_head": panels(w2, head_panel_order()),
        "w_zv": panels(w2, al(5 * D, 6 * D)),
        "w_mix_a": by_turns(panels(i["w_proj_a_2"][0], al(D)), panels(w2, al(6 * D, 7 * D))),
        "w_mix_b": by_turns(panels(i["w_proj_b_2"][0], al(D)), panels(w2, al(7 * D, 8 * D))),
        "w_out_2": panels(i["w_out_2"][0], al(D)), "w_ffn_in": panels(i["w_ffn_in_2"][0], ffn_order()),
        "w_ffn_out": panels(i["w_ffn_out_2"][0], al(D)),
        "w_in_3": panels(i["w_in_3"][0], c3), "w_out_3": panels(i["w_out_3"][0], al(D)),
        "ple_proj": np.concatenate([i["ple_proj_3"][0].reshape(2, P, D).transpose(1, 0, 2).reshape(P, 2 * D),
                                    np.zeros((P, 2 * D), np.float32)], axis=1)[None],
        "ple_gate": panels(i["ple_gate_w_3"][0], al(D)),
    }
    for name, count in PANELS:
        assert parts[name].shape == (count, P, KT * PANEL), (name, parts[name].shape)
    wstream = np.concatenate([parts[name] for name, _ in PANELS])
    fo = ffn_order()
    taps = np.concatenate([i["ffn_conv_w"][0], i["ffn_conv_b"]])[:, fo]
    taps = taps.reshape(4, FFN_PANELS, 4, P).transpose(3, 1, 0, 2).reshape(P, -1)
    lb = i["hgrn_lb_logits_2"]
    cols = {
        "norm_mix": feature_columns(i["norm_mix"]), "conv_w": feature_columns(i["mlstm_conv_w"][0]),
        "conv_b": feature_columns(i["mlstm_conv_b"]), "i_bias": pad_rows(i["i_bias"]), "f_bias": pad_rows(i["f_bias"]),
        "mlstm_norm": feature_columns(i["mlstm_norm"]), "idx_norm": np.concatenate([i["idx_k_norm"][0]] * 2)[:, None],
        "norm_ffn": feature_columns(i["norm_ffn"]), "ffn_conv": taps, "norm_final": feature_columns(i["norm_final"]),
        "c2": feature_columns(i["c_2"]), "b_ada": feature_columns(i["b_ada_2"]), "b_gate": feature_columns(i["b_gate_2"]),
        "lb0": feature_columns(lb[0]), "lb1": feature_columns(lb[1]), "hgrn_norm": feature_columns(i["hgrn_norm_w_2"]),
        "ln1_w2": feature_columns(i["ln1_w_2"]), "ln1_b2": feature_columns(i["ln1_b_2"]),
        "ln2_w2": feature_columns(i["ln2_w_2"]), "ln2_b2": feature_columns(i["ln2_b_2"]),
        "conv_w3": feature_columns(i["conv_w_3"][0]), "pool_scale": feature_columns(i["pool_scale_3"]),
        "ln1_g3": feature_columns(i["ln1_g_3"]), "ln1_b3": feature_columns(i["ln1_b_3"]),
        "ln2_g3": feature_columns(i["ln2_g_3"]), "ln2_b3": feature_columns(i["ln2_b_3"]),
        "ple_b": feature_columns(i["ple_gate_b_3"]), "ln3_g3": feature_columns(i["ln3_g_3"]),
        "ln3_b3": feature_columns(i["ln3_b_3"]),
    }
    params = np.concatenate([cols[name] for name in COLS.at], axis=1)
    assert params.shape[1] == COLS.n
    rel = i["rel_bias"][relative_bucket()].transpose(0, 2, 1)
    tiles = lambda a: np.ascontiguousarray(a.T.reshape(-1, P, a.shape[0]).transpose(1, 0, 2))
    wgu, wdn = i["w_gate_up_3"][0], i["w_down_3"][0]
    moe_w = np.concatenate([wgu.reshape(NE, KT, P, 4, PANEL)[:, :, :, [0, 2, 1, 3]].transpose(0, 3, 2, 1, 4)
                            .reshape(NE, 4, P, KT * PANEL),
                            wdn.reshape(NE, KT, P, 2, PANEL).transpose(0, 3, 2, 1, 4).reshape(NE, 2, P, KT * PANEL)], axis=1)
    return {
        "wstream": wstream, "xt": tiles(i["x"][0]), "params": params, "consts": constants(),
        "rel_bias": np.ascontiguousarray(rel),
        "gmlp_rows": np.stack([i["gmlp_ln_w_2"][0], i["gmlp_ln_b_2"][0], i["gmlp_bs_2"][0].reshape(-1)]),
        "gmlp_ws": np.ascontiguousarray(i["gmlp_ws_2"][0].transpose(2, 0, 1)),
        "pool_mix": np.ascontiguousarray(i["pool_mix_3"][0].transpose(1, 0, 2)),
        "pt": tiles(i["p_3"][0, 0]),
        "router_w": np.ascontiguousarray(i["router_w_3"][0].reshape(DT, P, NE).transpose(1, 0, 2)),
        "router_b": np.ascontiguousarray(i["router_b_3"]),
        "moe_w": moe_w.reshape(NE * 6, P, KT * PANEL),
        "moe_b": np.concatenate([i["b_gate_up_3"][0], i["b_down_3"][0]], axis=1),
    }


def kernel(**inputs):
    import concourse.bacc as bacc
    from concourse.bass_utils import run_bass_kernel_spmd

    arrays = {k: np.ascontiguousarray(v, dtype=np.float32) for k, v in lay_out({k: np.asarray(v) for k, v in inputs.items()}).items()}
    nc = bacc.Bacc("TRN2", target_bir_lowering=False, num_devices=1)
    ap = {k: nc.dram_tensor(k, v.shape, F32, kind="ExternalInput").ap() for k, v in arrays.items()}
    out = nc.dram_tensor("out", [P, DT, S], F32, kind="ExternalOutput").ap()
    build(nc, ap["wstream"], ap["xt"], ap["params"], ap["consts"], ap["rel_bias"], ap, out)
    r = run_bass_kernel_spmd(nc, [arrays], core_ids=[0])
    return r.results[0]["out"].transpose(2, 1, 0).reshape(1, S, D)
```
